# Optimizing a Trainium2 kernel written in Bass

```python
import math
import jax, jax.numpy as jnp
from jax import lax
import numpy as np

D_MODEL = 1024
BATCH = 1
SEQ = 512
DEPTH = 1

CHUNK = 64
Q_BLOCK = 128
N_MEM = 256
HEAD_DIM = 64
SB_HEADS = 8
SB_WIDTH = SB_HEADS * HEAD_DIM
HG_HEADS = 4
HG_KEY_DIM = 128
HG_VAL_DIM = 64
HG_KWIDTH = HG_HEADS * HG_KEY_DIM
HG_VWIDTH = HG_HEADS * HG_VAL_DIM
MEM_HEADS = 4
MEM_WIDTH = MEM_HEADS * HEAD_DIM
MIX_WIDTH = SB_WIDTH + HG_VWIDTH + MEM_WIDTH
SPLIT_SIZES = (SB_WIDTH, SB_WIDTH, SB_WIDTH, HG_KWIDTH, HG_KWIDTH, HG_VWIDTH, HG_VWIDTH, MEM_WIDTH)
IN_WIDTH = 3 * SB_WIDTH + 2 * HG_KWIDTH + 2 * HG_VWIDTH + MEM_WIDTH
PEER_HEADS = 8
N_KEYS = 128
N_EXPERTS = N_KEYS * N_KEYS
PEER_TOPK = 16
D_KEY = 256
HALF_KEY = D_KEY // 2
PEER_TOKEN_BLOCK = 128
EPS = 1e-6


def rms_norm(x, gain):
    xf = x.astype(jnp.float32)
    y = xf * lax.rsqrt(jnp.mean(xf * xf, axis=-1, keepdims=True) + EPS)
    return (y * gain.astype(jnp.float32)).astype(x.dtype)

def stick_breaking_attention(q, k, v):
    b, s, h, d = q.shape
    nb = s // Q_BLOCK
    qb = q.reshape(b, nb, Q_BLOCK, h, d).transpose(1, 0, 3, 2, 4)
    kh = k.transpose(0, 2, 1, 3)
    vh = v.transpose(0, 2, 1, 3)
    key_pos = jnp.arange(s)
    scale = 1.0 / math.sqrt(d)

    def block(args):
        q_blk, i = args
        q_pos = i * Q_BLOCK + jnp.arange(Q_BLOCK)
        z = jnp.einsum('bhqd,bhkd->bhqk', q_blk, kh).astype(jnp.float32) * scale
        mask = key_pos[None, :] < q_pos[:, None]
        log_1m = jnp.where(mask, jax.nn.log_sigmoid(-z), 0.0)
        tail = lax.cumsum(log_1m, axis=3, reverse=True) - log_1m
        log_a = jax.nn.log_sigmoid(z) + tail
        a = jnp.where(mask, jnp.exp(log_a), 0.0)
        return jnp.einsum('bhqk,bhkd->bhqd', a.astype(vh.dtype), vh)

    out = lax.map(block, (qb, jnp.arange(nb)))
    return out.transpose(1, 0, 3, 2, 4).reshape(b, s, h, d)

def hgrn2_recurrence(q, f_logit, i, lower_bound):
    b, s, h, dk = q.shape
    dv = i.shape[-1]
    nc = s // CHUNK
    f = lower_bound + (1.0 - lower_bound) * jax.nn.sigmoid(f_logit.astype(jnp.float32))
    log_f = jnp.log(f)
    k = 1.0 - f
    qf = jax.nn.silu(q.astype(jnp.float32))
    vf = i.astype(jnp.float32)

    def to_chunks(t):
        return t.reshape(b, nc, CHUNK, h, t.shape[-1]).transpose(1, 0, 3, 2, 4)

    causal = jnp.tril(jnp.ones((CHUNK, CHUNK), dtype=bool))[:, :, None]

    def step(state, inp):
        qc, kc, vc, gc = inp
        bcum = jnp.cumsum(gc, axis=2)
        diff = bcum[:, :, :, None, :] - bcum[:, :, None, :, :]
        decay = jnp.where(causal, jnp.exp(jnp.where(causal, diff, 0.0)), 0.0)
        scores = jnp.einsum('bhtk,bhtsk,bhsk->bhts', qc, decay, kc)
        intra = jnp.einsum('bhts,bhsv->bhtv', scores, vc)
        inter = jnp.einsum('bhtk,bhkv->bhtv', qc * jnp.exp(bcum), state)
        last = bcum[:, :, -1:, :]
        new_state = (jnp.exp(last[:, :, 0, :])[..., None] * state
                     + jnp.einsum('bhsk,bhsv->bhkv', kc * jnp.exp(last - bcum), vc))
        return new_state, intra + inter

    state0 = jnp.zeros((b, h, dk, dv), jnp.float32)
    _, out = lax.scan(step, state0, (to_chunks(qf), to_chunks(k), to_chunks(vf), to_chunks(log_f)))
    return out.transpose(1, 0, 3, 2, 4).reshape(b, s, h, dv)

def memory_attention(q, mem_k, mem_v, q_gain, k_gain):
    qn = rms_norm(q, q_gain)
    kn = rms_norm(mem_k, k_gain)
    scale = 1.0 / math.sqrt(q.shape[-1])
    logits = jnp.einsum('bshd,bmhd->bhsm', qn, kn).astype(jnp.float32) * scale
    p = jax.nn.softmax(logits, axis=-1)
    return jnp.einsum('bhsm,bmhd->bshd', p.astype(mem_v.dtype), mem_v)

def peer_ffn(h, w_query, sub_keys, expert_u, expert_v):
    b, s, d = h.shape
    nb = s // PEER_TOKEN_BLOCK
    hb = h.reshape(b, nb, PEER_TOKEN_BLOCK, d).transpose(1, 0, 2, 3)

    def block(x_blk):
        t = x_blk.shape[1]
        q = (x_blk @ w_query).reshape(b, t, PEER_HEADS, 2, HALF_KEY)
        scores = jnp.einsum('bthcd,hcnd->bthcn', q, sub_keys).astype(jnp.float32)
        top_s, top_i = lax.top_k(scores, PEER_TOPK)
        cand_s = top_s[..., 0, :, None] + top_s[..., 1, None, :]
        cand_i = top_i[..., 0, :, None] * N_KEYS + top_i[..., 1, None, :]
        cand_s = cand_s.reshape(b, t, PEER_HEADS, PEER_TOPK * PEER_TOPK)
        cand_i = cand_i.reshape(b, t, PEER_HEADS, PEER_TOPK * PEER_TOPK)
        best_s, pos = lax.top_k(cand_s, PEER_TOPK)
        expert_idx = jnp.take_along_axis(cand_i, pos, axis=-1)
        gate = jax.nn.softmax(best_s, axis=-1)
        u = expert_u[expert_idx]
        v = expert_v[expert_idx]
        act = jax.nn.gelu(jnp.einsum('btd,bthkd->bthk', x_blk, u).astype(jnp.float32), approximate=False)
        return jnp.einsum('bthk,bthkd->btd', (gate * act).astype(v.dtype), v)

    out = lax.map(block, hb)
    return out.transpose(1, 0, 2, 3).reshape(b, s, d)

def first_inputs(seed: int = 0) -> dict:
    key = jax.random.key(seed)
    ks = jax.random.split(key, 20)
    f32 = jnp.float32
    nrm = lambda k, shape, scale: jax.random.normal(k, shape, f32) * scale
    gain = lambda k, shape: 1.0 + 0.02 * jax.random.normal(k, shape, f32)
    return {
        "x": jax.random.normal(ks[0], (BATCH, SEQ, D_MODEL), f32),
        "mem": jax.random.normal(ks[1], (BATCH, N_MEM, D_MODEL), f32),
        "norm_mix_gain": gain(ks[2], (DEPTH, D_MODEL)),
        "w_in": nrm(ks[3], (DEPTH, D_MODEL, IN_WIDTH), D_MODEL ** -0.5),
        "gamma_lb": nrm(ks[4], (DEPTH + 1, HG_KWIDTH), 0.5),
        "sb_out_gain": gain(ks[5], (DEPTH, SB_HEADS, HEAD_DIM)),
        "hg_out_gain": gain(ks[6], (DEPTH, HG_HEADS, HG_VAL_DIM)),
        "mem_norm_gain": gain(ks[7], (D_MODEL,)),
        "w_mem_kv": nrm(ks[8], (DEPTH, D_MODEL, 2 * MEM_WIDTH), D_MODEL ** -0.5),
        "mem_q_gain": gain(ks[9], (DEPTH, HEAD_DIM)),
        "mem_k_gain": gain(ks[10], (DEPTH, HEAD_DIM)),
        "w_out": nrm(ks[11], (DEPTH, MIX_WIDTH, D_MODEL), MIX_WIDTH ** -0.5),
        "norm_ffn_gain": gain(ks[12], (DEPTH, D_MODEL)),
        "peer_w_query": nrm(ks[13], (DEPTH, D_MODEL, PEER_HEADS * D_KEY), D_MODEL ** -0.5),
        "peer_sub_keys": nrm(ks[14], (DEPTH, PEER_HEADS, 2, N_KEYS, HALF_KEY), HALF_KEY ** -0.5),
        "peer_u": nrm(ks[15], (DEPTH, N_EXPERTS, D_MODEL), D_MODEL ** -0.5),
        "peer_v": nrm(ks[16], (DEPTH, N_EXPERTS, D_MODEL), PEER_HEADS ** -0.5),
    }

def first_block(x, mem, norm_mix_gain, w_in, gamma_lb, sb_out_gain, hg_out_gain, mem_norm_gain,
              w_mem_kv, mem_q_gain, mem_k_gain, w_out, norm_ffn_gain, peer_w_query,
              peer_sub_keys, peer_u, peer_v):
    b, s, _ = x.shape
    m = mem.shape[1]
    lb_all = jnp.cumsum(jax.nn.softmax(gamma_lb.astype(jnp.float32), axis=0), axis=0)
    mem_n = rms_norm(mem, mem_norm_gain)
    split_points = [int(v) for v in np.cumsum(SPLIT_SIZES)[:-1]]
    for l in range(DEPTH):
        h = rms_norm(x, norm_mix_gain[l])
        proj = h @ w_in[l]
        sb_q, sb_k, sb_v, hg_q, hg_f, hg_i, hg_g, mem_q = jnp.split(proj, split_points, axis=-1)

        sb_o = stick_breaking_attention(sb_q.reshape(b, s, SB_HEADS, HEAD_DIM),
                                        sb_k.reshape(b, s, SB_HEADS, HEAD_DIM),
                                        sb_v.reshape(b, s, SB_HEADS, HEAD_DIM))
        sb_o = rms_norm(sb_o, sb_out_gain[l]).reshape(b, s, SB_WIDTH)

        lb = lb_all[l].reshape(HG_HEADS, HG_KEY_DIM)
        hg_o = hgrn2_recurrence(hg_q.reshape(b, s, HG_HEADS, HG_KEY_DIM),
                                hg_f.reshape(b, s, HG_HEADS, HG_KEY_DIM),
                                hg_i.reshape(b, s, HG_HEADS, HG_VAL_DIM), lb).astype(x.dtype)
        hg_o = rms_norm(hg_o, hg_out_gain[l]).reshape(b, s, HG_VWIDTH) * jax.nn.silu(hg_g)

        mem_kv = mem_n @ w_mem_kv[l]
        mem_k, mem_v = jnp.split(mem_kv, 2, axis=-1)
        mem_o = memory_attention(mem_q.reshape(b, s, MEM_HEADS, HEAD_DIM),
                                 mem_k.reshape(b, m, MEM_HEADS, HEAD_DIM),
                                 mem_v.reshape(b, m, MEM_HEADS, HEAD_DIM),
                                 mem_q_gain[l], mem_k_gain[l]).reshape(b, s, MEM_WIDTH)

        mixed = jnp.concatenate([sb_o, hg_o, mem_o], axis=-1)
        x = x + mixed @ w_out[l]

        x = x + peer_ffn(rms_norm(x, norm_ffn_gain[l]), peer_w_query[l], peer_sub_keys[l],
                         peer_u[l], peer_v[l])
    return x


N_MIXERS = 3
MIX_WIDTH_2 = 768
N_MEM_HEADS = 4
MEM_WIDTH_2 = N_MEM_HEADS * HEAD_DIM
BRANCH = MIX_WIDTH_2 + MEM_WIDTH_2
IN_WIDTH_2 = 3 * MIX_WIDTH_2 + MEM_WIDTH_2 + BRANCH
RMS_EPS = 1e-6
SUBLN_EPS = 1e-5
NEG_INF = -1e30

DSW_GROUPS = ((128, 1), (512, 4), (2048, 16))
DSW_HEADS_PER_GROUP = 4
DSW_HEADS = DSW_HEADS_PER_GROUP * len(DSW_GROUPS)
DSW_GROUP_WIDTH = DSW_HEADS_PER_GROUP * HEAD_DIM
BAND_BLOCK = 128

MOBA_HEADS = MIX_WIDTH_2 // HEAD_DIM
MOBA_BLOCK = 256
MOBA_TOPK = 3
MOBA_Q_CHUNK = 64

DIFF_HEADS = 6
DIFF_D = 64
DIFF_Q_BLOCK = 128
N_DIFF_LAYERS = len(range(2, DEPTH, N_MIXERS))


def alibi_slopes(n):
    return jnp.asarray(2.0 ** (-8.0 * np.arange(1, n + 1) / n), dtype=jnp.float32)

def rmsnorm(x, g, eps=RMS_EPS):
    xf = x.astype(jnp.float32)
    y = xf * lax.rsqrt(jnp.mean(xf * xf, axis=-1, keepdims=True) + eps)
    return (y * g.astype(jnp.float32)).astype(x.dtype)

def split_heads(t, n):
    b, s, _ = t.shape
    return t.reshape(b, s, n, -1).transpose(0, 2, 1, 3)

def merge_heads(t):
    b, h, s, d = t.shape
    return t.transpose(0, 2, 1, 3).reshape(b, s, h * d)

def banded_causal_attention(q, k, v, span, slopes):
    b, h, L, hd = q.shape
    nb = -(-L // BAND_BLOCK)
    Lp = nb * BAND_BLOCK
    pad = ((0, 0), (0, 0), (0, Lp - L), (0, 0))
    qb = jnp.pad(q, pad).reshape(b, h, nb, BAND_BLOCK, hd)
    kb = jnp.pad(k, pad).reshape(b, h, nb, BAND_BLOCK, hd)
    vb = jnp.pad(v, pad).reshape(b, h, nb, BAND_BLOCK, hd)
    shift = ((0, 0), (0, 0), (1, 0), (0, 0), (0, 0))
    kk = jnp.concatenate([jnp.pad(kb, shift)[:, :, :-1], kb], axis=3)
    vv = jnp.concatenate([jnp.pad(vb, shift)[:, :, :-1], vb], axis=3)
    dist = (jnp.arange(BAND_BLOCK)[:, None] + BAND_BLOCK) - jnp.arange(2 * BAND_BLOCK)[None, :]
    kpos = jnp.arange(nb)[:, None] * BAND_BLOCK - BAND_BLOCK + jnp.arange(2 * BAND_BLOCK)[None, :]
    valid = ((dist >= 0) & (dist <= span))[None, :, :] & (kpos >= 0)[:, None, :]
    s = jnp.einsum('bhnqd,bhnkd->bhnqk', qb, kk).astype(jnp.float32) * (hd ** -0.5)
    s = s - slopes[None, :, None, None, None] * dist.astype(jnp.float32)
    s = jnp.where(valid, s, NEG_INF)
    lse = jax.nn.logsumexp(s, axis=-1)
    p = jnp.exp(s - lse[..., None])
    out = jnp.einsum('bhnqk,bhnkd->bhnqd', p, vv.astype(jnp.float32))
    return out.reshape(b, h, Lp, hd)[:, :, :L], lse.reshape(b, h, Lp)[:, :, :L]

def dilated_window_mixer(q, k, v):
    b, S, _ = q.shape
    hg = DSW_HEADS_PER_GROUP
    slopes_all = alibi_slopes(DSW_HEADS)
    outs, lses = [], []
    for g, (window, dil) in enumerate(DSW_GROUPS):
        cols = slice(g * DSW_GROUP_WIDTH, (g + 1) * DSW_GROUP_WIDTH)
        U = S // dil

        def to_residue(t):
            t = t.reshape(b, U, dil, hg, HEAD_DIM).transpose(0, 3, 2, 1, 4)
            return t.reshape(b, hg * dil, U, HEAD_DIM)

        slopes = jnp.repeat(slopes_all[g * hg:(g + 1) * hg] * dil, dil)
        o, lse = banded_causal_attention(to_residue(q[..., cols]), to_residue(k[..., cols]),
                                         to_residue(v[..., cols]), window // dil, slopes)
        o = o.reshape(b, hg, dil, U, HEAD_DIM).transpose(0, 3, 2, 1, 4).reshape(b, S, hg, HEAD_DIM)
        lse = lse.reshape(b, hg, dil, U).transpose(0, 3, 2, 1).reshape(b, S, hg)
        outs.append(o)
        lses.append(lse)
    alpha = jax.nn.softmax(jnp.stack(lses, axis=0), axis=0)
    mixed = [(outs[g] * alpha[g][..., None]).reshape(b, S, DSW_GROUP_WIDTH) for g in range(len(DSW_GROUPS))]
    return jnp.concatenate(mixed, axis=-1).astype(q.dtype)

def moba_mixer(q, k, v):
    b, S, _ = q.shape
    H = MOBA_HEADS
    slopes = alibi_slopes(H)
    nblk = -(-S // MOBA_BLOCK)
    Sp = nblk * MOBA_BLOCK
    n_gate = max(nblk, MOBA_TOPK)
    pad = ((0, 0), (0, 0), (0, Sp - S), (0, 0))
    qh = jnp.pad(split_heads(q, H), pad)
    kb = jnp.pad(split_heads(k, H), pad).reshape(b, H, nblk, MOBA_BLOCK, HEAD_DIM)
    vb = jnp.pad(split_heads(v, H), pad).reshape(b, H, nblk, MOBA_BLOCK, HEAD_DIM)
    kmean = jnp.mean(kb.astype(jnp.float32), axis=3)
    nchunk = Sp // MOBA_Q_CHUNK
    qc = qh.reshape(b, H, nchunk, MOBA_Q_CHUNK, HEAD_DIM).transpose(2, 0, 1, 3, 4)
    bi = jnp.arange(b)[:, None, None, None]
    hi = jnp.arange(H)[None, :, None, None]
    scale = HEAD_DIM ** -0.5

    def one_chunk(args):
        c, qx = args
        t = c * MOBA_Q_CHUNK + jnp.arange(MOBA_Q_CHUNK)
        n = (c * MOBA_Q_CHUNK) // MOBA_BLOCK
        gate = jnp.einsum('bhqd,bhnd->bhqn', qx.astype(jnp.float32), kmean)
        gate = jnp.pad(gate, ((0, 0), (0, 0), (0, 0), (0, n_gate - nblk)), constant_values=NEG_INF)
        gate = jnp.where(jnp.arange(n_gate) < n, gate, NEG_INF)
        _, idx = lax.top_k(gate, MOBA_TOPK)
        idx = jnp.minimum(idx, nblk - 1)
        sel_ok = jnp.arange(MOBA_TOPK) < n
        ks = kb[bi, hi, idx]
        vs = vb[bi, hi, idx]
        kpos_sel = idx[..., None] * MOBA_BLOCK + jnp.arange(MOBA_BLOCK)
        dist_sel = (t[None, None, :, None, None] - kpos_sel).astype(jnp.float32)
        s_sel = jnp.einsum('bhqd,bhqjkd->bhqjk', qx, ks).astype(jnp.float32) * scale
        s_sel = s_sel - slopes[None, :, None, None, None] * dist_sel
        s_sel = jnp.where(sel_ok[:, None], s_sel, NEG_INF)
        k_own = lax.dynamic_index_in_dim(kb, n, axis=2, keepdims=False)
        v_own = lax.dynamic_index_in_dim(vb, n, axis=2, keepdims=False)
        dist_own = t[:, None] - (n * MOBA_BLOCK + jnp.arange(MOBA_BLOCK))[None, :]
        s_own = jnp.einsum('bhqd,bhkd->bhqk', qx, k_own).astype(jnp.float32) * scale
        s_own = jnp.where(dist_own >= 0,
                          s_own - slopes[None, :, None, None] * dist_own.astype(jnp.float32), NEG_INF)
        s_all = jnp.concatenate([s_sel.reshape(b, H, MOBA_Q_CHUNK, MOBA_TOPK * MOBA_BLOCK), s_own], axis=-1)
        p = jax.nn.softmax(s_all, axis=-1)
        p_sel = p[..., :MOBA_TOPK * MOBA_BLOCK].reshape(b, H, MOBA_Q_CHUNK, MOBA_TOPK, MOBA_BLOCK)
        p_own = p[..., MOBA_TOPK * MOBA_BLOCK:]
        return (jnp.einsum('bhqjk,bhqjkd->bhqd', p_sel, vs.astype(jnp.float32))
                + jnp.einsum('bhqk,bhkd->bhqd', p_own, v_own.astype(jnp.float32)))

    o = lax.map(one_chunk, (jnp.arange(nchunk), qc))
    o = o.transpose(1, 2, 0, 3, 4).reshape(b, H, Sp, HEAD_DIM)[:, :, :S]
    return merge_heads(o).astype(q.dtype)

def diff_mixer(q, k, v, lq1, lk1, lq2, lk2, subln_g, lambda_init):
    b, S, _ = q.shape
    H = DIFF_HEADS
    slopes = alibi_slopes(H)
    qh = q.reshape(b, S, H, 2, DIFF_D).transpose(0, 2, 3, 1, 4)
    kh = k.reshape(b, S, H, 2, DIFF_D).transpose(0, 2, 3, 1, 4)
    vh = split_heads(v, H).astype(jnp.float32)
    lam = (jnp.exp(jnp.sum(lq1.astype(jnp.float32) * lk1.astype(jnp.float32)))
           - jnp.exp(jnp.sum(lq2.astype(jnp.float32) * lk2.astype(jnp.float32))) + lambda_init)
    nqb = S // DIFF_Q_BLOCK
    qblocks = qh.reshape(b, H, 2, nqb, DIFF_Q_BLOCK, DIFF_D).transpose(3, 0, 1, 2, 4, 5)
    kpos = jnp.arange(S)

    def one_block(args):
        j, qx = args
        t = j * DIFF_Q_BLOCK + jnp.arange(DIFF_Q_BLOCK)
        dist = t[:, None] - kpos[None, :]
        s = jnp.einsum('bhmqd,bhmkd->bhmqk', qx, kh).astype(jnp.float32) * (DIFF_D ** -0.5)
        s = jnp.where(dist >= 0, s - slopes[None, :, None, None, None] * dist.astype(jnp.float32), NEG_INF)
        p = jax.nn.softmax(s, axis=-1)
        w = p[:, :, 0] - lam * p[:, :, 1]
        return jnp.einsum('bhqk,bhkd->bhqd', w, vh)

    o = lax.map(one_block, (jnp.arange(nqb), qblocks))
    o = o.transpose(1, 2, 0, 3, 4).reshape(b, H, S, 2 * DIFF_D)
    o = rmsnorm(o, subln_g, SUBLN_EPS) * (1.0 - lambda_init)
    return merge_heads(o).astype(q.dtype)

def memory_attention_2(qm, mem_n, w_mem_kv):
    kv = mem_n @ w_mem_kv
    km = split_heads(kv[..., :MEM_WIDTH_2], N_MEM_HEADS)
    vm = split_heads(kv[..., MEM_WIDTH_2:], N_MEM_HEADS)
    qh = split_heads(qm, N_MEM_HEADS)
    s = jnp.einsum('bhqd,bhkd->bhqk', qh, km).astype(jnp.float32) * (HEAD_DIM ** -0.5)
    p = jax.nn.softmax(s, axis=-1)
    return merge_heads(jnp.einsum('bhqk,bhkd->bhqd', p, vm.astype(jnp.float32))).astype(qm.dtype)

def second_inputs(seed: int = 0) -> dict:
    key = jax.random.key(seed)
    ks = jax.random.split(key, 14)
    f32 = jnp.float32
    nd = max(N_DIFF_LAYERS, 0)
    return {
        "x": jax.random.normal(ks[0], (BATCH, SEQ, D_MODEL), f32),
        "mem": jax.random.normal(ks[1], (BATCH, N_MEM, D_MODEL), f32),
        "norm_g": 1.0 + 0.02 * jax.random.normal(ks[2], (DEPTH, D_MODEL), f32),
        "w_in": jax.random.normal(ks[3], (DEPTH, D_MODEL, IN_WIDTH_2), f32) * D_MODEL ** -0.5,
        "w_out": jax.random.normal(ks[4], (DEPTH, BRANCH, D_MODEL), f32) * BRANCH ** -0.5,
        "mem_norm_g": 1.0 + 0.02 * jax.random.normal(ks[5], (DEPTH, D_MODEL), f32),
        "w_mem_kv": jax.random.normal(ks[6], (DEPTH, D_MODEL, 2 * MEM_WIDTH_2), f32) * D_MODEL ** -0.5,
        "diff_lambda_q1": 0.1 * jax.random.normal(ks[7], (nd, DIFF_D), f32),
        "diff_lambda_k1": 0.1 * jax.random.normal(ks[8], (nd, DIFF_D), f32),
        "diff_lambda_q2": 0.1 * jax.random.normal(ks[9], (nd, DIFF_D), f32),
        "diff_lambda_k2": 0.1 * jax.random.normal(ks[10], (nd, DIFF_D), f32),
        "diff_subln_g": 1.0 + 0.02 * jax.random.normal(ks[11], (nd, 2 * DIFF_D), f32),
        "final_norm_g": 1.0 + 0.02 * jax.random.normal(ks[12], (D_MODEL,), f32),
    }

def second_block(x, mem, norm_g, w_in, w_out, mem_norm_g, w_mem_kv, diff_lambda_q1, diff_lambda_k1,
              diff_lambda_q2, diff_lambda_k2, diff_subln_g, final_norm_g):
    c1, c2, c3, c4 = MIX_WIDTH_2, 2 * MIX_WIDTH_2, 3 * MIX_WIDTH_2, 3 * MIX_WIDTH_2 + MEM_WIDTH_2
    for i in range(DEPTH):
        h = rmsnorm(x, norm_g[i])
        proj = h @ w_in[i]
        q, k, v = proj[..., :c1], proj[..., c1:c2], proj[..., c2:c3]
        qm, gate = proj[..., c3:c4], proj[..., c4:]
        kind = i % N_MIXERS
        if kind == 0:
            mix = dilated_window_mixer(q, k, v)
        elif kind == 1:
            mix = moba_mixer(q, k, v)
        else:
            c = i // N_MIXERS
            lambda_init = 0.8 - 0.6 * math.exp(-0.3 * i)
            mix = diff_mixer(q, k, v, diff_lambda_q1[c], diff_lambda_k1[c], diff_lambda_q2[c],
                             diff_lambda_k2[c], diff_subln_g[c], lambda_init)
        mo = memory_attention_2(qm, rmsnorm(mem, mem_norm_g[i]), w_mem_kv[i])
        y = jnp.concatenate([mix, mo], axis=-1) * jax.nn.silu(gate)
        x = x + y @ w_out[i]
    return rmsnorm(x, final_norm_g)


def setup_inputs(seed=0):
    out = dict(first_inputs(seed))
    for name, value in second_inputs(seed + 1).items():
        if name != "x":
            out[name + "_2"] = value
    return out


def reference(
    x, mem, norm_mix_gain, w_in, gamma_lb, sb_out_gain, hg_out_gain, mem_norm_gain, w_mem_kv,
    mem_q_gain, mem_k_gain, w_out, norm_ffn_gain, peer_w_query, peer_sub_keys, peer_u, peer_v,
    mem_2, norm_g_2, w_in_2, w_out_2, mem_norm_g_2, w_mem_kv_2, diff_lambda_q1_2,
    diff_lambda_k1_2, diff_lambda_q2_2, diff_lambda_k2_2, diff_subln_g_2, final_norm_g_2,
):
    x = first_block(
        x, mem, norm_mix_gain, w_in, gamma_lb, sb_out_gain, hg_out_gain, mem_norm_gain,
        w_mem_kv, mem_q_gain, mem_k_gain, w_out, norm_ffn_gain, peer_w_query, peer_sub_keys,
        peer_u, peer_v,
    )
    return second_block(
        x, mem_2, norm_g_2, w_in_2, w_out_2, mem_norm_g_2, w_mem_kv_2, diff_lambda_q1_2,
        diff_lambda_k1_2, diff_lambda_q2_2, diff_lambda_k2_2, diff_subln_g_2, final_norm_g_2,
    )


_drawn_inputs = setup_inputs


def setup_inputs(seed=0):
    import zlib

    import numpy as np

    out = dict(_drawn_inputs(seed))
    spreads = {}
    factors = {'sb_out_gain': 2.897,
     'hg_out_gain': 4.799,
     'mem_norm_gain': 8.0,
     'mem_q_gain': 8.0,
     'mem_k_gain': 8.0,
     'norm_g_2': 8.0,
     'mem_norm_g_2': 8.0,
     'final_norm_g_2': 2.825}
    for name, (base, spread) in spreads.items():
        noise = np.random.default_rng([zlib.crc32(name.encode()), seed]).standard_normal(out[name].shape)
        drawn = base * np.exp(spread * noise) if base else spread * noise
        out[name] = __import__('jax').numpy.asarray(drawn.astype(out[name].dtype))
    for name, factor in factors.items():
        out[name] = (out[name] * factor).astype(out[name].dtype)
    return out
```

```python
from contextlib import ExitStack

import numpy as np

import concourse.bass as bass
from concourse import mybir

F32 = mybir.dt.float32
F32R = mybir.dt.float32r
U32 = mybir.dt.uint32
ALU = mybir.AluOpType
ACT = mybir.ActivationFunctionType
AX = mybir.AxisListType

EPS = 1e-6
NEG = -3.0e38
SLOPES = [float(np.float32(2.0 ** (-8.0 * n / 12))) for n in range(1, 13)]
LEVELS = [64, 32, 16, 8, 4, 2, 1]
G_MIX, G_FFN, G_N2, G_MEM, G_MEM2, G_OUT, G_LB, G_MQ, G_MK = 0, 8, 16, 24, 32, 40, 48, 56, 57
SMALL = 58
PARTS = ((0, 0), (0, 1), (1, 0))


class Engine:

    def __init__(self, nc, eng, name):
        self.e = eng
        self.sem = nc.alloc_semaphore(name)
        self.n = 0
        self.seen = {}

    def wait(self, *marks):
        for m in marks:
            if m is None:
                continue
            sem, v, key = m
            if self.seen.get(key, 0) < v:
                self.e.wait_ge(sem, v)
                self.seen[key] = v

    def did(self, ins):
        self.n += 1
        ins.then_inc(self.sem, 1)
        return self.last()

    def last(self):
        return (self.sem, self.n, id(self))

    def own(self):
        self.wait(self.last())


class Arrival:

    def __init__(self, nc, name):
        self.sem = nc.alloc_semaphore(name)
        self.n = 0

    def did(self, ins):
        self.n += 16
        ins.then_inc(self.sem, 16)
        return self.last()

    def last(self):
        return (self.sem, self.n, id(self))


def program(nc, a, out):
    V = Engine(nc, nc.vector, "s_dve")
    A = Engine(nc, nc.scalar, "s_act")
    T = Engine(nc, nc.tensor, "s_pe")
    P = Engine(nc, nc.gpsimd, "s_pool")
    S = Engine(nc, nc.sync, "s_sp")
    ve, ac, te, po, sp = nc.vector, nc.scalar, nc.tensor, nc.gpsimd, nc.sync

    def fence():
        marks = [x.last() for x in (V, A, T, P)]
        for x in (V, A, T, P, S):
            x.wait(*marks)

    ctx = ExitStack()

    def sb(name, shape, dt=F32, scope=None):
        return (scope or ctx).enter_context(nc.sbuf_tensor(name, shape, dt))

    ctx.__enter__()
    HS = sb("HS", [128, 2, 8, 512], F32R)
    WS = sb("WS", [128, 2, 2, 8, 256], F32R)
    WR = sb("WR", [128, 2, 8, 256])
    X = sb("X", [128, 4, 1024])
    CST = sb("CST", [128, 4, 128])
    GN = sb("GN", [128, SMALL])
    MKT = [sb(f"MKT{n}", [128, 2, 256]) for n in range(2)]
    MV = [sb(f"MV{n}", [128, 2, 256]) for n in range(2)]
    JK = sb("JK", [128, 1024])
    ST = sb("ST", [128, 64])
    SD = sb("SD", [128, 64])
    RS = sb("RS", [128, 64])
    PS = [ctx.enter_context(nc.psum_tensor(f"PS{n}", [128, 512], F32)) for n in range(8)]
    GD = nc.dram_tensor("gates", [8, 128, 128, 64], F32, kind="Internal")
    IDENT, TRI, ONES, IOTA = (CST[:, n, :] for n in range(4))

    bank_free = [[] for _ in range(8)]
    turn = [0]

    def bank():
        b = turn[0] % 8
        turn[0] += 1
        T.wait(*bank_free[b])
        return b

    d_w = [Arrival(nc, f"d_w{n}") for n in range(2)]
    raw_free = [[], []]
    ws_free = [[], []]
    blocks = [0]

    def prepare(src):
        s = blocks[0] % 2
        blocks[0] += 1
        S.wait(*raw_free[s])
        loaded = d_w[s].did(sp.dma_start(WR[:, s], src))
        A.wait(loaded, *ws_free[s])
        hi = A.did(ac.activation(WS[:, s, 0], WR[:, s], ACT.Copy))
        P.wait(loaded, hi)
        lo = P.did(po.tensor_tensor(WS[:, s, 1], WR[:, s], WS[:, s, 0].bitcast(F32), ALU.subtract))
        raw_free[s] = [hi, lo]
        return s, (hi, lo)

    def stream(list_of_blocks):
        ready = prepare(list_of_blocks[0][0])
        for n, (_, consume) in enumerate(list_of_blocks):
            after = prepare(list_of_blocks[n + 1][0]) if n + 1 < len(list_of_blocks) else None
            s, marks = ready
            T.wait(*marks)
            consume(s)
            ws_free[s] = [T.last()]
            ready = after

    def by_feature(s, half, o, cols):
        n = 0
        for k in range(8):
            for w, h in PARTS:
                ins = te.matmul(o, WS[:, s, w, k, half * 128:half * 128 + 128], HS[:, h, k, 0:cols],
                                start=n == 0, stop=n == 23)
                n += 1
        return T.did(ins)

    def by_token(s, tt, o):
        n = 0
        for k in range(8):
            for w, h in PARTS:
                ins = te.matmul(o, HS[:, h, k, tt * 128:tt * 128 + 128], WS[:, s, w, k, :],
                                start=n == 0, stop=n == 23)
                n += 1
        return T.did(ins)

    def inverse_root(n, width, eps, mark):
        V.wait(mark)
        m = V.did(ve.tensor_scalar(ST[:, 0:n], ST[:, 0:n], 1.0 / width, eps, ALU.mult, ALU.add))
        A.wait(m)
        m = A.did(ac.activation(SD[:, 0:n], ST[:, 0:n], ACT.Sqrt))
        V.wait(m)
        V.did(ve.reciprocal(RS[:, 0:n], SD[:, 0:n]))
        V.own()

    def scales(src, ntt, ready):
        for tt in range(ntt):
            A.wait(*ready[tt])
            A.own()
            m = A.did(ac.activation(JK[:, :], src[:, tt, :], ACT.Square, accum_out=ST[:, tt:tt + 1]))
        inverse_root(ntt, 1024, EPS, m)

    def head_norm(view, sq, n):
        V.did(ve.tensor_tensor(sq, view, view, ALU.mult))
        V.own()
        m = V.did(ve.tensor_reduce(ST[:, 0:n], sq, AX.X, ALU.add))
        inverse_root(n, 64, EPS, m)
        return V.did(ve.tensor_tensor(view, view, RS[:, 0:n].unsqueeze(2).to_broadcast([128, n, 64]), ALU.mult))

    def turn_parts(src, ntt, gain, ready):
        hs_free = T.last()
        for k in range(8):
            b = bank()
            T.wait(*ready)
            for tt in range(ntt):
                ins = te.transpose(PS[b][:, tt * 128:tt * 128 + 128], src[:, tt, k * 128:k * 128 + 128], IDENT)
            m = T.did(ins)
            w = ntt * 128
            g = GN[:, gain + k:gain + k + 1]
            A.wait(m, hs_free)
            hi = A.did(ac.activation(HS[:, 0, k, 0:w], PS[b][:, 0:w], ACT.Copy, scale=g))
            V.wait(hi)
            lo = V.did(ve.scalar_tensor_tensor(HS[:, 1, k, 0:w], PS[b][:, 0:w], g,
                                               HS[:, 0, k, 0:w].bitcast(F32), ALU.mult, ALU.subtract))
            bank_free[b] = [hi, lo]
        T.wait(hi, lo)

    def norm_turned(src, dst, ntt, gain, ready):
        scales(src, ntt, ready)
        for tt in range(ntt):
            m = V.did(ve.tensor_scalar(dst[:, tt, :], src[:, tt, :], RS[:, tt:tt + 1], None, ALU.mult))
        turn_parts(dst, ntt, gain, [m])

    def memory_attention(QT, KT, VAL, scale, Y, col, PM, PT, nM, SU, ready):
        T.wait(*ready)
        pm_free, pt_free = [None, None], [None, None]
        for u in range(8):
            h, half = u // 2, u % 2
            c, p0, s = h // 2, 64 * (h % 2), u % 2
            b = bank()
            for j in range(2):
                tt = 2 * half + j
                ins = te.matmul(PS[b][:, j * 256:j * 256 + 256], QT[p0:p0 + 64, c, tt * 128:tt * 128 + 128],
                                KT[p0:p0 + 64, c, :], start=True, stop=True)
            m = T.did(ins)
            V.wait(m)
            V.own()
            m = V.did(ve.tensor_reduce(nM[:, 2 * u:2 * u + 2], PS[b][:, :].rearrange("p (j m) -> p j m", j=2),
                                       AX.X, ALU.max, negate=True))
            V.wait(m)
            m = V.did(ve.tensor_scalar(nM[:, 2 * u:2 * u + 2], nM[:, 2 * u:2 * u + 2], scale, None, ALU.mult))
            A.wait(m, pm_free[s])
            for j in range(2):
                m = A.did(ac.activation(PM[:, s, j, :], PS[b][:, j * 256:j * 256 + 256], ACT.Exp, scale=scale,
                                        bias=nM[:, 2 * u + j:2 * u + j + 1],
                                        accum_out=SU[:, 2 * u + j:2 * u + j + 1]))
            bank_free[b] = [m]
            V.wait(m)
            V.did(ve.reciprocal(SU[:, 2 * u:2 * u + 2], SU[:, 2 * u:2 * u + 2]))
            b = bank()
            T.wait(m)
            for j in range(2):
                for mt in range(2):
                    ins = te.transpose(PS[b][:, (2 * j + mt) * 128:(2 * j + mt) * 128 + 128],
                                       PM[:, s, j, mt * 128:mt * 128 + 128], IDENT)
            m = T.did(ins)
            pm_free[s] = m
            A.wait(m, pt_free[s])
            m = A.did(ac.activation(PT[:, s, :], PS[b][:, :], ACT.Copy))
            bank_free[b] = [m]
            b = bank()
            T.wait(m)
            for j in range(2):
                for mt in range(2):
                    ins = te.matmul(PS[b][:, j * 64:j * 64 + 64],
                                    PT[:, s, (2 * j + mt) * 128:(2 * j + mt) * 128 + 128],
                                    VAL[:, mt, h * 64:h * 64 + 64], start=mt == 0, stop=mt == 1)
            m = T.did(ins)
            pt_free[s] = m
            V.wait(m)
            V.own()
            m = V.did(ve.tensor_tensor(
                Y[:, 2 * half:2 * half + 2, col + h * 64:col + h * 64 + 64],
                PS[b][:, 0:128].rearrange("p (j d) -> p j d", j=2),
                SU[:, 2 * u:2 * u + 2].unsqueeze(2).to_broadcast([128, 2, 64]), ALU.mult))
            bank_free[b] = [m]

    d_c = Arrival(nc, "d_c")
    d_m = [Arrival(nc, f"d_m{n}") for n in range(2)]
    d_x = Arrival(nc, "d_x")
    d_misc = Arrival(nc, "d_misc")
    d_misc2 = Arrival(nc, "d_misc2")
    d_misc3 = Arrival(nc, "d_misc3")
    got_cst = d_c.did(sp.dma_start(CST[:, :, :], a["cst"]))
    got_gn = d_misc.did(sp.dma_start(GN[:, :], a["small"]))
    for x in (A, V, T):
        x.wait(got_cst, got_gn)

    with ExitStack() as sc:
        ME = [sb(f"ME{n}", [128, 2, 1024], scope=sc) for n in range(2)]
        MK = sb("MK", [128, 2, 256], scope=sc)
        MQ2 = sb("MQ2", [128, 2, 256], scope=sc)
        got_me = [d_m[n].did(sp.dma_start(ME[n][:, :, :], a[f"mem{n}"])) for n in range(2)]
        got_x = d_x.did(sp.dma_start(X[:, :, :], a["x"]))

        def key_tokens(s):
            b = bank()
            for mt in range(2):
                m = by_token(s, mt, PS[b][:, mt * 256:mt * 256 + 256])
            V.wait(m)
            m = V.did(ve.tensor_copy(MK[:, :, :].rearrange("p a b -> p (a b)"), PS[b][:, :]))
            bank_free[b] = [m]

        def key_features(s):
            b = bank()
            for c in range(2):
                m = by_feature(s, c, PS[b][:, c * 256:c * 256 + 256], 256)
            V.wait(m)
            m = V.did(ve.tensor_copy(MKT[1][:, :, :].rearrange("p a b -> p (a b)"), PS[b][:, :]))
            bank_free[b] = [m]

        def values(n):
            def f(s):
                b = bank()
                for mt in range(2):
                    m = by_token(s, mt, PS[b][:, mt * 256:mt * 256 + 256])
                V.wait(m)
                m = V.did(ve.tensor_copy(MV[n][:, :, :].rearrange("p a b -> p (a b)"), PS[b][:, :]))
                bank_free[b] = [m]
            return f

        norm_turned(ME[0], ME[0], 2, G_MEM, [[got_me[0]]] * 2)
        stream([(a["w_mem"][0], key_tokens), (a["w_mem"][1], values(0))])
        V.own()
        m = head_norm(MK[:, :, :].rearrange("p a (h d) -> p (a h) d", d=64),
                      MQ2[:, :, :].rearrange("p a (h d) -> p (a h) d", d=64), 8)
        b = bank()
        T.wait(m)
        for c in range(2):
            for mt in range(2):
                ins = te.transpose(PS[b][:, c * 256 + mt * 128:c * 256 + mt * 128 + 128],
                                   MK[:, mt, c * 128:c * 128 + 128], IDENT)
        m = T.did(ins)
        V.wait(m)
        m = V.did(ve.tensor_scalar(MKT[0][:, :, :].rearrange("p a b -> p (a b)"), PS[b][:, :],
                                   GN[:, G_MK:G_MK + 1], None, ALU.mult))
        bank_free[b] = [m]
        norm_turned(ME[1], ME[1], 2, G_MEM2, [[got_me[1]]] * 2)
        stream([(a["w_mem2"][0], key_features), (a["w_mem2"][1], values(1))])
        fence()

    norm_turned(X, X, 4, G_MIX, [[got_x]] * 4)
    xn_read = T.last()
    MIX = X
    with ExitStack() as sc:
        SQK = sb("SQK", [128, 8, 512], scope=sc)
        SV = sb("SV", [128, 4, 512], scope=sc)
        HI = sb("HI", [128, 4, 256], scope=sc)
        HG = sb("HG", [128, 4, 256], scope=sc)
        MQ = sb("MQ", [128, 4, 256], scope=sc)
        with ExitStack() as hs:
            MASK = sb("MASK", [128, 8, 128], U32, scope=hs)
            QF = sb("QF", [128, 4, 512], scope=hs)
            KK = sb("KK", [128, 4, 512], scope=hs)
            BC = sb("BC", [128, 4, 512], scope=hs)
            LF = sb("LF", [128, 2, 512], scope=hs)
            LB = sb("LB", [128, 3, 2, 512], scope=hs)
            PX = sb("PX", [128, 2, 512], scope=hs)
            PX2 = sb("PX2", [128, 512], scope=hs)
            EX = sb("EX", [128, 2, 128], scope=hs)
            AT = sb("AT", [128, 2, 512], scope=hs)
            AC = sb("AC", [128, 6, 128], scope=hs)
            LW = sb("LW", [128, 4, 4], scope=hs)

            got_mask = d_misc2.did(sp.dma_start(MASK[:, :, :], a["mask"]))
            V.wait(got_mask)
            m = P.did(po.memset(AT[:, :, :], 0.0))
            V.wait(m)
            g0, g1 = GN[:, G_LB:G_LB + 4], GN[:, G_LB + 4:G_LB + 8]
            V.did(ve.tensor_tensor(LW[:, 0, :], g0, g1, ALU.max))
            V.own()
            V.did(ve.tensor_tensor(LW[:, 1, :], g0, LW[:, 0, :], ALU.subtract))
            m = V.did(ve.tensor_tensor(LW[:, 2, :], g1, LW[:, 0, :], ALU.subtract))
            A.wait(m)
            m = A.did(ac.activation(LW[:, 1:3, :], LW[:, 1:3, :], ACT.Exp))
            V.wait(m)
            V.did(ve.tensor_tensor(LW[:, 3, :], LW[:, 1, :], LW[:, 2, :], ALU.add))
            V.own()
            V.did(ve.reciprocal(LW[:, 3, :], LW[:, 3, :]))
            V.own()
            V.did(ve.tensor_tensor(LW[:, 0, :], LW[:, 1, :], LW[:, 3, :], ALU.mult))
            V.own()
            V.did(ve.tensor_scalar(LW[:, 1, :], LW[:, 0, :], -1.0, 1.0, ALU.mult, ALU.add))
            V.own()

            lf_free = [None, None]

            def query_feature(n):
                def f(s):
                    for c in range(2):
                        hd = 2 * n + c
                        b = bank()
                        m = by_feature(s, c, PS[b][:, :], 512)
                        A.wait(m)
                        m = A.did(ac.activation(QF[:, hd, :], PS[b][:, :], ACT.Silu))
                        bank_free[b] = [m]
                        V.wait(m)
                        P.wait(m)
                return f

            def forget_feature(n):
                def f(s):
                    for c in range(2):
                        hd = 2 * n + c
                        b = bank()
                        m = by_feature(s, c, PS[b][:, :], 512)
                        A.wait(m, lf_free[c])
                        m = A.did(ac.activation(LF[:, c, :], PS[b][:, :], ACT.Sigmoid))
                        bank_free[b] = [m]
                        V.wait(m)
                        V.did(ve.tensor_scalar(LF[:, c, :], LF[:, c, :], LW[:, 1, hd:hd + 1], LW[:, 0, hd:hd + 1],
                                               ALU.mult, ALU.add))
                        V.own()
                        m = V.did(ve.tensor_scalar(KK[:, hd, :], LF[:, c, :], -1.0, 1.0, ALU.mult, ALU.add))
                        P.wait(m)
                        T.wait(m)
                        A.wait(m)
                        m = A.did(ac.activation(LF[:, c, :], LF[:, c, :], ACT.Ln))
                        V.wait(m)
                        for tt in range(4):
                            m = V.did(ve.tensor_tensor_scan(BC[:, hd, tt * 128:tt * 128 + 128], ONES,
                                                            LF[:, c, tt * 128:tt * 128 + 128], 0.0,
                                                            ALU.mult, ALU.add))
                        lf_free[c] = m
                        V.own()
                        A.wait(m)
                return f

            def token_pairs(evict):
                def f(s):
                    for t2 in range(2):
                        b = bank()
                        for j in range(2):
                            m = by_token(s, 2 * t2 + j, PS[b][:, j * 256:j * 256 + 256])
                        bank_free[b] = [evict(t2, PS[b][:, :].rearrange("p (j c) -> p j c", j=2), m)]
                return f

            def into(dst, col):
                def f(t2, src, m):
                    V.wait(m)
                    return V.did(ve.tensor_copy(dst[:, 2 * t2:2 * t2 + 2, col:col + 256], src))
                return f

            def gate_into(t2, src, m):
                A.wait(m)
                return A.did(ac.activation(HG[:, 2 * t2:2 * t2 + 2, :], src, ACT.Silu))

            def sb_feature(n):
                def f(s):
                    for c in range(2):
                        b = bank()
                        m = by_feature(s, c, PS[b][:, :], 512)
                        V.wait(m)
                        m = V.did(ve.tensor_copy(SQK[:, 2 * n + c, :], PS[b][:, :]))
                        bank_free[b] = [m]
                return f

            steps = [(hd, lv) for hd in range(4) for lv in range(9)]
            px_free, lb_free = [None, None], [None] * 3
            x_free = [None]
            ac_free = [None]
            at_free = [None, None]
            prepared = {}

            def hg_prepare(n):
                hd, lv = steps[n]
                s, x = n % 3, n % 2
                if lv == 7:
                    prepared[n] = ()
                    return
                if lv < 7:
                    h = LEVELS[lv]
                    nb = 512 // (2 * h)
                    bv = BC[:, hd, :].rearrange("p (n c) -> p n c", c=2 * h)
                    pv = PX[:, x, :].rearrange("p (n c) -> p n c", c=2 * h)
                    ref = bv[:, :, h - 1:h].to_broadcast([128, nb, h])
                    V.wait(*(px_free[x] or ()))
                    V.did(ve.tensor_tensor(pv[:, :, h:], bv[:, :, h:], ref, ALU.subtract))
                    m = V.did(ve.tensor_tensor(pv[:, :, 0:h], ref, bv[:, :, 0:h], ALU.subtract))
                    A.wait(m)
                    m = A.did(ac.activation(PX[:, x, :], PX[:, x, :], ACT.Exp))
                    V.wait(m, lb_free[s])
                    P.wait(m, lb_free[s])
                    q = V.did(ve.tensor_tensor(LB[:, s, 0, :], QF[:, hd, :], PX[:, x, :], ALU.mult))
                    k = P.did(po.tensor_tensor(LB[:, s, 1, :], KK[:, hd, :], PX[:, x, :], ALU.mult))
                    px_free[x] = (q, k)
                    prepared[n] = (q, k)
                    return
                V.wait(*(px_free[x] or ()))
                V.wait(x_free[0])
                A.wait(*(px_free[x] or ()))
                bt = BC[:, hd, :].rearrange("p (n c) -> p n c", c=128)
                m = V.did(ve.tensor_tensor(PX2[:, :].rearrange("p (n c) -> p n c", c=128),
                                           bt[:, :, 127:128].to_broadcast([128, 4, 128]), bt, ALU.subtract))
                m1 = A.did(ac.activation(PX[:, x, :], BC[:, hd, :], ACT.Exp))
                A.wait(m)
                m2 = A.did(ac.activation(PX2[:, :], PX2[:, :], ACT.Exp))
                V.wait(m2, lb_free[s])
                P.wait(m2, lb_free[s])
                q = V.did(ve.tensor_tensor(LB[:, s, 0, :], QF[:, hd, :], PX[:, x, :], ALU.mult))
                k = P.did(po.tensor_tensor(LB[:, s, 1, :], KK[:, hd, :], PX2[:, :], ALU.mult))
                V.wait(q, k)
                V.did(ve.tensor_scalar(EX[:, 0, :], LB[:, s, 0, 384:512], PX[:, x, 383:384], None, ALU.mult))
                q = V.did(ve.tensor_scalar(EX[:, 1, :], LB[:, s, 1, 0:128], PX[:, x, 255:256], None, ALU.mult))
                px_free[x] = (q, k)
                prepared[n] = (q, k)

            def hg_scores(n):
                hd, lv = steps[n]
                s, z = n % 3, hd % 2
                T.wait(*prepared[n])
                if lv < 8:
                    b = bank()
                    for tt in range(4):
                        c = slice(tt * 128, tt * 128 + 128)
                        k = LB[:, s, 1, c] if lv < 7 else KK[:, hd, c]
                        q = LB[:, s, 0, c] if lv < 7 else QF[:, hd, c]
                        ins = te.matmul(PS[b][:, c], k, q, start=True, stop=True)
                    m = T.did(ins)
                    lb_free[s] = m
                    V.wait(m, at_free[z])
                    V.own()
                    m = V.did(ve.copy_predicated(
                        AT[:, z, :].rearrange("p (n c) -> p n c", c=128),
                        MASK[:, lv:lv + 1, :].to_broadcast([128, 4, 128]),
                        PS[b][:, :].rearrange("p (n c) -> p n c", c=128)))
                    bank_free[b] = [m]
                    return
                done = V.last()
                pairs = [(0, 1), (1, 2), (2, 3), (0, 2), (1, 3), (0, 3)]
                for lot in (pairs[0:4], pairs[4:6]):
                    b = bank()
                    for w, (j, i) in enumerate(lot):
                        k = EX[:, 1, :] if (j == 0 and i > 1) else LB[:, s, 1, j * 128:j * 128 + 128]
                        q = EX[:, 0, :] if (i == 3 and j < 2) else LB[:, s, 0, i * 128:i * 128 + 128]
                        ins = te.matmul(PS[b][:, w * 128:w * 128 + 128], k, q, start=True, stop=True)
                    m = T.did(ins)
                    A.wait(m, ac_free[0])
                    at = pairs.index(lot[0])
                    m2 = A.did(ac.activation(AC[:, at:at + len(lot), :].rearrange("p a b -> p (a b)"),
                                             PS[b][:, 0:128 * len(lot)], ACT.Copy))
                    bank_free[b] = [m2]
                lb_free[s] = m
                x_free[0] = m
                b = bank()
                T.wait(m2, done)
                for i in range(4):
                    lhs = [(AT[:, z, i * 128:i * 128 + 128], i)]
                    lhs += [(AC[:, w, :], j) for w, (j, i2) in enumerate(pairs) if i2 == i]
                    for w, (l, j) in enumerate(lhs):
                        ins = te.matmul(PS[b][:, i * 64:i * 64 + 64], l, HI[:, j, hd * 64:hd * 64 + 64],
                                        start=w == 0, stop=w == len(lhs) - 1)
                m = T.did(ins)
                ac_free[0] = m
                at_free[z] = m
                A.wait(m, xn_read)
                m = A.did(ac.activation(MIX[:, :, 512 + hd * 64:576 + hd * 64],
                                        PS[b][:, 0:256].rearrange("p (i d) -> p i d", d=64), ACT.Copy))
                bank_free[b] = [m]

            at_step = [0]

            def with_steps(consume, count=3):
                def f(s):
                    lo, hi = at_step[0], min(at_step[0] + count, len(steps))
                    at_step[0] = hi
                    for n in range(lo, hi):
                        hg_prepare(n)
                    consume(s)
                    T.wait(V.last())
                    for n in range(lo, hi):
                        hg_scores(n)
                return f

            w1 = a["w_in"]
            plan = [(w1[6], query_feature(0)), (w1[7], query_feature(1)),
                    (w1[8], forget_feature(0)), (w1[9], forget_feature(1)),
                    (w1[10], token_pairs(into(HI, 0)))]
            rest = [(11, token_pairs(gate_into)), (12, token_pairs(into(MQ, 0))),
                    (0, sb_feature(0)), (1, sb_feature(1)), (2, sb_feature(2)), (3, sb_feature(3)),
                    (4, token_pairs(into(SV, 0))), (5, token_pairs(into(SV, 256)))]
            plan += [(w1[n], with_steps(f)) for n, f in rest]
            stream(plan)
            while at_step[0] < len(steps):
                with_steps(lambda s: None)(0)
            fence()

        with ExitStack() as hs:
            MQT = sb("MQT", [128, 2, 512], scope=hs)
            ZS = sb("ZS", [128, 2, 1280], scope=hs)
            EE = sb("EE", [128, 1280], scope=hs)
            LL = sb("LL", [128, 2, 1280], scope=hs)
            AA = sb("AA", [128, 2, 1280], scope=hs)
            SQ = sb("SQ", [128, 4, 768], scope=hs)
            PM = sb("PM", [128, 2, 2, 256], scope=hs)
            PT = sb("PT", [128, 2, 512], scope=hs)
            nM = sb("nM", [128, 16], scope=hs)
            SU = sb("SU", [128, 16], scope=hs)
            AT4 = {0: (0, 512), 1: (512, 384), 3: (896, 128), 2: (1024, 256)}
            BANKS = [(0, 512, (0,)), (512, 512, (1, 3)), (1024, 256, (2,))]
            mark_l, mark_a, zs_free, ll_free, aa_free, ee_free = {}, {}, {}, {}, {}, [None]

            def sb_logits(h):
                z, c, p0 = h % 2, h // 2, 64 * (h % 2)
                marks = []
                V.wait(zs_free.get(h - 2))
                for off, width, tiles in BANKS:
                    b = bank()
                    for kt in tiles:
                        o, w = AT4[kt]
                        ins = te.matmul(PS[b][:, o - off:o - off + w], SQK[p0:p0 + 64, 4 + c, kt * 128:kt * 128 + 128],
                                        SQK[p0:p0 + 64, c, kt * 128:512], start=True, stop=True)
                    m = T.did(ins)
                    V.wait(m)
                    m = V.did(ve.tensor_scalar(ZS[:, z, off:off + width], PS[b][:, 0:width], 0.125, None, ALU.mult))
                    bank_free[b] = [m]
                A.wait(m, ee_free[0])
                A.did(ac.activation(EE[:, :], ZS[:, z, :], ACT.Abs))
                A.own()
                A.did(ac.activation(EE[:, :], EE[:, :], ACT.Exp, scale=-1.0))
                A.own()
                m = A.did(ac.activation(EE[:, :], EE[:, :], ACT.Ln, bias=1.0))
                V.wait(m, ll_free.get(h - 2))
                V.own()
                m = V.did(ve.scalar_tensor_tensor(LL[:, z, :], ZS[:, z, :], 0.0, EE[:, :], ALU.max, ALU.add))
                ee_free[0] = m
                P.wait(m)
                for kt in range(4):
                    o = AT4[kt][0]
                    m = P.did(po.affine_select(out=LL[:, z, o:o + 128], in_=LL[:, z, o:o + 128],
                                               compare_op=ALU.is_gt, fill=0.0, base=0, pattern=[[1, 128]],
                                               channel_multiplier=-1))
                mark_l[h] = m

            def sb_tail_scores(h):
                z = h % 2
                T.wait(mark_l[h])
                V.wait(aa_free.get(h - 2))
                for off, width, tiles in BANKS:
                    b = bank()
                    for kt in tiles:
                        o, w = AT4[kt]
                        ins = te.matmul(PS[b][:, o - off:o - off + w], TRI, LL[:, z, o:o + w],
                                        start=True, stop=kt == 3)
                        for k2 in range(kt + 1, 4):
                            o2, w2 = AT4[k2]
                            ins = te.matmul(PS[b][:, o - off + w - w2:o - off + w], ONES, LL[:, z, o2:o2 + w2],
                                            start=False, stop=k2 == 3)
                    m = T.did(ins)
                    V.wait(m)
                    m = V.did(ve.tensor_tensor(AA[:, z, off:off + width], ZS[:, z, off:off + width],
                                               PS[b][:, 0:width], ALU.subtract))
                    bank_free[b] = [m]
                ll_free[h] = T.last()
                zs_free[h] = m
                A.wait(m)
                m = A.did(ac.activation(AA[:, z, :], AA[:, z, :], ACT.Exp))
                P.wait(m)
                for kt in range(4):
                    o = AT4[kt][0]
                    m = P.did(po.affine_select(out=AA[:, z, o:o + 128], in_=AA[:, z, o:o + 128],
                                               compare_op=ALU.is_gt, fill=0.0, base=0, pattern=[[1, 128]],
                                               channel_multiplier=-1))
                mark_a[h] = m

            def sb_out(h):
                z = h % 2
                T.wait(mark_a[h])
                b = bank()
                for qt in range(4):
                    for kt in range(qt + 1):
                        o = AT4[kt][0] + (qt - kt) * 128
                        ins = te.matmul(PS[b][:, qt * 64:qt * 64 + 64], AA[:, z, o:o + 128],
                                        SV[:, kt, h * 64:h * 64 + 64], start=kt == 0, stop=kt == qt)
                m = T.did(ins)
                aa_free[h] = m
                V.wait(m)
                m = V.did(ve.tensor_copy(MIX[:, :, h * 64:h * 64 + 64],
                                         PS[b][:, 0:256].rearrange("p (i d) -> p i d", d=64)))
                bank_free[b] = [m]

            sb_logits(0)
            for h in range(8):
                if h + 1 < 8:
                    sb_logits(h + 1)
                sb_tail_scores(h)
                if h >= 1:
                    sb_out(h - 1)
            sb_out(7)

            V.own()
            m = head_norm(MQ[:, :, :].rearrange("p a (h d) -> p (a h) d", d=64),
                          EE[:, 0:1024].rearrange("p (n d) -> p n d", d=64), 16)
            for c in range(2):
                b = bank()
                T.wait(m)
                for tt in range(4):
                    ins = te.transpose(PS[b][:, tt * 128:tt * 128 + 128], MQ[:, tt, c * 128:c * 128 + 128], IDENT)
                t = T.did(ins)
                V.wait(t)
                e = V.did(ve.tensor_scalar(MQT[:, c, :], PS[b][:, :], GN[:, G_MQ:G_MQ + 1], None, ALU.mult))
                bank_free[b] = [e]
            memory_attention(MQT, MKT[0], MV[0], 0.125, MIX, 768, PM, PT, nM, SU, [e])

            V.wait(A.last())
            V.own()
            for tt in range(4):
                V.did(ve.tensor_tensor(SQ[:, tt, :], MIX[:, tt, 0:768], MIX[:, tt, 0:768], ALU.mult))
            V.own()
            m = V.did(ve.tensor_reduce(ST[:, 0:48], SQ[:, :, :].rearrange("p a (h d) -> p (a h) d", d=64),
                                       AX.X, ALU.add))
            inverse_root(48, 64, EPS, m)
            for tt in range(4):
                V.did(ve.tensor_tensor(
                    MIX[:, tt, 0:768].rearrange("p (h d) -> p h d", d=64),
                    MIX[:, tt, 0:768].rearrange("p (h d) -> p h d", d=64),
                    RS[:, tt * 12:tt * 12 + 12].unsqueeze(2).to_broadcast([128, 12, 64]), ALU.mult))
            V.own()
            m = V.did(ve.tensor_tensor(MIX[:, :, 512:768], MIX[:, :, 512:768], HG[:, :, :], ALU.mult))
            turn_parts(MIX, 4, G_OUT, [m])
            S.wait(T.last())
            got_x = d_x.did(sp.dma_start(X[:, :, :], a["x"]))
            V.wait(got_x)

            def add_out(col):
                def f(t2, src, m):
                    V.wait(m)
                    dst = X[:, 2 * t2:2 * t2 + 2, col:col + 256]
                    return V.did(ve.tensor_tensor(dst, dst, src, ALU.add))
                return f

            stream([(a["w_out"][n], token_pairs(add_out(256 * n))) for n in range(4)])
            fence()

    with ExitStack() as pe_scope:
        HKT = sb("HKT", [128, 3, 512], scope=pe_scope)
        with ExitStack() as sc:
            XN = sb("XN", [128, 4, 1024], scope=sc)
            norm_turned(X, XN, 4, G_FFN, [[V.last()]] * 4)
            fence()
        with ExitStack() as sc:
            KEYS = sb("KEYS", [128, 16, 128], scope=sc)
            QT = sb("QT", [128, 2, 512], scope=sc)
            SC = sb("SC", [128, 4, 16, 128], scope=sc)
            S2 = sb("S2", [128, 16, 128], scope=sc)
            CA = sb("CA", [128, 8, 256], scope=sc)
            EQ = sb("EQ", [128, 8, 256], scope=sc)
            TV = sb("TV", [128, 16, 16], scope=sc)
            TI = sb("TI", [128, 16, 16], U32, scope=sc)
            TF = sb("TF", [128, 16, 16], scope=sc)
            BV = sb("BV", [128, 8, 16], scope=sc)
            BI = sb("BI", [128, 8, 16], U32, scope=sc)
            BP = sb("BP", [128, 2, 8, 16], U32, scope=sc)
            BF = sb("BF", [128, 2, 8, 16], scope=sc)
            HK = sb("HK", [128, 2, 3, 128], scope=sc)
            SM = sb("SM", [128, 2, 8], scope=sc)
            got_keys = d_misc3.did(sp.dma_start(KEYS[:, :, :], a["keys"]))
            T.wait(got_keys)
            qt_free = [None, None]
            score_mark = [None]
            waiting = []

            def scores_of(hc, mark):
                T.wait(mark)
                b = bank()
                for tt in range(4):
                    ins = te.matmul(PS[b][:, tt * 128:tt * 128 + 128], QT[:, hc % 2, tt * 128:tt * 128 + 128],
                                    KEYS[:, hc, :], start=True, stop=True)
                m = T.did(ins)
                qt_free[hc % 2] = m
                A.wait(m)
                m = A.did(ac.activation(SC[:, :, hc, :], PS[b][:, :].rearrange("p (t n) -> p t n", t=4), ACT.Copy))
                bank_free[b] = [m]
                score_mark[0] = m

            def query_block(n):
                def f(s):
                    for c in range(2):
                        hc = 2 * n + c
                        b = bank()
                        m = by_feature(s, c, PS[b][:, :], 512)
                        V.wait(m, qt_free[hc % 2])
                        m = V.did(ve.tensor_copy(QT[:, hc % 2, :], PS[b][:, :]))
                        bank_free[b] = [m]
                        if waiting:
                            scores_of(*waiting.pop())
                        waiting.append((hc, m))
                return f

            stream([(a["w_query"][n], query_block(n)) for n in range(8)])
            scores_of(*waiting.pop())
            V.wait(score_mark[0])
            hk_free = [None, None]
            iota16 = IOTA[:, 0:16].unsqueeze(1).to_broadcast([128, 16, 16])
            for tt in range(4):
                z = tt % 2
                V.own()
                for q in range(16):
                    V.did(ve.max(TV[:, q, 0:8], SC[:, tt, q, :]))
                V.own()
                for q in range(16):
                    V.did(ve.match_replace(S2[:, q, :], TV[:, q, 0:8], SC[:, tt, q, :], NEG))
                V.own()
                for q in range(16):
                    V.did(ve.max(TV[:, q, 8:16], S2[:, q, :]))
                for q in range(16):
                    V.did(ve.max_index(TI[:, q, 0:8], TV[:, q, 0:8], SC[:, tt, q, :]))
                V.own()
                for q in range(16):
                    V.did(ve.max_index(TI[:, q, 8:16], TV[:, q, 8:16], S2[:, q, :]))
                tv = TV[:, :, :].rearrange("p (h c) k -> p h c k", c=2)
                for h in range(8):
                    V.did(ve.tensor_tensor(CA[:, h, :].rearrange("p (i j) -> p i j", i=16),
                                           tv[:, h, 0, :].unsqueeze(2).to_broadcast([128, 16, 16]),
                                           tv[:, h, 1, :].unsqueeze(1).to_broadcast([128, 16, 16]), ALU.add))
                V.own()
                V.did(ve.tensor_copy(TF[:, :, :], TI[:, :, :]))
                for h in range(8):
                    V.did(ve.max(BV[:, h, 0:8], CA[:, h, :]))
                V.own()
                for h in range(8):
                    V.did(ve.max_index(BI[:, h, 0:8], BV[:, h, 0:8], CA[:, h, :]))
                for h in range(8):
                    V.did(ve.match_replace(EQ[:, h, :], BV[:, h, 0:8], CA[:, h, :], NEG))
                V.own()
                for h in range(8):
                    V.did(ve.max(BV[:, h, 8:16], EQ[:, h, :]))
                V.own()
                for h in range(8):
                    V.did(ve.max_index(BI[:, h, 8:16], BV[:, h, 8:16], EQ[:, h, :]))
                V.own()
                V.did(ve.tensor_copy(SM[:, 0, :], BV[:, :, 0]))
                V.own()
                m = V.did(ve.tensor_tensor(BV[:, :, :], BV[:, :, :],
                                           SM[:, 0, :].unsqueeze(2).to_broadcast([128, 8, 16]), ALU.subtract))
                A.wait(m)
                m = A.did(ac.activation(BV[:, :, :], BV[:, :, :], ACT.Exp))
                V.did(ve.tensor_scalar(BP[:, 0], BI[:, :, :], 4, None, ALU.logical_shift_right))
                V.did(ve.tensor_scalar(BP[:, 1], BI[:, :, :], 15, None, ALU.bitwise_and))
                V.own()
                V.did(ve.tensor_copy(BF[:, :, :, :], BP[:, :, :, :]))
                V.wait(m, hk_free[z])
                V.did(ve.tensor_reduce(SM[:, 1, :], BV[:, :, :], AX.X, ALU.add))
                V.own()
                V.did(ve.reciprocal(SM[:, 1, :], SM[:, 1, :]))
                V.own()
                V.did(ve.tensor_tensor(HK[:, z, 2, :].rearrange("p (h k) -> p h k", h=8), BV[:, :, :],
                                       SM[:, 1, :].unsqueeze(2).to_broadcast([128, 8, 16]), ALU.mult))
                tf = TF[:, :, :].rearrange("p (h c) k -> p h c k", c=2)
                for c in range(2):
                    V.own()
                    for h in range(8):
                        V.did(ve.tensor_tensor(EQ[:, h, :].rearrange("p (k e) -> p k e", k=16),
                                               BF[:, c, h, :].unsqueeze(2).to_broadcast([128, 16, 16]), iota16,
                                               ALU.is_equal))
                    V.own()
                    for h in range(8):
                        V.did(ve.tensor_tensor(EQ[:, h, :].rearrange("p (k e) -> p k e", k=16),
                                               EQ[:, h, :].rearrange("p (k e) -> p k e", k=16),
                                               tf[:, h, c, :].unsqueeze(1).to_broadcast([128, 16, 16]), ALU.mult))
                    V.own()
                    m = V.did(ve.tensor_reduce(HK[:, z, c, :],
                                               EQ[:, :, :].rearrange("p h (k e) -> p (h k) e", e=16),
                                               AX.X, ALU.add))
                b = bank()
                T.wait(m)
                for c in range(3):
                    ins = te.transpose(PS[b][:, c * 128:c * 128 + 128], HK[:, z, c, :], IDENT)
                m = T.did(ins)
                hk_free[z] = m
                A.wait(m)
                m = A.did(ac.activation(HKT[:, :, tt * 128:tt * 128 + 128],
                                        PS[b][:, 0:384].rearrange("p (c t) -> p c t", c=3), ACT.Copy))
                bank_free[b] = [m]
            fence()

        with ExitStack() as sc:
            STG = [sb(f"STG{n}", [128, 128, 64], scope=sc) for n in range(2)]
            OI = sb("OI", [128, 2, 8, 128], scope=sc)
            OJ = sb("OJ", [128, 2, 8, 128], scope=sc)
            OA = sb("OA", [128, 2, 8, 128], scope=sc)
            oi_free, oj_free, oa_free = [None] * 2, [None] * 2, [None] * 2
            stg_free = [None, None]
            d_g = [Arrival(nc, f"d_g{n}") for n in range(2)]
            iota8 = IOTA.unsqueeze(1).to_broadcast([128, 8, 128])
            for t8 in range(64):
                z, tb = t8 % 2, t8 // 8
                cols = slice(t8 * 8, t8 * 8 + 8)
                V.wait(oi_free[z])
                mi = V.did(ve.tensor_tensor(OI[:, z], iota8, HKT[:, 0, cols].unsqueeze(2).to_broadcast([128, 8, 128]),
                                            ALU.is_equal))
                V.wait(oj_free[z])
                mj = V.did(ve.tensor_tensor(OJ[:, z], iota8, HKT[:, 1, cols].unsqueeze(2).to_broadcast([128, 8, 128]),
                                            ALU.is_equal))
                A.wait(mi, oa_free[z])
                for t in range(8):
                    ma = A.did(ac.activation(OA[:, z, t, :], OI[:, z, t, :], ACT.Copy,
                                             scale=HKT[:, 2, t8 * 8 + t:t8 * 8 + t + 1]))
                oi_free[z] = ma
                T.wait(mj, ma)
                for half in range(2):
                    b = bank()
                    for t in range(4):
                        ins = te.matmul(PS[b][:, t * 128:t * 128 + 128], OJ[:, z, half * 4 + t, :],
                                        OA[:, z, half * 4 + t, :], start=True, stop=True)
                    m = T.did(ins)
                    t0 = (t8 % 8) * 8 + half * 4
                    V.wait(m, stg_free[tb % 2])
                    e = V.did(ve.tensor_copy(STG[tb % 2][:, :, t0:t0 + 4],
                                             PS[b][:, :].rearrange("p (t i) -> p i t", t=4)))
                    bank_free[b] = [e]
                oj_free[z] = m
                oa_free[z] = m
                if t8 % 8 == 7:
                    S.wait(e)
                    stg_free[tb % 2] = d_g[tb % 2].did(sp.dma_start(GD[tb], STG[tb % 2][:, :, :]))
            S.wait(*stg_free)
            fence()

    with ExitStack() as sc:
        NU, NV, NW, GRP = 3, 6, 6, 4
        VH = sb("VH", [128, NV, 2, 1024], F32R, scope=sc)
        WH = sb("WH", [128, NW, 2, 512], F32R, scope=sc)
        GB = sb("GB", [128, 2, 8, GRP, 64], scope=sc)
        GA = sb("GA", [128, 3, 512], scope=sc)
        wr = WR[:, :, :, :].rearrange("p a b c -> p (a b c)")
        UR = wr[:, 0:2048].rearrange("p (s k e) -> p s k e", s=2, k=8)
        VR = wr[:, 2048:4096].rearrange("p (s d) -> p s d", s=2)
        ws = WS[:, :, :, :, :].rearrange("p a b c d -> p (a b c d)")
        UH = ws[:, 0:NU * 2048].rearrange("p (s w k e) -> p s w k e", s=NU, w=2, k=8)
        d_u = [Arrival(nc, f"d_u{n}") for n in range(2)]
        d_v = [Arrival(nc, f"d_v{n}") for n in range(2)]
        d_gb = [Arrival(nc, f"d_gb{n}") for n in range(2)]
        ur_free, vr_free = [()] * 2, [()] * 2
        uh_free, vh_free, wh_free = [None] * NU, [None] * NV, [None] * NW
        ga_free, gb_free = [()] * 3, [None] * 2
        u_mark, v_mark, w_mark, gb_mark, g_mark = {}, {}, {}, {}, {}

        def load_u(i):
            s, r = i % NU, i % 2
            S.wait(*ur_free[r])
            m = d_u[r].did(sp.dma_start(UR[:, r], a["u"][i]))
            A.wait(m, uh_free[s])
            hi = A.did(ac.activation(UH[:, s, 0], UR[:, r], ACT.Copy))
            V.wait(hi)
            lo = V.did(ve.tensor_tensor(UH[:, s, 1], UR[:, r], UH[:, s, 0].bitcast(F32), ALU.subtract))
            ur_free[r] = (hi, lo)
            u_mark[i] = (hi, lo)

        def load_v(i):
            s, r = i % NV, i % 2
            S.wait(*vr_free[r])
            m = d_v[r].did(sp.dma_start(VR[:, r], a["v"][i]))
            A.wait(m, vh_free[s])
            hi = A.did(ac.activation(VH[:, s, 0], VR[:, r], ACT.Copy))
            P.wait(hi)
            lo = P.did(po.tensor_tensor(VH[:, s, 1], VR[:, r], VH[:, s, 0].bitcast(F32), ALU.subtract))
            vr_free[r] = (hi, lo)
            v_mark[i] = (hi, lo)

        def load_g(g):
            S.wait(gb_free[g % 2])
            src = GD[:, :, g * GRP:g * GRP + GRP, :].rearrange("b p i t -> p b (i t)")
            gb_mark[g] = d_gb[g % 2].did(sp.dma_start(GB[:, g % 2].rearrange("p b i t -> p b (i t)"), src))

        def activate(i):
            s, z, g = i % NU, i % 3, i // GRP
            T.wait(*u_mark[i])
            b = bank()
            n = 0
            for k in range(8):
                for w, h in PARTS:
                    ins = te.matmul(PS[b][:, :], UH[:, s, w, k, :], HS[:, h, k, :], start=n == 0, stop=n == 23)
                    n += 1
            m = T.did(ins)
            uh_free[s] = m
            A.wait(m, *ga_free[z])
            m = A.did(ac.activation(GA[:, z, :], PS[b][:, :], ACT.Gelu))
            bank_free[b] = [m]
            V.wait(m, gb_mark[g])
            m = V.did(ve.tensor_tensor(GA[:, z, :].rearrange("p (b t) -> p b t", b=8),
                                       GA[:, z, :].rearrange("p (b t) -> p b t", b=8),
                                       GB[:, g % 2, :, i % GRP, :], ALU.mult))
            gb_free[g % 2] = m
            g_mark[i] = m

        def part(i):
            z = i % 3
            A.wait(g_mark[i], wh_free[i % NW])
            hi = A.did(ac.activation(WH[:, i % NW, 0, :], GA[:, z, :], ACT.Copy))
            V.wait(hi)
            lo = V.did(ve.tensor_tensor(WH[:, i % NW, 1, :], GA[:, z, :], WH[:, i % NW, 0, :].bitcast(F32),
                                        ALU.subtract))
            ga_free[z] = (hi, lo)
            w_mark[i] = (hi, lo)

        def combine(g, part):
            tt, dh = part // 2, part % 2
            b = bank()
            n = 0
            for i in range(g * GRP, g * GRP + GRP):
                T.wait(*w_mark[i], *v_mark[i])
                for w, v in PARTS:
                    ins = te.matmul(PS[b][:, :], WH[:, i % NW, w, tt * 128:tt * 128 + 128],
                                    VH[:, i % NV, v, dh * 512:dh * 512 + 512], start=n == 0, stop=n == 3 * GRP - 1)
                    n += 1
            m = T.did(ins)
            if part == 7:
                for i in range(g * GRP, g * GRP + GRP):
                    vh_free[i % NV] = m
                    wh_free[i % NW] = m
            V.wait(m)
            V.own()
            dst = X[:, tt, dh * 512:dh * 512 + 512]
            bank_free[b] = [V.did(ve.tensor_tensor(dst, dst, PS[b][:, :], ALU.add))]

        NG = 128 // GRP
        load_g(0)
        load_u(0)
        for g in range(NG + 1):
            if g + 1 < NG:
                load_g(g + 1)
            for ii in range(GRP):
                i = g * GRP + ii
                if i + 1 < 128:
                    load_u(i + 1)
                if g < NG:
                    if ii < 2:
                        load_v(i)
                    activate(i)
                    if ii < 2:
                        part(i)
                if g >= 1:
                    combine(g - 1, 2 * ii)
                    combine(g - 1, 2 * ii + 1)
            for ii in range(2, GRP):
                if g < NG:
                    part(g * GRP + ii)
                    load_v(g * GRP + ii)
        fence()

    with ExitStack() as sc:
        DT = sb("DT", [128, 3, 512], scope=sc)
        Y = sb("Y", [128, 4, 1024], scope=sc)
        QT2 = sb("QT2", [128, 6, 512], scope=sc)
        KT2 = sb("KT2", [128, 6, 512], scope=sc)
        V2 = sb("V2", [128, 4, 768], scope=sc)
        QM = sb("QM", [128, 2, 512], scope=sc)
        SP2 = sb("SP2", [128, 2, 1280], scope=sc)
        PT2 = sb("PT2", [128, 2, 1280], scope=sc)
        PM = sb("PM2", [128, 2, 2, 256], scope=sc)
        PT = sb("PTm", [128, 2, 512], scope=sc)
        nM = sb("nM2", [128, 32], scope=sc)
        SU = sb("SU2", [128, 32], scope=sc)
        d_d = Arrival(nc, "d_d")
        got_d = d_d.did(sp.dma_start(DT[:, :, :], a["dist"]))
        V.wait(got_d)
        norm_turned(X, Y, 4, G_N2, [[V.last()]] * 4)
        y_free = T.last()

        def features(dst, n, scale):
            def f(s):
                for c in range(2):
                    b = bank()
                    m = by_feature(s, c, PS[b][:, :], 512)
                    A.wait(m)
                    m = A.did(ac.activation(dst[:, 2 * n + c, :], PS[b][:, :], ACT.Copy, scale=scale))
                    bank_free[b] = [m]
            return f

        def pairs_of(evict):
            def f(s):
                for t2 in range(2):
                    b = bank()
                    for j in range(2):
                        m = by_token(s, 2 * t2 + j, PS[b][:, j * 256:j * 256 + 256])
                    bank_free[b] = [evict(t2, PS[b][:, :].rearrange("p (j c) -> p j c", j=2), m)]
            return f

        def v_into(col):
            def f(t2, src, m):
                V.wait(m)
                return V.did(ve.tensor_copy(V2[:, 2 * t2:2 * t2 + 2, col:col + 256], src))
            return f

        w2 = a["w_in2"]
        stream([(w2[n], features(QT2, n, 0.125)) for n in range(3)]
               + [(w2[3 + n], features(KT2, n, 1.0)) for n in range(3)]
               + [(w2[6 + n], pairs_of(v_into(256 * n))) for n in range(3)]
               + [(w2[9], features(QM, 0, 0.125))])

        T.wait(A.last(), V.last())
        V.wait(y_free)
        units = [(hh, qt) for hh in range(4) for qt in range(4)]
        sp_free, pt_free = [None, None], [None, None]
        exp_mark = {}

        def lay(qt):
            tiles, o = [], 0
            for g in range(3):
                c0 = max(0, qt - 1) if g == 0 else 0
                tiles.append((o, c0, qt + 1 - c0))
                o += (qt + 1 - c0) * 128
            return tiles, o

        def window_scores(u):
            hh, qt = units[u]
            z = u % 2
            tiles, total = lay(qt)
            for g, (o, c0, n) in enumerate(tiles):
                hd = g * 4 + hh
                c, p0 = hd // 2, 64 * (hd % 2)
                b = bank()
                m = T.did(te.matmul(PS[b][:, 0:n * 128], QT2[p0:p0 + 64, c, qt * 128:qt * 128 + 128],
                                    KT2[p0:p0 + 64, c, c0 * 128:(qt + 1) * 128], start=True, stop=True))
                V.wait(m, sp_free[z])
                m = V.did(ve.scalar_tensor_tensor(SP2[:, z, o:o + n * 128], DT[:, g, 512 - n * 128:512], SLOPES[hd],
                                                  PS[b][:, 0:n * 128], ALU.mult, ALU.add))
                bank_free[b] = [m]
            V.own()
            m = V.did(ve.tensor_reduce(nM[:, u:u + 1], SP2[:, z, 0:total], AX.X, ALU.max, negate=True))
            A.wait(m)
            m = A.did(ac.activation(SP2[:, z, 0:total], SP2[:, z, 0:total], ACT.Exp, bias=nM[:, u:u + 1],
                                    accum_out=SU[:, u:u + 1]))
            exp_mark[u] = m

        def window_out(u):
            hh, qt = units[u]
            z = u % 2
            tiles, total = lay(qt)
            nblk = total // 128
            V.wait(exp_mark[u])
            V.did(ve.reciprocal(SU[:, u:u + 1], SU[:, u:u + 1]))
            for lot in range(0, nblk, 4):
                k = min(4, nblk - lot)
                b = bank()
                T.wait(exp_mark[u])
                for w in range(k):
                    ins = te.transpose(PS[b][:, w * 128:w * 128 + 128],
                                       SP2[:, z, (lot + w) * 128:(lot + w) * 128 + 128], IDENT)
                m = T.did(ins)
                A.wait(m, pt_free[z])
                e = A.did(ac.activation(PT2[:, z, lot * 128:(lot + k) * 128], PS[b][:, 0:k * 128], ACT.Copy))
                bank_free[b] = [e]
            sp_free[z] = m
            b = bank()
            T.wait(e)
            for g, (o, c0, n) in enumerate(tiles):
                hd = g * 4 + hh
                for w in range(n):
                    ins = te.matmul(PS[b][:, g * 64:g * 64 + 64], PT2[:, z, o + w * 128:o + w * 128 + 128],
                                    V2[:, c0 + w, hd * 64:hd * 64 + 64], start=w == 0, stop=w == n - 1)
            m = T.did(ins)
            pt_free[z] = m
            V.wait(m)
            V.own()
            m = V.did(ve.tensor_scalar(
                Y[:, qt, 0:768].rearrange("p (g c) -> p g c", g=3)[:, :, hh * 64:hh * 64 + 64],
                PS[b][:, 0:192].rearrange("p (g d) -> p g d", g=3), SU[:, u:u + 1], None, ALU.mult))
            bank_free[b] = [m]

        window_scores(0)
        for u in range(16):
            if u + 1 < 16:
                window_scores(u + 1)
            window_out(u)
        V.own()
        memory_attention(QM, MKT[1], MV[1], 1.0, Y, 768, PM, PT, nM[:, 16:32], SU[:, 16:32], [])

        sg_free = [None, None]
        SG = SP2[:, :, 0:512].rearrange("p s (j c) -> p s j c", j=2)
        A.wait(T.last())

        def gate_block(n):
            def evict(t2, src, m):
                A.wait(m, sg_free[t2])
                m = A.did(ac.activation(SG[:, t2], src, ACT.Silu))
                V.wait(m)
                V.own()
                dst = Y[:, 2 * t2:2 * t2 + 2, n * 256:n * 256 + 256]
                sg_free[t2] = V.did(ve.tensor_tensor(dst, dst, SG[:, t2], ALU.mult))
                return m
            return evict

        stream([(w2[10 + n], pairs_of(gate_block(n))) for n in range(4)])
        hs_free = T.last()
        ready = V.last()
        for k in range(8):
            b = bank()
            T.wait(ready)
            for tt in range(4):
                ins = te.transpose(PS[b][:, tt * 128:tt * 128 + 128], Y[:, tt, k * 128:k * 128 + 128], IDENT)
            m = T.did(ins)
            A.wait(m, hs_free)
            hi = A.did(ac.activation(HS[:, 0, k, :], PS[b][:, :], ACT.Copy))
            V.wait(hi)
            lo = V.did(ve.tensor_tensor(HS[:, 1, k, :], PS[b][:, :], HS[:, 0, k, :].bitcast(F32), ALU.subtract))
            bank_free[b] = [hi, lo]
        T.wait(hi, lo)
        y_done = T.last()

        def add_out2(col):
            def f(t2, src, m):
                V.wait(m)
                V.own()
                dst = X[:, 2 * t2:2 * t2 + 2, col:col + 256]
                return V.did(ve.tensor_tensor(dst, dst, src, ALU.add))
            return f

        stream([(a["w_out2"][n], pairs_of(add_out2(256 * n))) for n in range(4)])
        FG = Y[:, 0, :]
        S.wait(y_done)
        got_f = d_misc3.did(sp.dma_start(FG, a["final"]))
        scales(X, 4, [[V.last()]] * 4)
        V.wait(got_f)
        d_o = [Arrival(nc, f"d_o{n}") for n in range(4)]
        for tt in range(4):
            m = V.did(ve.scalar_tensor_tensor(X[:, tt, :], X[:, tt, :], RS[:, tt:tt + 1], FG, ALU.mult, ALU.mult))
            S.wait(m)
            d_o[tt].did(sp.dma_start(out[tt], X[:, tt, :]))
        S.wait(*[d.last() for d in d_o])
        fence()
    ctx.__exit__(None, None, None)


def constants():
    p = np.arange(128)
    cst = np.zeros((128, 4, 128), np.float32)
    cst[:, 0] = np.eye(128)
    cst[:, 1] = p[:, None] >= p[None, :]
    cst[:, 2] = 1.0
    cst[:, 3] = p[None, :]
    mask = np.zeros((128, 8, 128), np.uint32)
    s, t = p[:, None], p[None, :]
    for n, h in enumerate(LEVELS):
        mask[:, n] = (s // (2 * h) == t // (2 * h)) & (s % (2 * h) < h) & (t % (2 * h) >= h)
    mask[:, 7] = s == t
    d = p[:, None] - np.arange(512)[None, :] + 384
    dist = np.zeros((128, 3, 512), np.float32)
    for g, (window, dil) in enumerate(((128, 1), (512, 4), (2048, 16))):
        dist[:, g] = np.where((d >= 0) & (d <= window) & (d % dil == 0), -d, -1e30)
    return cst, mask, dist


def kernel(**inputs):
    import concourse.bacc as _bacc
    from concourse import mybir as _mybir
    from concourse.bass_utils import run_bass_kernel_spmd as _run

    i = {k: np.asarray(v) for k, v in inputs.items()}

    def tiles(x):
        return np.ascontiguousarray(x.reshape(-1, 128, 1024).transpose(1, 0, 2))

    def weight(w):
        return np.ascontiguousarray(w.reshape(8, 128, -1, 256).transpose(2, 1, 0, 3))

    def column(g):
        return g.reshape(-1, 128).T

    cst, mask, dist = constants()
    small = np.concatenate(
        [column(i["norm_mix_gain"]), column(i["norm_ffn_gain"]), column(i["norm_g_2"]), column(i["mem_norm_gain"]),
         column(i["mem_norm_g_2"]), column(i["sb_out_gain"]), column(i["hg_out_gain"]), np.ones((128, 2), np.float32),
         column(i["gamma_lb"]), column(np.tile(i["mem_q_gain"][0], 2)), column(np.tile(i["mem_k_gain"][0], 2))], axis=1)
    arrays = {
        "x": tiles(i["x"][0]), "mem0": tiles(i["mem"][0]), "mem1": tiles(i["mem_2"][0]),
        "w_in": weight(i["w_in"][0]), "w_mem": weight(i["w_mem_kv"][0]), "w_out": weight(i["w_out"][0]),
        "w_query": weight(i["peer_w_query"][0]), "w_in2": weight(i["w_in_2"][0]),
        "w_mem2": weight(i["w_mem_kv_2"][0]), "w_out2": weight(i["w_out_2"][0]),
        "keys": np.ascontiguousarray(i["peer_sub_keys"][0].reshape(16, 128, 128).transpose(2, 0, 1)),
        "u": np.ascontiguousarray(i["peer_u"][0].reshape(128, 128, 8, 128).transpose(0, 3, 2, 1)),
        "v": np.ascontiguousarray(i["peer_v"][0].reshape(128, 128, 1024)),
        "small": np.ascontiguousarray(small), "final": np.tile(i["final_norm_g_2"][None, :], (128, 1)),
        "cst": cst, "mask": mask, "dist": dist,
    }
    nc = _bacc.Bacc("TRN2", target_bir_lowering=False, num_devices=1)
    named, sent = {}, {}
    for name, x in arrays.items():
        sent[f"in_{name}"] = x
        named[name] = nc.dram_tensor(f"in_{name}", x.shape, _mybir.dt.from_np(x.dtype), kind="ExternalInput").ap()
    out = nc.dram_tensor("out_0", (4, 128, 1024), _mybir.dt.float32, kind="ExternalOutput").ap()
    program(nc, named, out)
    r = _run(nc, [sent], core_ids=[0])
    return np.asarray(r.results[0]["out_0"]).reshape(1, 512, 1024)
```

```python
from contextlib import ExitStack

import numpy as np

import concourse.bass as bass
from concourse import mybir

F32 = mybir.dt.float32
F32R = mybir.dt.float32r
U32 = mybir.dt.uint32
ALU = mybir.AluOpType
ACT = mybir.ActivationFunctionType
AX = mybir.AxisListType

EPS = 1e-6
NEG = -3.0e38
SLOPES = [float(np.float32(2.0 ** (-8.0 * n / 12))) for n in range(1, 13)]
TBLK = 32
LEVELS = [64, 32, 16, 8, 4, 2, 1]
G_MIX, G_FFN, G_N2, G_MEM, G_MEM2, G_OUT, G_LB, G_MQ, G_MK = 0, 8, 16, 24, 32, 40, 48, 56, 57
SMALL = 58
PARTS = ((0, 0), (0, 1), (1, 0))


class Engine:

    def __init__(self, nc, eng, name):
        self.e = eng
        self.sem = nc.alloc_semaphore(name)
        self.n = 0
        self.seen = {}

    def wait(self, *marks):
        for m in marks:
            if m is None:
                continue
            sem, v, key = m
            if self.seen.get(key, 0) < v:
                self.e.wait_ge(sem, v)
                self.seen[key] = v

    def did(self, ins):
        self.n += 1
        ins.then_inc(self.sem, 1)
        return self.last()

    def last(self):
        return (self.sem, self.n, id(self))

    def own(self):
        self.wait(self.last())


class Arrival:

    def __init__(self, nc, name):
        self.sem = nc.alloc_semaphore(name)
        self.n = 0

    def did(self, ins):
        self.n += 16
        ins.then_inc(self.sem, 16)
        return self.last()

    def last(self):
        return (self.sem, self.n, id(self))


def program(nc, a, out):
    V = Engine(nc, nc.vector, "s_dve")
    A = Engine(nc, nc.scalar, "s_act")
    T = Engine(nc, nc.tensor, "s_pe")
    P = Engine(nc, nc.gpsimd, "s_pool")
    S = Engine(nc, nc.sync, "s_sp")
    ve, ac, te, po, sp = nc.vector, nc.scalar, nc.tensor, nc.gpsimd, nc.sync

    def fence():
        marks = [x.last() for x in (V, A, T, P)]
        for x in (V, A, T, P):
            x.wait(*marks)
        return marks

    ctx = ExitStack()

    def sb(name, shape, dt=F32, scope=None):
        return (scope or ctx).enter_context(nc.sbuf_tensor(name, shape, dt))

    ctx.__enter__()
    HS = sb("HS", [128, 2, 8, 512], F32R)
    WS = sb("WS", [128, 2, 2, 8, 256], F32R)
    WR = sb("WR", [128, 2, 8, 256])
    X = sb("X", [128, 4, 1024])
    CST = sb("CST", [128, 4, 128])
    GN = sb("GN", [128, SMALL])
    MKT = [sb(f"MKT{n}", [128, 2, 256]) for n in range(2)]
    MV = [sb(f"MV{n}", [128, 2, 256]) for n in range(2)]
    JK = sb("JK", [128, 1024])
    ST = sb("ST", [128, 64])
    SD = sb("SD", [128, 64])
    RS = sb("RS", [128, 64])
    PS = [ctx.enter_context(nc.psum_tensor(f"PS{n}", [128, 512], F32)) for n in range(8)]
    IDENT, TRI, ONES, IOTA = (CST[:, n, :] for n in range(4))

    bank_free = [[] for _ in range(8)]
    turn = [0]

    def bank():
        b = turn[0] % 8
        turn[0] += 1
        T.wait(*bank_free[b])
        return b

    d_w = [Arrival(nc, f"d_w{n}") for n in range(2)]
    raw_free = [[], []]
    ws_free = [[], []]
    hs_mark = [[] for _ in range(8)]
    fetched, parted, blocks = [], [], [0]

    def fetch(src):
        s = blocks[0] % 2
        blocks[0] += 1
        S.wait(*raw_free[s])
        fetched.append((s, d_w[s].did(sp.dma_start(WR[:, s], src))))

    def part_next():
        s, loaded = fetched.pop(0)
        A.wait(loaded, *ws_free[s])
        hi = A.did(ac.activation(WS[:, s, 0], WR[:, s], ACT.Copy))
        P.wait(loaded, hi)
        lo = P.did(po.tensor_tensor(WS[:, s, 1], WR[:, s], WS[:, s, 0].bitcast(F32), ALU.subtract))
        raw_free[s] = [hi, lo]
        parted.append((s, (hi, lo)))

    def stream(work, then=()):
        sources = [w[0] for w in work] + list(then)[0:2]
        n_fetched = len(fetched) + len(parted)
        while n_fetched < min(2, len(sources)):
            fetch(sources[n_fetched])
            n_fetched += 1
        if not parted:
            part_next()
        for n, (_, consume) in enumerate(work):
            if n + 1 < len(work) and len(parted) < 2:
                part_next()
            s, marks = parted.pop(0)
            if n_fetched < len(sources):
                fetch(sources[n_fetched])
                n_fetched += 1
            T.wait(*marks)
            consume(s)
            ws_free[s] = [T.last()]

    def by_feature(s, half, o, cols, src=None):
        n = 0
        src = HS if src is None else src
        for k in range(8):
            T.wait(*hs_mark[k])
            for w, h in PARTS:
                ins = te.matmul(o, WS[:, s, w, k, half * 128:half * 128 + 128], src[:, h, k, 0:cols],
                                start=n == 0, stop=n == 23)
                n += 1
        return T.did(ins)

    def by_token(s, tt, o, src=None):
        n = 0
        src = HS if src is None else src
        for k in range(8):
            T.wait(*hs_mark[k])
            for w, h in PARTS:
                ins = te.matmul(o, src[:, h, k, tt * 128:tt * 128 + 128], WS[:, s, w, k, :],
                                start=n == 0, stop=n == 23)
                n += 1
        return T.did(ins)

    def inverse_root(n, width, eps, mark):
        V.wait(mark)
        m = V.did(ve.tensor_scalar(ST[:, 0:n], ST[:, 0:n], 1.0 / width, eps, ALU.mult, ALU.add))
        A.wait(m)
        m = A.did(ac.activation(SD[:, 0:n], ST[:, 0:n], ACT.Sqrt))
        V.wait(m)
        V.did(ve.reciprocal(RS[:, 0:n], SD[:, 0:n]))
        V.own()

    def scales(src, ntt, ready):
        for tt in range(ntt):
            A.wait(*ready[tt])
            A.own()
            m = A.did(ac.activation(JK[:, :], src[:, tt, :], ACT.Square, accum_out=ST[:, tt:tt + 1]))
        inverse_root(ntt, 1024, EPS, m)

    def head_norm(view, sq, n):
        V.did(ve.tensor_tensor(sq, view, view, ALU.mult))
        V.own()
        m = V.did(ve.tensor_reduce(ST[:, 0:n], sq, AX.X, ALU.add))
        inverse_root(n, 64, EPS, m)
        return V.did(ve.tensor_tensor(view, view, RS[:, 0:n].unsqueeze(2).to_broadcast([128, n, 64]), ALU.mult))

    def turn_parts(src, ntt, gain, ready, dst=None):
        hs_free = T.last()
        dst = HS if dst is None else dst
        for k in range(8):
            b = bank()
            T.wait(*ready)
            for tt in range(ntt):
                ins = te.transpose(PS[b][:, tt * 128:tt * 128 + 128], src[:, tt, k * 128:k * 128 + 128], IDENT)
            m = T.did(ins)
            w = ntt * 128
            g = GN[:, gain + k:gain + k + 1]
            A.wait(m, hs_free)
            hi = A.did(ac.activation(dst[:, 0, k, 0:w], PS[b][:, 0:w], ACT.Copy, scale=g))
            V.wait(hi)
            lo = V.did(ve.scalar_tensor_tensor(dst[:, 1, k, 0:w], PS[b][:, 0:w], g,
                                               dst[:, 0, k, 0:w].bitcast(F32), ALU.mult, ALU.subtract))
            bank_free[b] = [hi, lo]
            hs_mark[k] = [hi, lo]

    def norm_turned(src, dst, ntt, gain, ready, parts=None):
        scales(src, ntt, ready)
        for tt in range(ntt):
            m = V.did(ve.tensor_scalar(dst[:, tt, :], src[:, tt, :], RS[:, tt:tt + 1], None, ALU.mult))
        turn_parts(dst, ntt, gain, [m], parts)

    def skew(*lines):
        for step in range(max(n + len(st) - 1 for n, st in lines)):
            for n, st in lines:
                for k, f in enumerate(st):
                    if 0 <= step - k < n:
                        f(step - k)

    def memory_attention(QT, KT, VAL, scale, Y, col, PM, PT, nM, SU, TMP=None):
        pm_free, pt_free, exp_mark, pt_mark = [None, None], [None, None], {}, {}

        def logits(u):
            h, half = u // 2, u % 2
            c, p0, s = h // 2, 64 * (h % 2), u % 2
            b = bank()
            for j in range(2):
                tt = 2 * half + j
                ins = te.matmul(PS[b][:, j * 256:j * 256 + 256], QT[p0:p0 + 64, c, tt * 128:tt * 128 + 128],
                                KT[p0:p0 + 64, c, :], start=True, stop=True)
            m = T.did(ins)
            V.wait(m)
            m = V.did(ve.tensor_reduce(nM[:, 2 * u:2 * u + 2], PS[b][:, :].rearrange("p (j m) -> p j m", j=2),
                                       AX.X, ALU.max, negate=True))
            V.wait(m)
            m = V.did(ve.tensor_scalar(nM[:, 2 * u:2 * u + 2], nM[:, 2 * u:2 * u + 2], scale, None, ALU.mult))
            A.wait(m, pm_free[s])
            for j in range(2):
                m = A.did(ac.activation(PM[:, s, j, :], PS[b][:, j * 256:j * 256 + 256], ACT.Exp, scale=scale,
                                        bias=nM[:, 2 * u + j:2 * u + j + 1],
                                        accum_out=SU[:, 2 * u + j:2 * u + j + 1]))
            bank_free[b] = [m]
            exp_mark[u] = m

        def turned(u):
            s = u % 2
            b = bank()
            T.wait(exp_mark[u])
            for j in range(2):
                for mt in range(2):
                    ins = te.transpose(PS[b][:, (2 * j + mt) * 128:(2 * j + mt) * 128 + 128],
                                       PM[:, s, j, mt * 128:mt * 128 + 128], IDENT)
            m = T.did(ins)
            pm_free[s] = m
            A.wait(m, pt_free[s])
            m = A.did(ac.activation(PT[:, s, :], PS[b][:, :], ACT.Copy))
            bank_free[b] = [m]
            pt_mark[u] = m

        def outs(u):
            h, half = u // 2, u % 2
            s = u % 2
            V.wait(exp_mark[u])
            V.did(ve.reciprocal(SU[:, 2 * u:2 * u + 2], SU[:, 2 * u:2 * u + 2]))
            b = bank()
            T.wait(pt_mark[u])
            for j in range(2):
                for mt in range(2):
                    ins = te.matmul(PS[b][:, j * 64:j * 64 + 64],
                                    PT[:, s, (2 * j + mt) * 128:(2 * j + mt) * 128 + 128],
                                    VAL[:, mt, h * 64:h * 64 + 64], start=mt == 0, stop=mt == 1)
            m = T.did(ins)
            pt_free[s] = m
            V.wait(m)
            V.own()
            dst = Y[:, 2 * half:2 * half + 2, col + h * 64:col + h * 64 + 64]
            m = V.did(ve.tensor_tensor(
                dst if TMP is None else TMP, PS[b][:, 0:128].rearrange("p (j d) -> p j d", j=2),
                SU[:, 2 * u:2 * u + 2].unsqueeze(2).to_broadcast([128, 2, 64]), ALU.mult))
            bank_free[b] = [m]
            if TMP is not None:
                V.own()
                V.did(ve.tensor_tensor(dst, dst, TMP, ALU.mult))

        return logits, turned, outs

    d_c = Arrival(nc, "d_c")
    d_m = [Arrival(nc, f"d_m{n}") for n in range(2)]
    d_x = [Arrival(nc, f"d_x{n}") for n in range(4)]
    d_misc = Arrival(nc, "d_misc")
    d_misc2 = Arrival(nc, "d_misc2")
    d_misc3 = Arrival(nc, "d_misc3")
    got_cst = d_c.did(sp.dma_start(CST[:, :, :], a["cst"]))
    got_gn = d_misc.did(sp.dma_start(GN[:, :], a["small"]))
    for x in (A, V, T):
        x.wait(got_cst, got_gn)

    w1 = a["w_in"]
    got_x = [d.did(sp.dma_start(X[:, tt, :], a["x"][:, tt, :])) for tt, d in enumerate(d_x)]
    fetch(w1[6])
    fetch(w1[7])
    norm_turned(X, X, 4, G_MIX, [[g] for g in got_x])
    xn_read = T.last()
    MIX = X
    with ExitStack() as sc:
        with nc.sbuf_tensor("HSM", [128, 2, 8, 256], F32R) as HSM:
            with nc.sbuf_tensor("ME", [128, 2, 1024], F32) as ME:
                got_me = [d_m[0].did(sp.dma_start(ME[:, :, :], a["mem0"])), None]
        SQK = sb("SQK", [128, 8, 512], scope=sc)
        SV = sb("SV", [128, 4, 512], scope=sc)
        HI = sb("HI", [128, 4, 256], scope=sc)
        HG = sb("HG", [128, 4, 256], scope=sc)
        MQ = sb("MQ", [128, 4, 256], scope=sc)
        MK = sb("MK", [128, 2, 256], scope=sc)
        with ExitStack() as hs:
            MASK = sb("MASK", [128, 8, 128], U32, scope=hs)
            QF = sb("QF", [128, 4, 512], scope=hs)
            KK = sb("KK", [128, 4, 512], scope=hs)
            BC = sb("BC", [128, 4, 512], scope=hs)
            LF = sb("LF", [128, 2, 512], scope=hs)
            LB = sb("LB", [128, 3, 2, 512], scope=hs)
            PX = sb("PX", [128, 2, 512], scope=hs)
            PX2 = sb("PX2", [128, 512], scope=hs)
            EX = sb("EX", [128, 2, 128], scope=hs)
            AT = sb("AT", [128, 2, 512], scope=hs)
            AC = sb("AC", [128, 6, 128], scope=hs)
            LW = sb("LW", [128, 4, 4], scope=hs)

            got_mask = d_misc2.did(sp.dma_start(MASK[:, :, :], a["mask"]))
            V.wait(got_mask)
            m = P.did(po.memset(AT[:, :, :], 0.0))
            V.wait(m)
            g0, g1 = GN[:, G_LB:G_LB + 4], GN[:, G_LB + 4:G_LB + 8]
            V.did(ve.tensor_tensor(LW[:, 0, :], g0, g1, ALU.max))
            V.own()
            V.did(ve.tensor_tensor(LW[:, 1, :], g0, LW[:, 0, :], ALU.subtract))
            m = V.did(ve.tensor_tensor(LW[:, 2, :], g1, LW[:, 0, :], ALU.subtract))
            A.wait(m)
            m = A.did(ac.activation(LW[:, 1:3, :], LW[:, 1:3, :], ACT.Exp))
            V.wait(m)
            V.did(ve.tensor_tensor(LW[:, 3, :], LW[:, 1, :], LW[:, 2, :], ALU.add))
            V.own()
            V.did(ve.reciprocal(LW[:, 3, :], LW[:, 3, :]))
            V.own()
            V.did(ve.tensor_tensor(LW[:, 0, :], LW[:, 1, :], LW[:, 3, :], ALU.mult))
            V.own()
            V.did(ve.tensor_scalar(LW[:, 1, :], LW[:, 0, :], -1.0, 1.0, ALU.mult, ALU.add))
            V.own()

            lf_free = [None, None]

            def query_feature(n):
                def f(s):
                    for c in range(2):
                        hd = 2 * n + c
                        b = bank()
                        m = by_feature(s, c, PS[b][:, :], 512)
                        A.wait(m)
                        m = A.did(ac.activation(QF[:, hd, :], PS[b][:, :], ACT.Silu))
                        bank_free[b] = [m]
                        V.wait(m)
                        P.wait(m)
                return f

            def forget_feature(n):
                def f(s):
                    for c in range(2):
                        hd = 2 * n + c
                        b = bank()
                        m = by_feature(s, c, PS[b][:, :], 512)
                        A.wait(m, lf_free[c])
                        m = A.did(ac.activation(LF[:, c, :], PS[b][:, :], ACT.Sigmoid))
                        bank_free[b] = [m]
                        V.wait(m)
                        V.did(ve.tensor_scalar(LF[:, c, :], LF[:, c, :], LW[:, 1, hd:hd + 1], LW[:, 0, hd:hd + 1],
                                               ALU.mult, ALU.add))
                        V.own()
                        m = V.did(ve.tensor_scalar(KK[:, hd, :], LF[:, c, :], -1.0, 1.0, ALU.mult, ALU.add))
                        P.wait(m)
                        T.wait(m)
                        A.wait(m)
                        m = A.did(ac.activation(LF[:, c, :], LF[:, c, :], ACT.Ln))
                        V.wait(m)
                        for tt in range(4):
                            m = V.did(ve.tensor_tensor_scan(BC[:, hd, tt * 128:tt * 128 + 128], ONES,
                                                            LF[:, c, tt * 128:tt * 128 + 128], 0.0,
                                                            ALU.mult, ALU.add))
                        lf_free[c] = m
                        V.own()
                        A.wait(m)
                return f

            def token_pairs(evict):
                def f(s):
                    for t2 in range(2):
                        b = bank()
                        for j in range(2):
                            m = by_token(s, 2 * t2 + j, PS[b][:, j * 256:j * 256 + 256])
                        bank_free[b] = [evict(t2, PS[b][:, :].rearrange("p (j c) -> p j c", j=2), m)]
                return f

            def into(dst, col):
                def f(t2, src, m):
                    V.wait(m)
                    return V.did(ve.tensor_copy(dst[:, 2 * t2:2 * t2 + 2, col:col + 256], src))
                return f

            def gate_into(t2, src, m):
                A.wait(m)
                return A.did(ac.activation(HG[:, 2 * t2:2 * t2 + 2, :], src, ACT.Silu))

            def sb_feature(n):
                def f(s):
                    for c in range(2):
                        b = bank()
                        m = by_feature(s, c, PS[b][:, :], 512)
                        V.wait(m)
                        m = V.did(ve.tensor_copy(SQK[:, 2 * n + c, :], PS[b][:, :]))
                        bank_free[b] = [m]
                return f

            steps = [(hd, lv) for hd in range(4) for lv in range(9)]
            px_free, lb_free = [None, None], [None] * 3
            x_free = [None]
            ac_free = [None]
            at_free = [None, None]
            prepared = {}

            def hg_prepare(n):
                hd, lv = steps[n]
                s, x = n % 3, n % 2
                if lv == 7:
                    prepared[n] = ()
                    return
                if lv < 7:
                    h = LEVELS[lv]
                    nb = 512 // (2 * h)
                    bv = BC[:, hd, :].rearrange("p (n c) -> p n c", c=2 * h)
                    pv = PX[:, x, :].rearrange("p (n c) -> p n c", c=2 * h)
                    ref = bv[:, :, h - 1:h].to_broadcast([128, nb, h])
                    V.wait(*(px_free[x] or ()))
                    V.did(ve.tensor_tensor(pv[:, :, h:], bv[:, :, h:], ref, ALU.subtract))
                    m = V.did(ve.tensor_tensor(pv[:, :, 0:h], ref, bv[:, :, 0:h], ALU.subtract))
                    A.wait(m)
                    m = A.did(ac.activation(PX[:, x, :], PX[:, x, :], ACT.Exp))
                    V.wait(m, lb_free[s])
                    P.wait(m, lb_free[s])
                    q = V.did(ve.tensor_tensor(LB[:, s, 0, :], QF[:, hd, :], PX[:, x, :], ALU.mult))
                    k = P.did(po.tensor_tensor(LB[:, s, 1, :], KK[:, hd, :], PX[:, x, :], ALU.mult))
                    px_free[x] = (q, k)
                    prepared[n] = (q, k)
                    return
                V.wait(*(px_free[x] or ()))
                V.wait(x_free[0])
                A.wait(*(px_free[x] or ()))
                bt = BC[:, hd, :].rearrange("p (n c) -> p n c", c=128)
                m = V.did(ve.tensor_tensor(PX2[:, :].rearrange("p (n c) -> p n c", c=128),
                                           bt[:, :, 127:128].to_broadcast([128, 4, 128]), bt, ALU.subtract))
                m1 = A.did(ac.activation(PX[:, x, :], BC[:, hd, :], ACT.Exp))
                A.wait(m)
                m2 = A.did(ac.activation(PX2[:, :], PX2[:, :], ACT.Exp))
                V.wait(m2, lb_free[s])
                P.wait(m2, lb_free[s])
                q = V.did(ve.tensor_tensor(LB[:, s, 0, :], QF[:, hd, :], PX[:, x, :], ALU.mult))
                k = P.did(po.tensor_tensor(LB[:, s, 1, :], KK[:, hd, :], PX2[:, :], ALU.mult))
                V.wait(q, k)
                V.did(ve.tensor_scalar(EX[:, 0, :], LB[:, s, 0, 384:512], PX[:, x, 383:384], None, ALU.mult))
                q = V.did(ve.tensor_scalar(EX[:, 1, :], LB[:, s, 1, 0:128], PX[:, x, 255:256], None, ALU.mult))
                px_free[x] = (q, k)
                prepared[n] = (q, k)

            def hg_scores(n):
                hd, lv = steps[n]
                s, z = n % 3, hd % 2
                T.wait(*prepared[n])
                if lv < 8:
                    b = bank()
                    for tt in range(4):
                        c = slice(tt * 128, tt * 128 + 128)
                        k = LB[:, s, 1, c] if lv < 7 else KK[:, hd, c]
                        q = LB[:, s, 0, c] if lv < 7 else QF[:, hd, c]
                        ins = te.matmul(PS[b][:, c], k, q, start=True, stop=True)
                    m = T.did(ins)
                    lb_free[s] = m
                    V.wait(m, at_free[z])
                    V.own()
                    m = V.did(ve.copy_predicated(
                        AT[:, z, :].rearrange("p (n c) -> p n c", c=128),
                        MASK[:, lv:lv + 1, :].to_broadcast([128, 4, 128]),
                        PS[b][:, :].rearrange("p (n c) -> p n c", c=128)))
                    bank_free[b] = [m]
                    return
                done = V.last()
                pairs = [(0, 1), (1, 2), (2, 3), (0, 2), (1, 3), (0, 3)]
                for lot in (pairs[0:4], pairs[4:6]):
                    b = bank()
                    for w, (j, i) in enumerate(lot):
                        k = EX[:, 1, :] if (j == 0 and i > 1) else LB[:, s, 1, j * 128:j * 128 + 128]
                        q = EX[:, 0, :] if (i == 3 and j < 2) else LB[:, s, 0, i * 128:i * 128 + 128]
                        ins = te.matmul(PS[b][:, w * 128:w * 128 + 128], k, q, start=True, stop=True)
                    m = T.did(ins)
                    A.wait(m, ac_free[0])
                    at = pairs.index(lot[0])
                    m2 = A.did(ac.activation(AC[:, at:at + len(lot), :].rearrange("p a b -> p (a b)"),
                                             PS[b][:, 0:128 * len(lot)], ACT.Copy))
                    bank_free[b] = [m2]
                lb_free[s] = m
                x_free[0] = m
                b = bank()
                T.wait(m2, done)
                for i in range(4):
                    lhs = [(AT[:, z, i * 128:i * 128 + 128], i)]
                    lhs += [(AC[:, w, :], j) for w, (j, i2) in enumerate(pairs) if i2 == i]
                    for w, (l, j) in enumerate(lhs):
                        ins = te.matmul(PS[b][:, i * 64:i * 64 + 64], l, HI[:, j, hd * 64:hd * 64 + 64],
                                        start=w == 0, stop=w == len(lhs) - 1)
                m = T.did(ins)
                ac_free[0] = m
                at_free[z] = m
                A.wait(m, xn_read)
                m = A.did(ac.activation(MIX[:, :, 512 + hd * 64:576 + hd * 64],
                                        PS[b][:, 0:256].rearrange("p (i d) -> p i d", d=64), ACT.Copy))
                bank_free[b] = [m]

            at_step = [0]

            def with_steps(consume, count=3):
                def f(s):
                    lo, hi = at_step[0], min(at_step[0] + count, len(steps))
                    at_step[0] = hi
                    for n in range(lo, hi):
                        hg_prepare(n)
                    consume(s)
                    for n in range(lo, hi):
                        hg_scores(n)
                return f

            sq_free, me_free = [None], [None]

            def memory_in(n):
                if n == 1:
                    S.wait(me_free[0])
                    got_me[1] = d_m[1].did(sp.dma_start(ME[:, :, :], a["mem1"]))
                kept = [list(x) for x in hs_mark]
                norm_turned(ME, ME, 2, (G_MEM, G_MEM2)[n], [[got_me[n]]] * 2, HSM)
                me_free[0] = T.last()
                marks = [list(x) for x in hs_mark]
                hs_mark[:] = kept
                return marks

            mem_marks = {}

            def memory_block(n, consume, last):
                def f(s):
                    kept = list(hs_mark)
                    hs_mark[:] = mem_marks[n]
                    consume(s)
                    hs_mark[:] = kept
                    if last:
                        sq_free[0] = T.last()
                return f

            def mem_pair(dst):
                def f(s):
                    b = bank()
                    for mt in range(2):
                        m = by_token(s, mt, PS[b][:, mt * 256:mt * 256 + 256], HSM)
                    A.wait(m)
                    bank_free[b] = [A.did(ac.activation(dst[:, :, :].rearrange("p a b -> p (a b)"), PS[b][:, :],
                                                        ACT.Copy))]
                return f

            def key_features(s):
                b = bank()
                for c in range(2):
                    m = by_feature(s, c, PS[b][:, c * 256:c * 256 + 256], 256, HSM)
                A.wait(m)
                bank_free[b] = [A.did(ac.activation(MKT[1][:, :, :].rearrange("p a b -> p (a b)"), PS[b][:, :],
                                                    ACT.Copy))]

            def before(n, consume):
                def f(s):
                    mem_marks[n] = memory_in(n)
                    consume(s)
                return f

            def free_sq(consume):
                def f(s):
                    V.wait(sq_free[0])
                    A.wait(sq_free[0])
                    consume(s)
                return f

            wm, wm2 = a["w_mem"], a["w_mem2"]
            plan = [(w1[6], query_feature(0)), (w1[7], query_feature(1)),
                    (w1[8], forget_feature(0)), (w1[9], forget_feature(1)),
                    (w1[10], before(0, with_steps(token_pairs(into(HI, 0)), 2))),
                    (wm[0], with_steps(memory_block(0, mem_pair(MK), False))),
                    (wm[1], with_steps(memory_block(0, mem_pair(MV[0]), True))),
                    (w1[11], before(1, with_steps(token_pairs(gate_into)))),
                    (w1[12], with_steps(token_pairs(into(MQ, 0)))),
                    (wm2[0], with_steps(memory_block(1, key_features, False))),
                    (wm2[1], with_steps(memory_block(1, mem_pair(MV[1]), True)))]
            rest = [(0, sb_feature(0)), (1, sb_feature(1)), (2, sb_feature(2)), (3, sb_feature(3)),
                    (4, token_pairs(into(SV, 0))), (5, token_pairs(into(SV, 256)))]
            plan += [(w1[n], with_steps(free_sq(f))) for n, f in rest]
            stream(plan, [a["w_out"][0], a["w_out"][1]])
            while at_step[0] < len(steps):
                with_steps(lambda s: None)(0)
            fence()

        with ExitStack() as hs:
            MQT = sb("MQT", [128, 2, 512], scope=hs)
            ZS = sb("ZS", [128, 2, 1280], scope=hs)
            EE = sb("EE", [128, 1280], scope=hs)
            LL = sb("LL", [128, 2, 1280], scope=hs)
            AA = sb("AA", [128, 2, 1280], scope=hs)
            SQ = sb("SQ", [128, 2, 768], scope=hs)
            NQ = SQ[:, :, :].rearrange("p a b -> p (a b)")
            PM = sb("PM", [128, 2, 2, 256], scope=hs)
            PT = sb("PT", [128, 2, 512], scope=hs)
            nM = sb("nM", [128, 16], scope=hs)
            SU = sb("SU", [128, 16], scope=hs)
            AT4 = {0: (0, 512), 1: (512, 384), 3: (896, 128), 2: (1024, 256)}
            BANKS = [(0, 512, (0,)), (512, 512, (1, 3)), (1024, 256, (2,))]
            mark_l, mark_a, zs_free, ll_free, aa_free, ee_free = {}, {}, {}, {}, {}, [None]

            def sb_logits(h):
                z, c, p0 = h % 2, h // 2, 64 * (h % 2)
                marks = []
                V.wait(zs_free.get(h - 2))
                for off, width, tiles in BANKS:
                    b = bank()
                    for kt in tiles:
                        o, w = AT4[kt]
                        ins = te.matmul(PS[b][:, o - off:o - off + w], SQK[p0:p0 + 64, 4 + c, kt * 128:kt * 128 + 128],
                                        SQK[p0:p0 + 64, c, kt * 128:512], start=True, stop=True)
                    m = T.did(ins)
                    V.wait(m)
                    m = V.did(ve.tensor_scalar(ZS[:, z, off:off + width], PS[b][:, 0:width], 0.125, None, ALU.mult))
                    bank_free[b] = [m]
                A.wait(m, ee_free[0])
                A.did(ac.activation(EE[:, :], ZS[:, z, :], ACT.Abs))
                A.own()
                A.did(ac.activation(EE[:, :], EE[:, :], ACT.Exp, scale=-1.0))
                A.own()
                m = A.did(ac.activation(EE[:, :], EE[:, :], ACT.Ln, bias=1.0))
                V.wait(m, ll_free.get(h - 2))
                V.own()
                m = V.did(ve.scalar_tensor_tensor(LL[:, z, :], ZS[:, z, :], 0.0, EE[:, :], ALU.max, ALU.add))
                ee_free[0] = m
                P.wait(m)
                for kt in range(4):
                    o = AT4[kt][0]
                    m = P.did(po.affine_select(out=LL[:, z, o:o + 128], in_=LL[:, z, o:o + 128],
                                               compare_op=ALU.is_gt, fill=0.0, base=0, pattern=[[1, 128]],
                                               channel_multiplier=-1))
                mark_l[h] = m

            def sb_tail_scores(h):
                z = h % 2
                T.wait(mark_l[h])
                V.wait(aa_free.get(h - 2))
                for off, width, tiles in BANKS:
                    b = bank()
                    for kt in tiles:
                        o, w = AT4[kt]
                        ins = te.matmul(PS[b][:, o - off:o - off + w], TRI, LL[:, z, o:o + w],
                                        start=True, stop=kt == 3)
                        for k2 in range(kt + 1, 4):
                            o2, w2 = AT4[k2]
                            ins = te.matmul(PS[b][:, o - off + w - w2:o - off + w], ONES, LL[:, z, o2:o2 + w2],
                                            start=False, stop=k2 == 3)
                    m = T.did(ins)
                    V.wait(m)
                    m = V.did(ve.tensor_tensor(AA[:, z, off:off + width], ZS[:, z, off:off + width],
                                               PS[b][:, 0:width], ALU.subtract))
                    bank_free[b] = [m]
                ll_free[h] = T.last()
                zs_free[h] = m
                A.wait(m)
                m = A.did(ac.activation(AA[:, z, :], AA[:, z, :], ACT.Exp))
                P.wait(m)
                for kt in range(4):
                    o = AT4[kt][0]
                    m = P.did(po.affine_select(out=AA[:, z, o:o + 128], in_=AA[:, z, o:o + 128],
                                               compare_op=ALU.is_gt, fill=0.0, base=0, pattern=[[1, 128]],
                                               channel_multiplier=-1))
                mark_a[h] = m

            def sb_out(h):
                z = h % 2
                T.wait(mark_a[h])
                b = bank()
                for qt in range(4):
                    for kt in range(qt + 1):
                        o = AT4[kt][0] + (qt - kt) * 128
                        ins = te.matmul(PS[b][:, qt * 64:qt * 64 + 64], AA[:, z, o:o + 128],
                                        SV[:, kt, h * 64:h * 64 + 64], start=kt == 0, stop=kt == qt)
                m = T.did(ins)
                aa_free[h] = m
                V.wait(m)
                m = V.did(ve.tensor_copy(MIX[:, :, h * 64:h * 64 + 64],
                                         PS[b][:, 0:256].rearrange("p (i d) -> p i d", d=64)))
                bank_free[b] = [m]

            def normed_turned(src, n, dst, gain):
                w = 256 * n
                flat = src[:, :, :].rearrange("p a (h d) -> p (a h) d", d=64)
                V.wait(A.last())
                V.own()
                m = head_norm(flat, NQ[:, 0:w].rearrange("p (n d) -> p n d", d=64), 4 * n)
                for c in range(2):
                    b = bank()
                    T.wait(m)
                    for tt in range(n):
                        ins = te.transpose(PS[b][:, tt * 128:tt * 128 + 128], src[:, tt, c * 128:c * 128 + 128],
                                           IDENT)
                    t = T.did(ins)
                    V.wait(t)
                    e = V.did(ve.tensor_scalar(dst[:, c, :], PS[b][:, 0:128 * n], GN[:, gain:gain + 1], None, ALU.mult))
                    bank_free[b] = [e]
                T.wait(e)

            sb_logits(0)
            normed_turned(MQ, 4, MQT, G_MQ)
            normed_turned(MK, 2, MKT[0], G_MK)

            def later(f):
                return lambda u: f(u) if u > 0 else None

            skew((8, (later(sb_logits), sb_tail_scores, sb_out)),
                 (8, memory_attention(MQT, MKT[0], MV[0], 0.125, MIX, 768, PM, PT, nM, SU)))

            V.wait(A.last())
            V.own()
            for t2 in range(2):
                mix = MIX[:, 2 * t2:2 * t2 + 2, 0:768]
                V.did(ve.tensor_tensor(SQ[:, :, :], mix, mix, ALU.mult))
                V.own()
                m = V.did(ve.tensor_reduce(ST[:, 24 * t2:24 * t2 + 24],
                                           SQ[:, :, :].rearrange("p a (h d) -> p (a h) d", d=64), AX.X, ALU.add))
                V.own()
            inverse_root(48, 64, EPS, m)
            for tt in range(4):
                V.did(ve.tensor_tensor(
                    MIX[:, tt, 0:768].rearrange("p (h d) -> p h d", d=64),
                    MIX[:, tt, 0:768].rearrange("p (h d) -> p h d", d=64),
                    RS[:, tt * 12:tt * 12 + 12].unsqueeze(2).to_broadcast([128, 12, 64]), ALU.mult))
            V.own()
            m = V.did(ve.tensor_tensor(MIX[:, :, 512:768], MIX[:, :, 512:768], HG[:, :, :], ALU.mult))
            turn_parts(MIX, 4, G_OUT, [m])
            S.wait(T.last())
            got_x = d_x[0].did(sp.dma_start(X[:, :, :], a["x"]))
            V.wait(got_x)

            def add_out(col):
                def f(t2, src, m):
                    V.wait(m)
                    dst = X[:, 2 * t2:2 * t2 + 2, col:col + 256]
                    return V.did(ve.tensor_tensor(dst, dst, src, ALU.add))
                return f

            stream([(a["w_out"][n], token_pairs(add_out(256 * n))) for n in range(4)],
                   [a["w_query"][0], a["w_query"][1]])
            fence()

    NU, NV, NW, GRP = 3, 6, 8, 4
    NG = 128 // GRP
    AHEAD = list(range(0, 128, 2))
    TB = 512 // TBLK
    GD = nc.dram_tensor("gates", [TB, 128, 128, TBLK], F32, kind="Internal")
    AD = nc.dram_tensor("activations", [len(AHEAD), 128, 512], F32, kind="Internal")
    ahead_at = {i: n for n, i in enumerate(AHEAD)}
    with ExitStack() as pe_scope:
        GA = sb("GA", [128, 3, 512], scope=pe_scope)
        wr = WR[:, :, :, :].rearrange("p a b c -> p (a b c)")
        UR = wr[:, 0:2048].rearrange("p (s k e) -> p s k e", s=2, k=8)
        VR = wr[:, 2048:4096].rearrange("p (s e d) -> p s e d", s=2, e=2)
        ws = WS[:, :, :, :, :].rearrange("p a b c d -> p (a b c d)")
        UH = ws[:, 0:NU * 2048].rearrange("p (s w k e) -> p s w k e", s=NU, w=2, k=8)
        d_u = [Arrival(nc, f"d_u{n}") for n in range(2)]
        d_v = [Arrival(nc, f"d_v{n}") for n in range(2)]
        d_gb = [Arrival(nc, f"d_gb{n}") for n in range(2)]
        d_keep = [Arrival(nc, f"d_keep{n}") for n in range(3)]
        d_back = [Arrival(nc, f"d_back{n}") for n in range(3)]
        ur_free, vr_free = [()] * 2, [()] * 2
        uh_free, vh_free, wh_free = [None] * NU, [None] * NV, [None] * NW
        ga_free, gb_free = [()] * 3, [None] * 2
        u_mark, v_mark, w_mark, gb_mark, g_mark, ga_mark, keep_mark, vr_mark, ur_mark = [{} for _ in range(9)]
        n_u, n_fu, n_ga = [0], [0], [0]
        u_slot, ga_slot = {}, {}

        def fetch_u(i):
            r = n_fu[0] % 2
            n_fu[0] += 1
            S.wait(*ur_free[r])
            ur_mark[i] = (r, d_u[r].did(sp.dma_start(UR[:, r], a["u"][i])))

        def part_u(i, E=V):
            r, loaded = ur_mark[i]
            s = n_u[0] % NU
            u_slot[i] = s
            n_u[0] += 1
            A.wait(loaded, uh_free[s])
            hi = A.did(ac.activation(UH[:, s, 0], UR[:, r], ACT.Copy))
            E.wait(hi)
            lo = E.did(E.e.tensor_tensor(UH[:, s, 1], UR[:, r], UH[:, s, 0].bitcast(F32), ALU.subtract))
            ur_free[r] = (hi, lo)
            u_mark[i] = (hi, lo)

        def activate_by(i, steps):
            s, z = u_slot[i], n_ga[0] % 3
            ga_slot[i] = z
            n_ga[0] += 1
            b = bank()
            T.wait(*u_mark[i])
            n = 0
            for k in range(8):
                T.wait(*hs_mark[k])
                for w, h in PARTS:
                    ins = te.matmul(PS[b][:, :], UH[:, s, w, k, :], HS[:, h, k, :], start=n == 0, stop=n == 23)
                    n += 1
                if (k + 1) % (8 // steps) == 0 and k < 7:
                    yield
            m = T.did(ins)
            uh_free[s] = m
            A.wait(m, *ga_free[z])
            m = A.did(ac.activation(GA[:, z, :], PS[b][:, :], ACT.Gelu))
            bank_free[b] = [m]
            ga_mark[i] = m

        def activate(i):
            for _ in activate_by(i, 1):
                pass

        to_keep = []
        next_ahead = [0]

        def keep_one():
            i = to_keep.pop(0)
            z = ga_slot[i]
            A.wait(ga_mark[i])
            keep_mark[i] = d_keep[z].did(ac.dma_start(AD[ahead_at[i]], GA[:, z, :]))
            ga_free[z] = (keep_mark[i],)

        def ahead_by(steps):
            while next_ahead[0] < len(AHEAD):
                n = next_ahead[0]
                next_ahead[0] += 1
                if n + 1 < len(AHEAD):
                    part_u(AHEAD[n + 1], P)
                if n + 2 < len(AHEAD):
                    fetch_u(AHEAD[n + 2])
                yield from activate_by(AHEAD[n], steps)
                to_keep.append(AHEAD[n])
                if len(to_keep) > 1:
                    keep_one()
                yield

        def ahead(count):
            for _, _ in zip(range(count), ahead_by(1)):
                pass

        with ExitStack() as sc:
            XN = sb("XN", [128, 4, 1024], scope=sc)
            norm_turned(X, XN, 4, G_FFN, [[V.last()]] * 4)
            fence()
        HKT = sb("HKT", [128, 3, 512], scope=pe_scope)
        with ExitStack() as sc:
            SC = sb("SC", [128, 4, 16, 128], scope=sc)
            with ExitStack() as qs:
                KEYS = sb("KEYS", [128, 16, 128], scope=qs)
                QT = sb("QT", [128, 2, 512], scope=qs)
                S.wait(V.last(), T.last())
                got_keys = d_misc3.did(sp.dma_start(KEYS[:, :, :], a["keys"]))
                T.wait(got_keys)
                qt_free = [None, None]
                score_mark = [None]
                waiting = []

                def scores_of(hc, mark):
                    T.wait(mark)
                    b = bank()
                    for tt in range(4):
                        ins = te.matmul(PS[b][:, tt * 128:tt * 128 + 128], QT[:, hc % 2, tt * 128:tt * 128 + 128],
                                        KEYS[:, hc, :], start=True, stop=True)
                    m = T.did(ins)
                    qt_free[hc % 2] = m
                    A.wait(m)
                    m = A.did(ac.activation(SC[:, :, hc, :], PS[b][:, :].rearrange("p (t n) -> p t n", t=4), ACT.Copy))
                    bank_free[b] = [m]
                    score_mark[0] = m

                def query_block(n):
                    def f(s):
                        for c in range(2):
                            hc = 2 * n + c
                            b = bank()
                            m = by_feature(s, c, PS[b][:, :], 512)
                            V.wait(m, qt_free[hc % 2])
                            m = V.did(ve.tensor_copy(QT[:, hc % 2, :], PS[b][:, :]))
                            bank_free[b] = [m]
                            if waiting:
                                scores_of(*waiting.pop())
                            waiting.append((hc, m))
                    return f

                stream([(a["w_query"][n], query_block(n)) for n in range(8)])
                scores_of(*waiting.pop())
                ur_free[:] = [raw_free[0] + raw_free[1]] * 2
                vr_free[:] = ur_free
                uh_free[:] = [T.last()] * NU
                fetch_u(AHEAD[0])
                part_u(AHEAD[0], P)
                fetch_u(AHEAD[1])
                fence()
            CA = sb("CA", [128, 8, 256], scope=sc)
            S2 = CA[:, :, :].rearrange("p h (c n) -> p (h c) n", c=2)
            C2 = sb("C2", [128, 8, 256], scope=sc)
            EQ = sb("EQ", [128, 2, 128, 16], scope=sc)
            TV = sb("TV", [128, 16, 16], scope=sc)
            TI = sb("TI", [128, 16, 16], U32, scope=sc)
            TF = sb("TF", [128, 2, 16, 16], scope=sc)
            BV = sb("BV", [128, 8, 16], scope=sc)
            BI = sb("BI", [128, 8, 16], U32, scope=sc)
            BP = sb("BP", [128, 2, 8, 16], U32, scope=sc)
            BF = sb("BF", [128, 2, 2, 128], scope=sc)
            HK = sb("HK", [128, 2, 3, 128], scope=sc)
            SM = sb("SM", [128, 2, 8], scope=sc)
            hk_free, pick_mark, exp_mark = [None, None], {}, {}
            iota16 = IOTA[:, 0:16].unsqueeze(1).to_broadcast([128, 128, 16])

            def choose(tt):
                z = tt % 2
                V.own()
                for q in range(16):
                    V.did(ve.max(TV[:, q, 0:8], SC[:, tt, q, :]))
                V.own()
                for q in range(16):
                    V.did(ve.match_replace(S2[:, q, :], TV[:, q, 0:8], SC[:, tt, q, :], NEG))
                for q in range(16):
                    V.did(ve.max_index(TI[:, q, 0:8], TV[:, q, 0:8], SC[:, tt, q, :]))
                V.own()
                for q in range(16):
                    V.did(ve.max(TV[:, q, 8:16], S2[:, q, :]))
                V.own()
                for q in range(16):
                    V.did(ve.max_index(TI[:, q, 8:16], TV[:, q, 8:16], S2[:, q, :]))
                V.own()
                tv = TV[:, :, :].rearrange("p (h c) k -> p h c k", c=2)
                V.did(ve.tensor_tensor(CA[:, :, :].rearrange("p h (i j) -> p h i j", i=16),
                                       tv[:, :, 0, :].unsqueeze(3).to_broadcast([128, 8, 16, 16]),
                                       tv[:, :, 1, :].unsqueeze(2).to_broadcast([128, 8, 16, 16]), ALU.add))
                V.wait(pick_mark.get(tt - 2))
                V.did(ve.tensor_copy(TF[:, z], TI[:, :, :]))

            def choose_pairs(tt):
                z = tt % 2
                V.own()
                for h in range(8):
                    V.did(ve.max(BV[:, h, 0:8], CA[:, h, :]))
                V.own()
                for h in range(8):
                    V.did(ve.match_replace(C2[:, h, :], BV[:, h, 0:8], CA[:, h, :], NEG))
                for h in range(8):
                    V.did(ve.max_index(BI[:, h, 0:8], BV[:, h, 0:8], CA[:, h, :]))
                V.own()
                for h in range(8):
                    V.did(ve.max(BV[:, h, 8:16], C2[:, h, :]))
                V.own()
                for h in range(8):
                    V.did(ve.max_index(BI[:, h, 8:16], BV[:, h, 8:16], C2[:, h, :]))
                V.did(ve.tensor_copy(SM[:, 0, :], BV[:, :, 0]))
                V.own()
                V.did(ve.tensor_scalar(BP[:, 0], BI[:, :, :], 4, None, ALU.logical_shift_right))
                V.did(ve.tensor_scalar(BP[:, 1], BI[:, :, :], 15, None, ALU.bitwise_and))
                m = V.did(ve.tensor_tensor(BV[:, :, :], BV[:, :, :],
                                           SM[:, 0, :].unsqueeze(2).to_broadcast([128, 8, 16]), ALU.subtract))
                A.wait(m)
                exp_mark[tt] = A.did(ac.activation(BV[:, :, :], BV[:, :, :], ACT.Exp))
                V.wait(pick_mark.get(tt - 2))
                V.own()
                m = V.did(ve.tensor_copy(BF[:, z].rearrange("p c (h k) -> p c h k", h=8), BP[:, :, :, :]))
                tf = TF[:, z].rearrange("p (h c) k -> p h c k", c=2)
                V.own()
                for c in range(2):
                    o = V.did(ve.tensor_tensor(EQ[:, c], BF[:, z, c, :].unsqueeze(2).to_broadcast([128, 128, 16]),
                                               iota16, ALU.is_equal))
                    P.wait(o)
                    eq = EQ[:, c].rearrange("p (h k) e -> p h k e", h=8)
                    pick_mark[tt] = P.did(po.tensor_tensor(
                        eq, eq, tf[:, :, c, :].unsqueeze(2).to_broadcast([128, 8, 16, 16]), ALU.mult))

            def turn_chosen(tt):
                z = tt % 2
                V.wait(exp_mark[tt], hk_free[z])
                V.did(ve.tensor_reduce(SM[:, 1, :], BV[:, :, :], AX.X, ALU.add))
                V.own()
                V.did(ve.reciprocal(SM[:, 1, :], SM[:, 1, :]))
                V.own()
                V.did(ve.tensor_tensor(HK[:, z, 2, :].rearrange("p (h k) -> p h k", h=8), BV[:, :, :],
                                       SM[:, 1, :].unsqueeze(2).to_broadcast([128, 8, 16]), ALU.mult))
                V.wait(pick_mark[tt])
                for c in range(2):
                    m = V.did(ve.tensor_reduce(HK[:, z, c, :], EQ[:, c], AX.X, ALU.add))
                b = bank()
                T.wait(m)
                for c in range(3):
                    ins = te.transpose(PS[b][:, c * 128:c * 128 + 128], HK[:, z, c, :], IDENT)
                m = T.did(ins)
                hk_free[z] = m
                A.wait(m)
                m = A.did(ac.activation(HKT[:, :, tt * 128:tt * 128 + 128],
                                        PS[b][:, 0:384].rearrange("p (c t) -> p c t", c=3), ACT.Copy))
                bank_free[b] = [m]

            for tt in range(4):
                ahead(5)
                choose(tt)
                if tt:
                    turn_chosen(tt - 1)
                ahead(4)
                choose_pairs(tt)
            ahead(6)
            turn_chosen(3)
            fence()

        with ExitStack() as sc:
            STG = [sb(f"STG{n}", [128, 128, TBLK], scope=sc) for n in range(2)]
            OI = sb("OI", [128, 3, 8, 128], scope=sc)
            OJ = sb("OJ", [128, 3, 8, 128], scope=sc)
            OA = sb("OA", [128, 3, 8, 128], scope=sc)
            oi_free, oj_free, oa_free = [None] * 3, [None] * 3, [None] * 3
            stg_free = [None, None]
            d_g = [Arrival(nc, f"d_g{n}") for n in range(2)]
            iota8 = IOTA.unsqueeze(1).to_broadcast([128, 8, 128])
            PER = TBLK // 8
            one_mark, made = {}, []

            def one_hots(t8):
                z = t8 % 3
                cols = slice(t8 * 8, t8 * 8 + 8)

                def spread_out(c):
                    return HKT[:, c, cols].unsqueeze(2).to_broadcast([128, 8, 128])

                V.wait(oi_free[z])
                mi = V.did(ve.tensor_tensor(OI[:, z], iota8, spread_out(0), ALU.is_equal))
                V.wait(oj_free[z])
                mj = V.did(ve.tensor_tensor(OJ[:, z], iota8, spread_out(1), ALU.is_equal))
                if t8 % 2:
                    P.wait(mi, oa_free[z])
                    ma = P.did(po.tensor_tensor(OA[:, z], OI[:, z], spread_out(2), ALU.mult))
                else:
                    A.wait(mi, oa_free[z])
                    for t in range(8):
                        ma = A.did(ac.activation(OA[:, z, t, :], OI[:, z, t, :], ACT.Copy,
                                                 scale=HKT[:, 2, t8 * 8 + t:t8 * 8 + t + 1]))
                oi_free[z] = ma
                one_mark[t8] = (mj, ma)

            def gates(t8):
                z, tb = t8 % 3, t8 // PER
                T.wait(*one_mark[t8])
                for half in range(2):
                    b = bank()
                    for t in range(4):
                        ins = te.matmul(PS[b][:, t * 128:t * 128 + 128], OJ[:, z, half * 4 + t, :],
                                        OA[:, z, half * 4 + t, :], start=True, stop=True)
                    m = T.did(ins)
                    t0 = (t8 % PER) * 8 + half * 4
                    src = PS[b][:, :].rearrange("p (t i) -> p i t", t=4)
                    dst = STG[tb % 2][:, :, t0:t0 + 4]
                    if half > t8 % 2:
                        V.wait(m, stg_free[tb % 2])
                        e = V.did(ve.tensor_copy(dst, src))
                    else:
                        A.wait(m, stg_free[tb % 2])
                        e = A.did(ac.activation(dst, src, ACT.Copy))
                    bank_free[b] = [e]
                    made.append(e)
                oj_free[z] = m
                oa_free[z] = m
                if t8 % PER == PER - 1:
                    S.wait(*made[-2 * PER:])
                    stg_free[tb % 2] = d_g[tb % 2].did(sp.dma_start(GD[tb], STG[tb % 2][:, :, :]))

            one_hots(0)
            one_hots(1)
            pieces = ahead_by(4)
            for _ in range(8):
                next(pieces)
            for t8 in range(64):
                if t8 + 2 < 64:
                    one_hots(t8 + 2)
                gates(t8)
                next(pieces, None)
            for _ in pieces:
                pass
            while to_keep:
                keep_one()
            S.wait(*stg_free)
            S.wait(*keep_mark.values())
            marks = fence()
            S.wait(*marks)

    with ExitStack() as sc:
        VH = sb("VH", [128, NV, 2, 2, 512], F32R, scope=sc)
        WH6 = sb("WH", [128, 6, 2, 512], F32R, scope=sc)
        WH2 = ws[:, NU * 2048:8192].rearrange("p (s w t) -> p s w t", s=2, w=2)
        WH = [WH6[:, n] for n in range(6)] + [WH2[:, n] for n in range(2)]
        GB = sb("GB", [128, 2, TB, GRP, TBLK], scope=sc)
        GA = sb("GA2", [128, 3, 512], scope=sc)
        ga_free[:] = [()] * 3

        def fetch_v(u):
            g, dh, i = u // 4, u % 4 // 2, u // 4 * GRP + u % 2 * 2
            S.wait(*vr_free[u % 2])
            src = a["v"][i:i + 2, :, dh * 512:dh * 512 + 512].rearrange("e p d -> p e d")
            vr_mark[u] = d_v[u % 2].did(sp.dma_start(VR[:, u % 2], src))

        def part_v(u):
            s, r = u % NV, u % 2
            A.wait(vr_mark[u], vh_free[s])
            hi = A.did(ac.activation(VH[:, s, 0], VR[:, r], ACT.Copy))
            P.wait(hi)
            lo = P.did(po.tensor_tensor(VH[:, s, 1], VR[:, r], VH[:, s, 0].bitcast(F32), ALU.subtract))
            vr_free[r] = (hi, lo)
            v_mark[u] = (hi, lo)

        def load_g(g):
            S.wait(gb_free[g % 2])
            src = GD[:, :, g * GRP:g * GRP + GRP, :].rearrange("b p i t -> p b (i t)")
            gb_mark[g] = d_gb[g % 2].did(sp.dma_start(GB[:, g % 2].rearrange("p b i t -> p b (i t)"), src))

        def bring(i):
            z = n_ga[0] % 3
            ga_slot[i] = z
            n_ga[0] += 1
            S.wait(*ga_free[z])
            ga_mark[i] = d_back[z].did(sp.dma_start(GA[:, z, :], AD[ahead_at[i]]))

        def gated(i):
            z, g = ga_slot[i], i // GRP
            V.wait(ga_mark[i], gb_mark[g])
            m = V.did(ve.tensor_tensor(GA[:, z, :].rearrange("p (b t) -> p b t", b=TB),
                                       GA[:, z, :].rearrange("p (b t) -> p b t", b=TB),
                                       GB[:, g % 2, :, i % GRP, :], ALU.mult))
            gb_free[g % 2] = m
            g_mark[i] = m

        def part(i):
            z = ga_slot[i]
            A.wait(g_mark[i], wh_free[i % NW])
            hi = A.did(ac.activation(WH[i % NW][:, 0, :], GA[:, z, :], ACT.Copy))
            V.wait(hi)
            lo = V.did(ve.tensor_tensor(WH[i % NW][:, 1, :], GA[:, z, :], WH[i % NW][:, 0, :].bitcast(F32),
                                        ALU.subtract))
            ga_free[z] = (hi, lo)
            w_mark[i] = (hi, lo)

        def combine(g, p):
            dh, tt = p // 4, p % 4
            b = bank()
            n = 0
            for ii in range(GRP):
                i, u = g * GRP + ii, g * 4 + 2 * dh + ii // 2
                T.wait(*w_mark[i], *v_mark[u])
                for w, v in PARTS:
                    ins = te.matmul(PS[b][:, :], WH[i % NW][:, w, tt * 128:tt * 128 + 128],
                                    VH[:, u % NV, v, ii % 2, :], start=n == 0, stop=n == 3 * GRP - 1)
                    n += 1
            m = T.did(ins)
            if tt == 3:
                vh_free[(g * 4 + 2 * dh) % NV] = m
                vh_free[(g * 4 + 2 * dh + 1) % NV] = m
            if p == 7:
                for i in range(g * GRP, g * GRP + GRP):
                    wh_free[i % NW] = m
            V.wait(m)
            V.own()
            dst = X[:, tt, dh * 512:dh * 512 + 512]
            bank_free[b] = [V.did(ve.tensor_tensor(dst, dst, PS[b][:, :], ALU.add))]

        now = [i for i in range(128) if i not in ahead_at]
        load_g(0)
        fetch_u(now[0])
        part_u(now[0])
        fetch_u(now[1])
        fetch_v(0)
        fetch_v(1)
        bring(0)
        n_now = 0
        for g in range(NG + 1):
            if g + 1 < NG:
                load_g(g + 1)
            for ii in range(GRP):
                i = g * GRP + ii
                if g < NG:
                    if i not in ahead_at:
                        n_now += 1
                        if n_now < len(now):
                            part_u(now[n_now])
                    part_v(i)
                    if i not in ahead_at:
                        if n_now + 1 < len(now):
                            fetch_u(now[n_now + 1])
                        activate(i)
                    if i + 1 in ahead_at:
                        bring(i + 1)
                    if i + 2 < 128:
                        fetch_v(i + 2)
                    gated(i)
                    part(i)
                if g >= 1:
                    combine(g - 1, 2 * ii)
                    combine(g - 1, 2 * ii + 1)
        raw_free[:] = [[m for f in (*ur_free, *vr_free) for m in f]] * 2
        ws_free[:] = [[T.last()]] * 2
        fetch(a["w_in2"][0])
        fetch(a["w_in2"][1])
        fence()

    with ExitStack() as sc:
        DT = sb("DT", [128, 3, 512], scope=sc)
        Y = sb("Y", [128, 4, 1024], scope=sc)
        QT2 = sb("QT2", [128, 6, 512], scope=sc)
        KT2 = sb("KT2", [128, 6, 512], scope=sc)
        V2 = sb("V2", [128, 4, 768], scope=sc)
        QM = sb("QM", [128, 2, 512], scope=sc)
        SP2 = sb("SP2", [128, 3, 1280], scope=sc)
        PT2 = sb("PT2", [128, 2, 1280], scope=sc)
        PM = sb("PM2", [128, 2, 2, 256], scope=sc)
        PT = sb("PTm", [128, 2, 512], scope=sc)
        TMP = sb("TMP", [128, 2, 64], scope=sc)
        nM = sb("nM2", [128, 32], scope=sc)
        SU = sb("SU2", [128, 32], scope=sc)
        d_d = Arrival(nc, "d_d")
        S.wait(V.last(), T.last())
        got_d = d_d.did(sp.dma_start(DT[:, :, :], a["dist"]))
        V.wait(got_d)
        norm_turned(X, Y, 4, G_N2, [[V.last()]] * 4)
        y_free = T.last()

        def features(dst, n, scale):
            def f(s):
                for c in range(2):
                    b = bank()
                    m = by_feature(s, c, PS[b][:, :], 512)
                    A.wait(m)
                    m = A.did(ac.activation(dst[:, 2 * n + c, :], PS[b][:, :], ACT.Copy, scale=scale))
                    bank_free[b] = [m]
            return f

        def pairs_of(evict):
            def f(s):
                for t2 in range(2):
                    b = bank()
                    for j in range(2):
                        m = by_token(s, 2 * t2 + j, PS[b][:, j * 256:j * 256 + 256])
                    bank_free[b] = [evict(t2, PS[b][:, :].rearrange("p (j c) -> p j c", j=2), m)]
            return f

        def v_into(col):
            def f(t2, src, m):
                V.wait(m)
                return V.did(ve.tensor_copy(V2[:, 2 * t2:2 * t2 + 2, col:col + 256], src))
            return f

        def gate_into(n):
            def f(t2, src, m):
                A.wait(m, y_free)
                return A.did(ac.activation(Y[:, 2 * t2:2 * t2 + 2, n * 256:n * 256 + 256], src, ACT.Silu))
            return f

        w2 = a["w_in2"]
        stream([(w2[n], features(QT2, n, 0.125)) for n in range(3)]
               + [(w2[3 + n], features(KT2, n, 1.0)) for n in range(3)]
               + [(w2[6 + n], pairs_of(v_into(256 * n))) for n in range(3)]
               + [(w2[9], features(QM, 0, 0.125))]
               + [(w2[10 + n], pairs_of(gate_into(n))) for n in range(4)],
               [a["w_out2"][0], a["w_out2"][1]])

        T.wait(A.last(), V.last())
        V.wait(A.last())
        units = [(hh, qt) for hh in range(4) for qt in range(4)]
        sp_free, pt_free = [None] * 3, [None] * 2
        exp_mark, pt_mark = {}, {}

        def lay(qt):
            tiles, o = [], 0
            for g in range(3):
                c0 = max(0, qt - 1) if g == 0 else 0
                tiles.append((o, c0, qt + 1 - c0))
                o += (qt + 1 - c0) * 128
            return tiles, o

        def window_scores(u):
            hh, qt = units[u]
            z = u % 3
            tiles, total = lay(qt)
            for g, (o, c0, n) in enumerate(tiles):
                hd = g * 4 + hh
                c, p0 = hd // 2, 64 * (hd % 2)
                b = bank()
                m = T.did(te.matmul(PS[b][:, 0:n * 128], QT2[p0:p0 + 64, c, qt * 128:qt * 128 + 128],
                                    KT2[p0:p0 + 64, c, c0 * 128:(qt + 1) * 128], start=True, stop=True))
                V.wait(m, sp_free[z])
                m = V.did(ve.scalar_tensor_tensor(SP2[:, z, o:o + n * 128], DT[:, g, 512 - n * 128:512], SLOPES[hd],
                                                  PS[b][:, 0:n * 128], ALU.mult, ALU.add))
                bank_free[b] = [m]
            V.own()
            m = V.did(ve.tensor_reduce(nM[:, u:u + 1], SP2[:, z, 0:total], AX.X, ALU.max, negate=True))
            A.wait(m)
            m = A.did(ac.activation(SP2[:, z, 0:total], SP2[:, z, 0:total], ACT.Exp, bias=nM[:, u:u + 1],
                                    accum_out=SU[:, u:u + 1]))
            exp_mark[u] = m

        def window_turned(u):
            z, w2 = u % 3, u % 2
            tiles, total = lay(units[u][1])
            nblk = total // 128
            for lot in range(0, nblk, 4):
                k = min(4, nblk - lot)
                b = bank()
                T.wait(exp_mark[u])
                for w in range(k):
                    ins = te.transpose(PS[b][:, w * 128:w * 128 + 128],
                                       SP2[:, z, (lot + w) * 128:(lot + w) * 128 + 128], IDENT)
                m = T.did(ins)
                A.wait(m, pt_free[w2])
                e = A.did(ac.activation(PT2[:, w2, lot * 128:(lot + k) * 128], PS[b][:, 0:k * 128], ACT.Copy))
                bank_free[b] = [e]
            sp_free[z] = m
            pt_mark[u] = e

        def window_out(u):
            hh, qt = units[u]
            w2 = u % 2
            tiles, total = lay(qt)
            V.wait(exp_mark[u])
            V.did(ve.reciprocal(SU[:, u:u + 1], SU[:, u:u + 1]))
            b = bank()
            T.wait(pt_mark[u])
            for g, (o, c0, n) in enumerate(tiles):
                hd = g * 4 + hh
                for w in range(n):
                    ins = te.matmul(PS[b][:, g * 64:g * 64 + 64], PT2[:, w2, o + w * 128:o + w * 128 + 128],
                                    V2[:, c0 + w, hd * 64:hd * 64 + 64], start=w == 0, stop=w == n - 1)
            m = T.did(ins)
            pt_free[w2] = m
            V.wait(m)
            V.own()
            dst = Y[:, qt, 0:768].rearrange("p (g c) -> p g c", g=3)[:, :, hh * 64:hh * 64 + 64]
            m = V.did(ve.scalar_tensor_tensor(dst, PS[b][:, 0:192].rearrange("p (g d) -> p g d", g=3), SU[:, u:u + 1],
                                              dst, ALU.mult, ALU.mult))
            bank_free[b] = [m]

        mem_stages = memory_attention(QM, MKT[1], MV[1], 1.0, Y, 768, PM, PT, nM[:, 16:32], SU[:, 16:32],
                                      TMP[:, :, :])
        every_other = [lambda v, f=f: f(v // 2) if v % 2 == 0 else None for f in mem_stages]
        skew((16, (window_scores, window_turned, window_out)),
             (16, (every_other[0], lambda v: None, every_other[1], lambda v: None, every_other[2])))

        hs_free = T.last()
        ready = V.last()
        for k in range(8):
            b = bank()
            T.wait(ready)
            for tt in range(4):
                ins = te.transpose(PS[b][:, tt * 128:tt * 128 + 128], Y[:, tt, k * 128:k * 128 + 128], IDENT)
            m = T.did(ins)
            A.wait(m, hs_free)
            hi = A.did(ac.activation(HS[:, 0, k, :], PS[b][:, :], ACT.Copy))
            V.wait(hi)
            lo = V.did(ve.tensor_tensor(HS[:, 1, k, :], PS[b][:, :], HS[:, 0, k, :].bitcast(F32), ALU.subtract))
            bank_free[b] = [hi, lo]
            hs_mark[k] = [hi, lo]
        y_done = T.last()

        def add_out2(col):
            def f(t2, src, m):
                V.wait(m)
                V.own()
                dst = X[:, 2 * t2:2 * t2 + 2, col:col + 256]
                return V.did(ve.tensor_tensor(dst, dst, src, ALU.add))
            return f

        stream([(a["w_out2"][n], pairs_of(add_out2(256 * n))) for n in range(4)])
        FG = Y[:, 0, :]
        S.wait(y_done)
        got_f = d_misc3.did(sp.dma_start(FG, a["final"]))
        scales(X, 4, [[V.last()]] * 4)
        V.wait(got_f)
        d_o = [Arrival(nc, f"d_o{n}") for n in range(4)]
        for tt in range(4):
            m = V.did(ve.scalar_tensor_tensor(X[:, tt, :], X[:, tt, :], RS[:, tt:tt + 1], FG, ALU.mult, ALU.mult))
            S.wait(m)
            d_o[tt].did(sp.dma_start(out[tt], X[:, tt, :]))
        S.wait(*[d.last() for d in d_o])
        fence()
    ctx.__exit__(None, None, None)


def constants():
    p = np.arange(128)
    cst = np.zeros((128, 4, 128), np.float32)
    cst[:, 0] = np.eye(128)
    cst[:, 1] = p[:, None] >= p[None, :]
    cst[:, 2] = 1.0
    cst[:, 3] = p[None, :]
    mask = np.zeros((128, 8, 128), np.uint32)
    s, t = p[:, None], p[None, :]
    for n, h in enumerate(LEVELS):
        mask[:, n] = (s // (2 * h) == t // (2 * h)) & (s % (2 * h) < h) & (t % (2 * h) >= h)
    mask[:, 7] = s == t
    d = p[:, None] - np.arange(512)[None, :] + 384
    dist = np.zeros((128, 3, 512), np.float32)
    for g, (window, dil) in enumerate(((128, 1), (512, 4), (2048, 16))):
        dist[:, g] = np.where((d >= 0) & (d <= window) & (d % dil == 0), -d, -1e30)
    return cst, mask, dist


def kernel(**inputs):
    import concourse.bacc as _bacc
    from concourse import mybir as _mybir
    from concourse.bass_utils import run_bass_kernel_spmd as _run

    i = {k: np.asarray(v) for k, v in inputs.items()}

    def tiles(x):
        return np.ascontiguousarray(x.reshape(-1, 128, 1024).transpose(1, 0, 2))

    def weight(w):
        return np.ascontiguousarray(w.reshape(8, 128, -1, 256).transpose(2, 1, 0, 3))

    def column(g):
        return g.reshape(-1, 128).T

    cst, mask, dist = constants()
    small = np.concatenate(
        [column(i["norm_mix_gain"]), column(i["norm_ffn_gain"]), column(i["norm_g_2"]), column(i["mem_norm_gain"]),
         column(i["mem_norm_g_2"]), column(i["sb_out_gain"]), column(i["hg_out_gain"]), np.ones((128, 2), np.float32),
         column(i["gamma_lb"]), column(np.tile(i["mem_q_gain"][0], 2)), column(np.tile(i["mem_k_gain"][0], 2))], axis=1)
    arrays = {
        "x": tiles(i["x"][0]), "mem0": tiles(i["mem"][0]), "mem1": tiles(i["mem_2"][0]),
        "w_in": weight(i["w_in"][0]), "w_mem": weight(i["w_mem_kv"][0]), "w_out": weight(i["w_out"][0]),
        "w_query": weight(i["peer_w_query"][0]), "w_in2": weight(i["w_in_2"][0]),
        "w_mem2": weight(i["w_mem_kv_2"][0]), "w_out2": weight(i["w_out_2"][0]),
        "keys": np.ascontiguousarray(i["peer_sub_keys"][0].reshape(16, 128, 128).transpose(2, 0, 1)),
        "u": np.ascontiguousarray(i["peer_u"][0].reshape(128, 128, 8, 128).transpose(0, 3, 2, 1)),
        "v": np.ascontiguousarray(i["peer_v"][0].reshape(128, 128, 1024)),
        "small": np.ascontiguousarray(small), "final": np.tile(i["final_norm_g_2"][None, :], (128, 1)),
        "cst": cst, "mask": mask, "dist": dist,
    }
    nc = _bacc.Bacc("TRN2", target_bir_lowering=False, num_devices=1)
    named, sent = {}, {}
    for name, x in arrays.items():
        sent[f"in_{name}"] = x
        named[name] = nc.dram_tensor(f"in_{name}", x.shape, _mybir.dt.from_np(x.dtype), kind="ExternalInput").ap()
    out = nc.dram_tensor("out_0", (4, 128, 1024), _mybir.dt.float32, kind="ExternalOutput").ap()
    program(nc, named, out)
    r = _run(nc, [sent], core_ids=[0])
    return np.asarray(r.results[0]["out_0"]).reshape(1, 512, 1024)
```

```python
from contextlib import ExitStack

import numpy as np

import concourse.bass as bass
from concourse import mybir

F32 = mybir.dt.float32
F32R = mybir.dt.float32r
U32 = mybir.dt.uint32
ALU = mybir.AluOpType
ACT = mybir.ActivationFunctionType
AX = mybir.AxisListType

EPS = 1e-6
NEG = -3.0e38
SLOPES = [float(np.float32(2.0 ** (-8.0 * n / 12))) for n in range(1, 13)]
TBLK = 32
LEVELS = [64, 32, 16, 8, 4, 2, 1]
G_MIX, G_FFN, G_N2, G_MEM, G_MEM2, G_OUT, G_LB, G_MQ, G_MK = 0, 8, 16, 24, 32, 40, 48, 56, 57
SMALL = 58
PARTS = ((0, 0), (0, 1), (1, 0))


class Engine:

    def __init__(self, nc, eng, name):
        self.e = eng
        self.sem = nc.alloc_semaphore(name)
        self.n = 0
        self.seen = {}

    def wait(self, *marks):
        for m in marks:
            if m is None:
                continue
            sem, v, key = m
            if self.seen.get(key, 0) < v:
                self.e.wait_ge(sem, v)
                self.seen[key] = v

    def did(self, ins):
        self.n += 1
        ins.then_inc(self.sem, 1)
        return self.last()

    def last(self):
        return (self.sem, self.n, id(self))

    def own(self):
        self.wait(self.last())


class Arrival:

    def __init__(self, nc, name):
        self.sem = nc.alloc_semaphore(name)
        self.n = 0

    def did(self, ins):
        self.n += 16
        ins.then_inc(self.sem, 16)
        return self.last()

    def last(self):
        return (self.sem, self.n, id(self))


def program(nc, a, out):
    V = Engine(nc, nc.vector, "s_dve")
    A = Engine(nc, nc.scalar, "s_act")
    T = Engine(nc, nc.tensor, "s_pe")
    P = Engine(nc, nc.gpsimd, "s_pool")
    S = Engine(nc, nc.sync, "s_sp")
    ve, ac, te, po, sp = nc.vector, nc.scalar, nc.tensor, nc.gpsimd, nc.sync

    def fence():
        marks = [x.last() for x in (V, A, T, P)]
        for x in (V, A, P):
            x.wait(*marks)
        return marks

    ctx = ExitStack()

    def sb(name, shape, dt=F32, scope=None):
        return (scope or ctx).enter_context(nc.sbuf_tensor(name, shape, dt))

    ctx.__enter__()
    HS = sb("HS", [128, 2, 8, 512], F32R)
    WS = sb("WS", [128, 2, 2, 8, 256], F32R)
    WR = sb("WR", [128, 2, 8, 256])
    X = sb("X", [128, 4, 1024])
    CST = sb("CST", [128, 4, 128])
    GN = sb("GN", [128, SMALL])
    MKT = [sb(f"MKT{n}", [128, 2, 256]) for n in range(2)]
    MV = [sb(f"MV{n}", [128, 2, 256]) for n in range(2)]
    JK = sb("JK", [128, 1024])
    ST = sb("ST", [128, 64])
    SD = sb("SD", [128, 64])
    RS = sb("RS", [128, 64])
    SQS = sb("SQS", [128, 4, 4])
    PS = [ctx.enter_context(nc.psum_tensor(f"PS{n}", [128, 512], F32)) for n in range(8)]
    IDENT, TRI, ONES, IOTA = (CST[:, n, :] for n in range(4))

    bank_free = [[] for _ in range(8)]
    turn, held = [0], set()

    def bank():
        while turn[0] % 8 in held:
            turn[0] += 1
        b = turn[0] % 8
        turn[0] += 1
        T.wait(*bank_free[b])
        return b

    d_w = [Arrival(nc, f"d_w{n}") for n in range(2)]
    raw_free = [[], []]
    ws_free = [[], []]
    ws_mark = [[], []]
    hs_mark = [[] for _ in range(8)]
    fetched, parted, blocks = [], [], [0]

    def fetch(src):
        s = blocks[0] % 2
        blocks[0] += 1
        S.wait(*raw_free[s])
        fetched.append((s, d_w[s].did(sp.dma_start(WR[:, s], src))))

    def part_next():
        s, loaded = fetched.pop(0)
        A.wait(loaded, *ws_free[s])
        P.wait(loaded)
        ws_mark[s] = []
        for k in (slice(0, 4), slice(4, 8)):
            hi = A.did(ac.activation(WS[:, s, 0, k], WR[:, s, k], ACT.Copy))
            P.wait(hi)
            lo = P.did(po.tensor_tensor(WS[:, s, 1, k], WR[:, s, k], WS[:, s, 0, k].bitcast(F32), ALU.subtract))
            ws_mark[s].append((hi, lo))
        raw_free[s] = [hi, lo]
        parted.append(s)

    def stream(work, then=()):
        sources = [w[0] for w in work] + list(then)[0:2]
        n_fetched = len(fetched) + len(parted)
        while n_fetched < min(2, len(sources)):
            fetch(sources[n_fetched])
            n_fetched += 1
        if not parted:
            part_next()
        for n, (_, consume) in enumerate(work):
            first = bool(leading)
            if len(parted) < 2 and fetched and not first:
                part_next()
            s = parted.pop(0)
            if first:
                next(leading[0])
                next(leading[0])
            if n_fetched < len(sources):
                fetch(sources[n_fetched])
                n_fetched += 1
            consume(s)
            ws_free[s] = [T.last()]

    def by_feature(s, half, o, cols, src=None):
        n = 0
        src = HS if src is None else src
        for k in range(8):
            T.wait(*hs_mark[k], *ws_mark[s][k // 4])
            for w, h in PARTS:
                ins = te.matmul(o, WS[:, s, w, k, half * 128:half * 128 + 128], src[:, h, k, 0:cols],
                                start=n == 0, stop=n == 23)
                n += 1
        return T.did(ins)

    def by_token(s, tt, o, src=None):
        n = 0
        src = HS if src is None else src
        for k in range(8):
            T.wait(*hs_mark[k], *ws_mark[s][k // 4])
            for w, h in PARTS:
                ins = te.matmul(o, src[:, h, k, tt * 128:tt * 128 + 128], WS[:, s, w, k, :],
                                start=n == 0, stop=n == 23)
                n += 1
        return T.did(ins)

    leading, lead_order = [], []

    def lead(s, groups):
        turned = leading.pop()
        marks = []
        for step, k in enumerate(lead_order or range(8)):
            next(turned, None)
            if step == 2 and fetched and not parted:
                part_next()
            T.wait(*hs_mark[k], *ws_mark[s][k // 4])
            for b, cols, operands in groups:
                for n, (w, h) in enumerate(PARTS):
                    ins = te.matmul(PS[b][:, 0:cols], *operands(w, h, k), start=step == 0 and n == 0,
                                    stop=step == 7 and n == 2)
                if step == 7:
                    marks.append(T.did(ins))
        lead_order.clear()
        return marks

    def take(n):
        banks = [bank() for _ in range(n)]
        held.update(banks)
        return banks

    def features_of(s):
        if leading:
            banks = take(2)
            marks = lead(s, [(b, 512, lambda w, h, k, c=c: (WS[:, s, w, k, c * 128:c * 128 + 128], HS[:, h, k, :]))
                          for c, b in enumerate(banks)])
            for c in range(2):
                held.discard(banks[c])
                yield c, banks[c], marks[c]
            return
        for c in range(2):
            b = bank()
            yield c, b, by_feature(s, c, PS[b][:, :], 512)

    def tokens_of(s):
        if leading:
            banks = take(4)
            marks = lead(s, [(b, 256, lambda w, h, k, t=t: (HS[:, h, k, t * 128:t * 128 + 128], WS[:, s, w, k, :]))
                          for t, b in enumerate(banks)])
            for t, b in enumerate(banks):
                held.discard(b)
                yield slice(t, t + 1), PS[b][:, 0:256].unsqueeze(1), b, marks[t]
            return
        for t in (0, 2):
            b = bank()
            for j in range(2):
                m = by_token(s, t + j, PS[b][:, j * 256:j * 256 + 256])
            yield slice(t, t + 2), PS[b][:, :].rearrange("p (j c) -> p j c", j=2), b, m

    def inverse_root(n, width, eps, mark):
        V.wait(mark)
        m = V.did(ve.tensor_scalar(ST[:, 0:n], ST[:, 0:n], 1.0 / width, eps, ALU.mult, ALU.add))
        A.wait(m)
        m = A.did(ac.activation(SD[:, 0:n], ST[:, 0:n], ACT.Sqrt))
        V.wait(m)
        V.did(ve.reciprocal(RS[:, 0:n], SD[:, 0:n]))
        V.own()

    one = P.did(po.memset(ST[:, 63:64], 1.0))

    def ready_root():
        A.wait(one)
        A.own()
        A.did(ac.activation(SD[:, 63:64], ST[:, 63:64], ACT.Sqrt))

    def scales(src, ntt, ready):
        for tt in range(ntt):
            A.wait(*ready[tt])
            A.own()
            m = A.did(ac.activation(JK[:, :], src[:, tt, :], ACT.Square, accum_out=ST[:, tt:tt + 1]))
        inverse_root(ntt, 1024, EPS, m)

    def head_norm(view, sq, n):
        V.did(ve.tensor_tensor(sq, view, view, ALU.mult))
        V.own()
        m = V.did(ve.tensor_reduce(ST[:, 0:n], sq, AX.X, ALU.add))
        inverse_root(n, 64, EPS, m)
        return V.did(ve.tensor_tensor(view, view, RS[:, 0:n].unsqueeze(2).to_broadcast([128, n, 64]), ALU.mult))

    def turn_by_k(src, ntt, gain, ready, dst=None, then=None, order=range(8)):
        hs_free = T.last()
        dst = HS if dst is None else dst
        for k in order:
            b = bank()
            T.wait(*(ready(k) if callable(ready) else ready))
            for tt in range(ntt):
                ins = te.transpose(PS[b][:, tt * 128:tt * 128 + 128], src[:, tt, k * 128:k * 128 + 128], IDENT)
            m = T.did(ins)
            w = ntt * 128
            A.wait(m, hs_free)
            if gain is None:
                hi = A.did(ac.activation(dst[:, 0, k, 0:w], PS[b][:, 0:w], ACT.Copy))
                V.wait(hi)
                lo = V.did(ve.tensor_tensor(dst[:, 1, k, 0:w], PS[b][:, 0:w], dst[:, 0, k, 0:w].bitcast(F32),
                                            ALU.subtract))
            else:
                g = GN[:, gain + k:gain + k + 1]
                hi = A.did(ac.activation(dst[:, 0, k, 0:w], PS[b][:, 0:w], ACT.Copy, scale=g))
                V.wait(hi)
                lo = V.did(ve.scalar_tensor_tensor(dst[:, 1, k, 0:w], PS[b][:, 0:w], g,
                                                   dst[:, 0, k, 0:w].bitcast(F32), ALU.mult, ALU.subtract))
            bank_free[b] = [hi, lo]
            hs_mark[k] = [hi, lo]
            if then:
                then(k)
            yield

    def turn_parts(*args, **kw):
        for _ in turn_by_k(*args, **kw):
            pass

    def scaled(src, dst, ntt):
        A.wait(V.last())
        marks = []
        for tt in range(ntt):
            if tt % 2:
                marks.append(A.did(ac.activation(dst[:, tt, :], src[:, tt, :], ACT.Copy, scale=RS[:, tt:tt + 1])))
            else:
                marks.append(V.did(ve.tensor_scalar(dst[:, tt, :], src[:, tt, :], RS[:, tt:tt + 1], None, ALU.mult)))
        return marks

    def normed(src, dst, ntt, ready):
        scales(src, ntt, ready)
        return scaled(src, dst, ntt)

    def square(tt, n, width):
        c = slice(n * width, n * width + width)
        A.own()
        return A.did(ac.activation(JK[:, c], X[:, tt, c], ACT.Square, accum_out=SQS[:, tt, n:n + 1]))

    def norm_of_squares(dst, n, mark):
        V.wait(mark)
        V.own()
        m = V.did(ve.tensor_reduce(ST[:, 0:4], SQS[:, :, 0:n], AX.X, ALU.add))
        inverse_root(4, 1024, EPS, m)
        return scaled(X, dst, 4) if dst is not None else None

    def skew(*lines, oldest_first=False):
        for step in range(max(n + len(st) - 1 for n, st in lines)):
            for n, st in lines:
                for k, f in list(enumerate(st))[::-1 if oldest_first else 1]:
                    if 0 <= step - k < n:
                        f(step - k)

    def memory_attention(QT, KT, VAL, scale, Y, col, PM, PT, nM, SU, TMP=None):
        pm_free, pt_free, exp_mark, pt_mark = [None, None], [None, None], {}, {}

        def logits(u):
            h, half = u // 2, u % 2
            c, p0, s = h // 2, 64 * (h % 2), u % 2
            b = bank()
            for j in range(2):
                tt = 2 * half + j
                ins = te.matmul(PS[b][:, j * 256:j * 256 + 256], QT[p0:p0 + 64, c, tt * 128:tt * 128 + 128],
                                KT[p0:p0 + 64, c, :], start=True, stop=True)
            m = T.did(ins)
            V.wait(m)
            m = V.did(ve.tensor_reduce(nM[:, 2 * u:2 * u + 2], PS[b][:, :].rearrange("p (j m) -> p j m", j=2),
                                       AX.X, ALU.max, negate=True))
            V.wait(m)
            m = V.did(ve.tensor_scalar(nM[:, 2 * u:2 * u + 2], nM[:, 2 * u:2 * u + 2], scale, None, ALU.mult))
            A.wait(m, pm_free[s])
            for j in range(2):
                m = A.did(ac.activation(PM[:, s, j, :], PS[b][:, j * 256:j * 256 + 256], ACT.Exp, scale=scale,
                                        bias=nM[:, 2 * u + j:2 * u + j + 1],
                                        accum_out=SU[:, 2 * u + j:2 * u + j + 1]))
            bank_free[b] = [m]
            exp_mark[u] = m

        def turned(u):
            s = u % 2
            b = bank()
            T.wait(exp_mark[u])
            for j in range(2):
                for mt in range(2):
                    ins = te.transpose(PS[b][:, (2 * j + mt) * 128:(2 * j + mt) * 128 + 128],
                                       PM[:, s, j, mt * 128:mt * 128 + 128], IDENT)
            m = T.did(ins)
            pm_free[s] = m
            A.wait(m, pt_free[s])
            m = A.did(ac.activation(PT[:, s, :], PS[b][:, :], ACT.Copy))
            bank_free[b] = [m]
            pt_mark[u] = m

        def outs(u):
            h, half = u // 2, u % 2
            s = u % 2
            V.wait(exp_mark[u])
            V.did(ve.reciprocal(SU[:, 2 * u:2 * u + 2], SU[:, 2 * u:2 * u + 2]))
            b = bank()
            T.wait(pt_mark[u])
            for j in range(2):
                for mt in range(2):
                    ins = te.matmul(PS[b][:, j * 64:j * 64 + 64],
                                    PT[:, s, (2 * j + mt) * 128:(2 * j + mt) * 128 + 128],
                                    VAL[:, mt, h * 64:h * 64 + 64], start=mt == 0, stop=mt == 1)
            m = T.did(ins)
            pt_free[s] = m
            V.wait(m)
            V.own()
            dst = Y[:, 2 * half:2 * half + 2, col + h * 64:col + h * 64 + 64]
            m = V.did(ve.tensor_tensor(
                dst if TMP is None else TMP, PS[b][:, 0:128].rearrange("p (j d) -> p j d", j=2),
                SU[:, 2 * u:2 * u + 2].unsqueeze(2).to_broadcast([128, 2, 64]), ALU.mult))
            bank_free[b] = [m]
            if TMP is not None:
                V.own()
                V.did(ve.tensor_tensor(dst, dst, TMP, ALU.mult))

        return logits, turned, outs

    d_c = Arrival(nc, "d_c")
    d_m = [Arrival(nc, f"d_m{n}") for n in range(2)]
    d_x = [Arrival(nc, f"d_x{n}") for n in range(4)]
    d_misc = Arrival(nc, "d_misc")
    d_misc2 = Arrival(nc, "d_misc2")
    d_misc3 = Arrival(nc, "d_misc3")
    got_x = [d.did(sp.dma_start(X[:, tt, :], a["x"][:, tt, :])) for tt, d in enumerate(d_x)]
    got_cst = d_c.did(sp.dma_start(CST[:, :, :], a["cst"]))
    got_gn = d_misc.did(sp.dma_start(GN[:, :], a["small"]))

    w1 = a["w_in"]
    fetch(w1[6])
    fetch(w1[7])
    ready_root()
    x_normed = normed(X, X, 4, [[g] for g in got_x])
    for x in (A, V, T):
        x.wait(got_cst, got_gn)
    part_next()
    leading.append(turn_by_k(X, 4, G_MIX, x_normed))
    xn_read = [None]
    MIX = X
    with ExitStack() as sc:
        with nc.sbuf_tensor("HSM", [128, 2, 8, 256], F32R) as HSM:
            with nc.sbuf_tensor("ME", [128, 2, 1024], F32) as ME:
                got_me = [d_m[0].did(sp.dma_start(ME[:, :, :], a["mem0"])), None]
        SQK = sb("SQK", [128, 8, 512], scope=sc)
        SV = sb("SV", [128, 4, 512], scope=sc)
        HI = sb("HI", [128, 4, 256], scope=sc)
        HG = sb("HG", [128, 4, 256], scope=sc)
        MQ = sb("MQ", [128, 4, 256], scope=sc)
        MK = sb("MK", [128, 2, 256], scope=sc)
        with ExitStack() as hs:
            MASK = sb("MASK", [128, 8, 128], U32, scope=hs)
            QF = sb("QF", [128, 4, 512], scope=hs)
            KK = sb("KK", [128, 4, 512], scope=hs)
            BC = sb("BC", [128, 4, 512], scope=hs)
            LF = sb("LF", [128, 2, 512], scope=hs)
            LB = sb("LB", [128, 4, 2, 512], scope=hs)
            PX = sb("PX", [128, 2, 512], scope=hs)
            PX2 = sb("PX2", [128, 512], scope=hs)
            AT = sb("AT", [128, 2, 512], scope=hs)
            AC, EX = (LF[:, :, :].rearrange("p a b -> p (a b)").rearrange("p (n c) -> p n c", c=128)[:, n]
                      for n in (slice(0, 6), slice(6, 8)))
            LW = sb("LW", [128, 4, 4], scope=hs)

            got_mask = d_misc2.did(sp.dma_start(MASK[:, :, :], a["mask"]))
            at_zero = P.did(po.memset(AT[:, :, :], 0.0))

            def lower_bounds():
                g0, g1 = GN[:, G_LB:G_LB + 4], GN[:, G_LB + 4:G_LB + 8]
                V.did(ve.tensor_tensor(LW[:, 0, :], g0, g1, ALU.max))
                V.own()
                V.did(ve.tensor_tensor(LW[:, 1, :], g0, LW[:, 0, :], ALU.subtract))
                m = V.did(ve.tensor_tensor(LW[:, 2, :], g1, LW[:, 0, :], ALU.subtract))
                A.wait(m)
                m = A.did(ac.activation(LW[:, 1:3, :], LW[:, 1:3, :], ACT.Exp))
                V.wait(m)
                V.did(ve.tensor_tensor(LW[:, 3, :], LW[:, 1, :], LW[:, 2, :], ALU.add))
                V.own()
                V.did(ve.reciprocal(LW[:, 3, :], LW[:, 3, :]))
                V.own()
                V.did(ve.tensor_tensor(LW[:, 0, :], LW[:, 1, :], LW[:, 3, :], ALU.mult))
                V.own()
                V.did(ve.tensor_scalar(LW[:, 1, :], LW[:, 0, :], -1.0, 1.0, ALU.mult, ALU.add))
                V.own()

            lf_free = [None, None]
            qf_mark, kk_mark, bc_mark = {}, {}, {}

            def query_feature(n):
                def f(s):
                    for c, b, m in features_of(s):
                        hd = 2 * n + c
                        A.wait(m)
                        m = A.did(ac.activation(QF[:, hd, :], PS[b][:, :], ACT.Silu))
                        bank_free[b] = [m]
                        qf_mark[hd] = m
                    xn_read[0] = xn_read[0] or T.last()
                return f

            def forget_feature(n):
                def f(s):
                    for c, b, m in features_of(s):
                        hd = 2 * n + c
                        A.wait(m, lf_free[c])
                        m = A.did(ac.activation(LF[:, c, :], PS[b][:, :], ACT.Sigmoid))
                        bank_free[b] = [m]
                        V.wait(m)
                        V.did(ve.tensor_scalar(LF[:, c, :], LF[:, c, :], LW[:, 1, hd:hd + 1], LW[:, 0, hd:hd + 1],
                                               ALU.mult, ALU.add))
                        V.own()
                        kk_mark[hd] = V.did(ve.tensor_scalar(KK[:, hd, :], LF[:, c, :], -1.0, 1.0, ALU.mult, ALU.add))
                    for c in range(2):
                        hd = 2 * n + c
                        A.wait(kk_mark[hd])
                        m = A.did(ac.activation(LF[:, c, :], LF[:, c, :], ACT.Ln))
                        V.wait(m)
                        for tt in range(4):
                            m = V.did(ve.tensor_tensor_scan(BC[:, hd, tt * 128:tt * 128 + 128], ONES,
                                                            LF[:, c, tt * 128:tt * 128 + 128], 0.0,
                                                            ALU.mult, ALU.add))
                        lf_free[c] = m
                        bc_mark[hd] = m
                return f

            def token_pairs(evict):
                def f(s):
                    for tts, src, b, m in tokens_of(s):
                        bank_free[b] = [evict(tts, src, m)]
                return f

            def into(dst, col):
                def f(tts, src, m):
                    V.wait(m)
                    return V.did(ve.tensor_copy(dst[:, tts, col:col + 256], src))
                return f

            def gate_into(tts, src, m):
                A.wait(m)
                return A.did(ac.activation(HG[:, tts, :], src, ACT.Silu))

            def sb_feature(n):
                def f(s):
                    for c in range(2):
                        b = bank()
                        m = by_feature(s, c, PS[b][:, :], 512)
                        V.wait(m)
                        m = V.did(ve.tensor_copy(SQK[:, 2 * n + c, :], PS[b][:, :]))
                        bank_free[b] = [m]
                return f

            steps = [(hd, lv) for hd in range(4) for lv in range(9)]
            px_free, lb_free = [None, None], [None] * 4
            x_free = [None]
            ac_free = [None]
            at_free = [None, None]
            prepared = {}
            outs_waiting = []

            def hg_prepare(n):
                hd, lv = steps[n]
                s, x = n % 4, n % 2
                V.wait(qf_mark[hd], bc_mark[hd])
                A.wait(bc_mark[hd])
                P.wait(kk_mark[hd])
                if lv == 7:
                    prepared[n] = ()
                    return
                if lv < 7:
                    h = LEVELS[lv]
                    nb = 512 // (2 * h)
                    bv = BC[:, hd, :].rearrange("p (n c) -> p n c", c=2 * h)
                    pv = PX[:, x, :].rearrange("p (n c) -> p n c", c=2 * h)
                    ref = bv[:, :, h - 1:h].to_broadcast([128, nb, h])
                    V.wait(*(px_free[x] or ()))
                    V.did(ve.tensor_tensor(pv[:, :, h:], bv[:, :, h:], ref, ALU.subtract))
                    m = V.did(ve.tensor_tensor(pv[:, :, 0:h], ref, bv[:, :, 0:h], ALU.subtract))
                    A.wait(m)
                    m = A.did(ac.activation(PX[:, x, :], PX[:, x, :], ACT.Exp))
                    V.wait(m, lb_free[s])
                    P.wait(m, lb_free[s])
                    q = V.did(ve.tensor_tensor(LB[:, s, 0, :], QF[:, hd, :], PX[:, x, :], ALU.mult))
                    k = P.did(po.tensor_tensor(LB[:, s, 1, :], KK[:, hd, :], PX[:, x, :], ALU.mult))
                    px_free[x] = (q, k)
                    prepared[n] = (q, k)
                    return
                for E in (V, A):
                    E.wait(*bc_mark.values())
                V.wait(*(px_free[x] or ()))
                V.wait(x_free[0])
                A.wait(*(px_free[x] or ()))
                bt = BC[:, hd, :].rearrange("p (n c) -> p n c", c=128)
                m = V.did(ve.tensor_tensor(PX2[:, :].rearrange("p (n c) -> p n c", c=128),
                                           bt[:, :, 127:128].to_broadcast([128, 4, 128]), bt, ALU.subtract))
                m1 = A.did(ac.activation(PX[:, x, :], BC[:, hd, :], ACT.Exp))
                A.wait(m)
                m2 = A.did(ac.activation(PX2[:, :], PX2[:, :], ACT.Exp))
                V.wait(m2, lb_free[s])
                P.wait(m2, lb_free[s])
                q = V.did(ve.tensor_tensor(LB[:, s, 0, :], QF[:, hd, :], PX[:, x, :], ALU.mult))
                k = P.did(po.tensor_tensor(LB[:, s, 1, :], KK[:, hd, :], PX2[:, :], ALU.mult))
                V.wait(q, k)
                V.did(ve.tensor_scalar(EX[:, 0, :], LB[:, s, 0, 384:512], PX[:, x, 383:384], None, ALU.mult))
                q = V.did(ve.tensor_scalar(EX[:, 1, :], LB[:, s, 1, 0:128], PX[:, x, 255:256], None, ALU.mult))
                px_free[x] = (q, k)
                prepared[n] = (q, k)

            def hg_scores(n):
                hd, lv = steps[n]
                s, z = n % 4, hd % 2
                T.wait(*prepared[n])
                T.wait(qf_mark[hd], kk_mark[hd])
                if lv < 8:
                    b = bank()
                    for tt in range(4):
                        c = slice(tt * 128, tt * 128 + 128)
                        k = LB[:, s, 1, c] if lv < 7 else KK[:, hd, c]
                        q = LB[:, s, 0, c] if lv < 7 else QF[:, hd, c]
                        ins = te.matmul(PS[b][:, c], k, q, start=True, stop=True)
                    m = T.did(ins)
                    lb_free[s] = m
                    V.wait(m, at_free[z], got_mask, at_zero)
                    V.own()
                    m = V.did(ve.copy_predicated(
                        AT[:, z, :].rearrange("p (n c) -> p n c", c=128),
                        MASK[:, lv:lv + 1, :].to_broadcast([128, 4, 128]),
                        PS[b][:, :].rearrange("p (n c) -> p n c", c=128)))
                    bank_free[b] = [m]
                    return
                done = V.last()
                pairs = [(0, 1), (1, 2), (2, 3), (0, 2), (1, 3), (0, 3)]
                for lot in (pairs[0:4], pairs[4:6]):
                    b = bank()
                    for w, (j, i) in enumerate(lot):
                        k = EX[:, 1, :] if (j == 0 and i > 1) else LB[:, s, 1, j * 128:j * 128 + 128]
                        q = EX[:, 0, :] if (i == 3 and j < 2) else LB[:, s, 0, i * 128:i * 128 + 128]
                        ins = te.matmul(PS[b][:, w * 128:w * 128 + 128], k, q, start=True, stop=True)
                    m = T.did(ins)
                    A.wait(m, ac_free[0])
                    at = pairs.index(lot[0])
                    m2 = A.did(ac.activation(AC[:, at:at + len(lot), :].rearrange("p a b -> p (a b)"),
                                             PS[b][:, 0:128 * len(lot)], ACT.Copy))
                    bank_free[b] = [m2]
                lb_free[s] = m
                x_free[0] = m
                outs_waiting.append((hd, pairs, (m2, done)))

            def hg_outs():
                if not outs_waiting:
                    return
                hd, pairs, marks = outs_waiting.pop()
                z = hd % 2
                b = bank()
                T.wait(*marks)
                for i in range(4):
                    lhs = [(AT[:, z, i * 128:i * 128 + 128], i)]
                    lhs += [(AC[:, w, :], j) for w, (j, i2) in enumerate(pairs) if i2 == i]
                    for w, (l, j) in enumerate(lhs):
                        ins = te.matmul(PS[b][:, i * 64:i * 64 + 64], l, HI[:, j, hd * 64:hd * 64 + 64],
                                        start=w == 0, stop=w == len(lhs) - 1)
                m = T.did(ins)
                ac_free[0] = m
                at_free[z] = m
                A.wait(m, xn_read[0])
                m = A.did(ac.activation(MIX[:, :, 512 + hd * 64:576 + hd * 64],
                                        PS[b][:, 0:256].rearrange("p (i d) -> p i d", d=64), ACT.Copy))
                bank_free[b] = [m]

            at_step = [0]

            def with_steps(consume, count=3):
                def f(s):
                    lo, hi = at_step[0], min(at_step[0] + count, len(steps))
                    at_step[0] = hi
                    for n in range(lo, hi):
                        hg_prepare(n)
                    consume(s)
                    hg_outs()
                    for n in range(lo, hi):
                        hg_scores(n)
                return f

            sq_free, me_free = [None], [None]
            me_normed, mem_marks = {}, {}

            def memory_normed(n):
                if n == 1:
                    S.wait(me_free[0])
                    got_me[1] = d_m[1].did(sp.dma_start(ME[:, :, :], a["mem1"]))
                me_normed[n] = normed(ME, ME, 2, [[got_me[n]]] * 2)

            def memory_turned(n):
                kept = [list(x) for x in hs_mark]
                turn_parts(ME, 2, (G_MEM, G_MEM2)[n], me_normed[n], HSM)
                me_free[0] = T.last()
                mem_marks[n] = [list(x) for x in hs_mark]
                hs_mark[:] = kept


            def memory_block(n, consume, last):
                def f(s):
                    kept = list(hs_mark)
                    hs_mark[:] = mem_marks[n]
                    consume(s)
                    hs_mark[:] = kept
                    if last:
                        sq_free[0] = T.last()
                return f

            def mem_pair(dst):
                def f(s):
                    b = bank()
                    for mt in range(2):
                        m = by_token(s, mt, PS[b][:, mt * 256:mt * 256 + 256], HSM)
                    A.wait(m)
                    bank_free[b] = [A.did(ac.activation(dst[:, :, :].rearrange("p a b -> p (a b)"), PS[b][:, :],
                                                        ACT.Copy))]
                return f

            def key_features(s):
                b = bank()
                for c in range(2):
                    m = by_feature(s, c, PS[b][:, c * 256:c * 256 + 256], 256, HSM)
                A.wait(m)
                bank_free[b] = [A.did(ac.activation(MKT[1][:, :, :].rearrange("p a b -> p (a b)"), PS[b][:, :],
                                                    ACT.Copy))]

            def ahead_of(first, consume):
                def f(s):
                    first()
                    consume(s)
                return f

            def free_sq(consume):
                def f(s):
                    V.wait(sq_free[0])
                    A.wait(sq_free[0])
                    consume(s)
                return f

            wm, wm2 = a["w_mem"], a["w_mem2"]
            plan = [(w1[6], query_feature(0)), (w1[7], ahead_of(lambda: (lower_bounds(), memory_normed(0)), query_feature(1))),
                    (w1[8], forget_feature(0)),
                    (w1[9], forget_feature(1)),
                    (w1[10], ahead_of(lambda: memory_turned(0), with_steps(token_pairs(into(HI, 0)), 4))),
                    (wm[0], ahead_of(lambda: memory_normed(1), memory_block(0, mem_pair(MK), False))),
                    (wm[1], memory_block(0, mem_pair(MV[0]), True)),
                    (w1[11], ahead_of(lambda: memory_turned(1), with_steps(token_pairs(gate_into), 4))),
                    (w1[12], with_steps(token_pairs(into(MQ, 0)), 4)),
                    (wm2[0], memory_block(1, key_features, False)),
                    (wm2[1], memory_block(1, mem_pair(MV[1]), True))]
            rest = [(0, sb_feature(0)), (1, sb_feature(1)), (2, sb_feature(2)), (3, sb_feature(3)),
                    (4, token_pairs(into(SV, 0))), (5, token_pairs(into(SV, 256)))]
            plan += [(w1[n], with_steps(free_sq(f), 4)) for n, f in rest]

            def heads_normed(src, n):
                V.wait(A.last())
                V.own()
                m = head_norm(src[:, :, :].rearrange("p a (h d) -> p (a h) d", d=64),
                              JK[:, 0:256 * n].rearrange("p (n d) -> p n d", d=64), 4 * n)
                return m

            normed_marks = []
            for at, src, n in ((13, MQ, 4), (14, MK, 2)):
                plan[at] = (plan[at][0], ahead_of(lambda src=src, n=n: normed_marks.append(heads_normed(src, n)),
                                                  plan[at][1]))
            stream(plan, [a["w_out"][0], a["w_out"][1]])
            while at_step[0] < len(steps):
                with_steps(lambda s: None)(0)
            hg_outs()
            fence()

        with ExitStack() as hs:
            MQT = sb("MQT", [128, 2, 512], scope=hs)
            ZS = sb("ZS", [128, 2, 1280], scope=hs)
            EE = sb("EE", [128, 1280], scope=hs)
            LL = sb("LL", [128, 2, 1280], scope=hs)
            AA = sb("AA", [128, 2, 1280], scope=hs)
            SQ = sb("SQ", [128, 1536], scope=hs)
            PM = sb("PM", [128, 2, 2, 256], scope=hs)
            PT = sb("PT", [128, 2, 512], scope=hs)
            nM = sb("nM", [128, 16], scope=hs)
            SU = sb("SU", [128, 16], scope=hs)
            AT4 = {0: (0, 512), 1: (512, 384), 3: (896, 128), 2: (1024, 256)}
            BANKS = [(0, 512, (0,)), (512, 512, (1, 3)), (1024, 256, (2,))]
            mark_l, mark_a, zs_free, ll_free, aa_free, ee_free = {}, {}, {}, {}, {}, [None]

            def sb_logits(h, meanwhile=None):
                z, c, p0 = h % 2, h // 2, 64 * (h % 2)
                marks = []
                V.wait(zs_free.get(h - 2))
                for off, width, tiles in BANKS:
                    b = bank()
                    for kt in tiles:
                        o, w = AT4[kt]
                        ins = te.matmul(PS[b][:, o - off:o - off + w], SQK[p0:p0 + 64, 4 + c, kt * 128:kt * 128 + 128],
                                        SQK[p0:p0 + 64, c, kt * 128:512], start=True, stop=True)
                    m = T.did(ins)
                    V.wait(m)
                    m = V.did(ve.tensor_scalar(ZS[:, z, off:off + width], PS[b][:, 0:width], 0.125, None, ALU.mult))
                    bank_free[b] = [m]
                A.wait(m, ee_free[0])
                A.did(ac.activation(EE[:, :], ZS[:, z, :], ACT.Abs))
                A.own()
                A.did(ac.activation(EE[:, :], EE[:, :], ACT.Exp, scale=-1.0))
                A.own()
                m = A.did(ac.activation(EE[:, :], EE[:, :], ACT.Ln, bias=1.0))
                if meanwhile:
                    meanwhile()
                V.wait(m, ll_free.get(h - 2))
                V.own()
                m = V.did(ve.scalar_tensor_tensor(LL[:, z, :], ZS[:, z, :], 0.0, EE[:, :], ALU.max, ALU.add))
                ee_free[0] = m
                P.wait(m)
                for kt in range(4):
                    o = AT4[kt][0]
                    m = P.did(po.affine_select(out=LL[:, z, o:o + 128], in_=LL[:, z, o:o + 128],
                                               compare_op=ALU.is_gt, fill=0.0, base=0, pattern=[[1, 128]],
                                               channel_multiplier=-1))
                mark_l[h] = m

            def sb_tail_scores(h):
                z = h % 2
                T.wait(mark_l[h])
                V.wait(aa_free.get(h - 2))
                for off, width, tiles in BANKS:
                    b = bank()
                    for kt in tiles:
                        o, w = AT4[kt]
                        ins = te.matmul(PS[b][:, o - off:o - off + w], TRI, LL[:, z, o:o + w],
                                        start=True, stop=kt == 3)
                        for k2 in range(kt + 1, 4):
                            o2, w2 = AT4[k2]
                            ins = te.matmul(PS[b][:, o - off + w - w2:o - off + w], ONES, LL[:, z, o2:o2 + w2],
                                            start=False, stop=k2 == 3)
                    m = T.did(ins)
                    V.wait(m)
                    m = V.did(ve.tensor_tensor(AA[:, z, off:off + width], ZS[:, z, off:off + width],
                                               PS[b][:, 0:width], ALU.subtract))
                    bank_free[b] = [m]
                ll_free[h] = T.last()
                zs_free[h] = m
                A.wait(m)
                m = A.did(ac.activation(AA[:, z, :], AA[:, z, :], ACT.Exp))
                P.wait(m)
                for kt in range(4):
                    o = AT4[kt][0]
                    m = P.did(po.affine_select(out=AA[:, z, o:o + 128], in_=AA[:, z, o:o + 128],
                                               compare_op=ALU.is_gt, fill=0.0, base=0, pattern=[[1, 128]],
                                               channel_multiplier=-1))
                mark_a[h] = m

            def sb_out(h):
                z = h % 2
                T.wait(mark_a[h])
                b = bank()
                for qt in range(4):
                    for kt in range(qt + 1):
                        o = AT4[kt][0] + (qt - kt) * 128
                        ins = te.matmul(PS[b][:, qt * 64:qt * 64 + 64], AA[:, z, o:o + 128],
                                        SV[:, kt, h * 64:h * 64 + 64], start=kt == 0, stop=kt == qt)
                m = T.did(ins)
                aa_free[h] = m
                V.wait(m)
                m = V.did(ve.tensor_copy(MIX[:, :, h * 64:h * 64 + 64],
                                         PS[b][:, 0:256].rearrange("p (i d) -> p i d", d=64)))
                bank_free[b] = [m]

            def heads_turned(src, n, dst, gain, ready):
                for c in range(2):
                    b = bank()
                    T.wait(ready)
                    for tt in range(n):
                        ins = te.transpose(PS[b][:, tt * 128:tt * 128 + 128], src[:, tt, c * 128:c * 128 + 128],
                                           IDENT)
                    t = T.did(ins)
                    V.wait(t)
                    e = V.did(ve.tensor_scalar(dst[:, c, :], PS[b][:, 0:128 * n], GN[:, gain:gain + 1], None, ALU.mult))
                    bank_free[b] = [e]
                heads_mark.append(e)

            heads_mark = []
            def mix_normed(c0, c1, o):
                n = (c1 - c0) // 64
                at = slice(o, o + 4 * n)
                mix = MIX[:, :, c0:c1].rearrange("p t (h d) -> p t h d", d=64)
                sq = SQ[:, 0:4 * (c1 - c0)].rearrange("p (t h d) -> p t h d", t=4, d=64)
                root = []

                def squares():
                    V.own()
                    V.did(ve.tensor_tensor(sq, mix, mix, ALU.mult))
                    V.own()
                    V.did(ve.tensor_reduce(ST[:, at], sq.rearrange("p t h d -> p (t h) d"), AX.X, ALU.add))
                    V.own()
                    m = V.did(ve.tensor_scalar(ST[:, at], ST[:, at], 1.0 / 64, EPS, ALU.mult, ALU.add))
                    A.wait(m)
                    root.append(A.did(ac.activation(SD[:, at], ST[:, at], ACT.Sqrt)))

                def scale():
                    V.wait(*root)
                    V.did(ve.reciprocal(RS[:, at], SD[:, at]))
                    V.own()
                    m = V.did(ve.tensor_tensor(
                        mix, mix, RS[:, at].rearrange("p (t h) -> p t h", t=4).unsqueeze(3).to_broadcast(
                            [128, 4, n, 64]), ALU.mult))
                    if c0 == 512:
                        V.own()
                        m = V.did(ve.tensor_tensor(MIX[:, :, c0:c1], MIX[:, :, c0:c1], HG[:, :, :], ALU.mult))
                    return m

                return squares, scale

            hg_squares, hg_scale = mix_normed(512, 768, 0)
            heads_turned(MQ, 4, MQT, G_MQ, normed_marks[0])
            heads_turned(MK, 2, MKT[0], G_MK, normed_marks[1])
            sb_logits(0, hg_squares)
            hg_scale()
            while fetched:
                part_next()
            T.wait(*heads_mark)

            def later(f):
                return lambda u: f(u) if u > 0 else None

            def from_step(n, parts):
                return (1, tuple([lambda u: None] * n + [lambda u, f=f: f() for f in parts]))

            skew((8, (later(sb_logits), sb_tail_scores, sb_out)),
                 (8, memory_attention(MQT, MKT[0], MV[0], 0.125, MIX, 768, PM, PT, nM, SU)),
                 from_step(8, mix_normed(0, 384, 16)))

            others = V.last()
            squares, scale = mix_normed(384, 512, 40)
            squares()
            m = scale()
            turned_ks = set()

            def bring_x(k):
                turned_ks.add(k)
                n = k // 2
                if {2 * n, 2 * n + 1} <= turned_ks:
                    S.wait(T.last())
                    c = slice(n * 256, n * 256 + 256)
                    got_x[n] = d_x[n].did(sp.dma_start(X[:, :, c], a["x"][:, :, c]))

            lead_order[:] = [0, 1, 2, 4, 5, 6, 7, 3]
            leading.append(turn_by_k(MIX, 4, G_OUT, lambda k: [m if k == 3 else others], then=bring_x,
                                     order=list(lead_order)))

            def add_out(n):
                def f(tts, src, m):
                    V.wait(m, got_x[n])
                    dst = X[:, tts, n * 256:n * 256 + 256]
                    m = V.did(ve.tensor_tensor(dst, dst, src, ALU.add))
                    if n == 0 and tts.start == 0:
                        ready_root()
                    A.wait(m)
                    for tt in range(tts.start, tts.stop):
                        square(tt, n, 256)
                    return m
                return f

            stream([(a["w_out"][n], token_pairs(add_out(n))) for n in range(4)],
                   [a["w_query"][0], a["w_query"][1]])
            marks = fence()
            S.wait(*marks)

    NU, NV, NW, GRP = 3, 6, 8, 4
    NG = 128 // GRP
    AHEAD = list(range(0, 128, 2))
    TB = 512 // TBLK
    GD = nc.dram_tensor("gates", [TB, 128, 128, TBLK], F32, kind="Internal")
    AD = nc.dram_tensor("activations", [len(AHEAD), 128, 512], F32, kind="Internal")
    ahead_at = {i: n for n, i in enumerate(AHEAD)}
    now = [i for i in range(128) if i not in ahead_at]
    order = AHEAD + now
    expert_scope = ExitStack()
    GA = sb("GA", [128, 3, 512], scope=expert_scope)
    with ExitStack() as pe_scope:
        wr = WR[:, :, :, :].rearrange("p a b c -> p (a b c)")
        UR = wr[:, 2048:4096].rearrange("p (s k e) -> p s k e", s=2, k=8)
        VR = wr[:, 0:2048].rearrange("p (s e d) -> p s e d", s=2, e=2)
        ws = WS[:, :, :, :, :].rearrange("p a b c d -> p (a b c d)")
        UH = [ws[:, o:o + 2048].rearrange("p (w k e) -> p w k e", w=2, k=8) for o in (4096, 6144, 0)]
        d_u = [Arrival(nc, f"d_u{n}") for n in range(2)]
        d_v = [Arrival(nc, f"d_v{n}") for n in range(2)]
        d_gb = [Arrival(nc, f"d_gb{n}") for n in range(2)]
        d_keep = [Arrival(nc, f"d_keep{n}") for n in range(3)]
        d_back = [Arrival(nc, f"d_back{n}") for n in range(3)]
        ur_free, vr_free = [()] * 2, [()] * 2
        uh_free, vh_free, wh_free = [None] * NU, [None] * NV, [None] * NW
        ga_free, gb_free = [()] * 3, [None] * 2
        u_mark, v_mark, w_mark, gb_mark, g_mark, ga_mark, keep_mark, vr_mark, ur_mark = [{} for _ in range(9)]
        n_u, n_fu, n_ga = [0], [0], [0]
        u_slot, ga_slot = {}, {}

        def fetch_u(i):
            r = n_fu[0] % 2
            n_fu[0] += 1
            S.wait(*ur_free[r])
            ur_mark[i] = (r, d_u[r].did(sp.dma_start(UR[:, r], a["u"][i])))

        def part_u(i, E=V):
            r, loaded = ur_mark[i]
            s = n_u[0] % NU
            u_slot[i] = s
            n_u[0] += 1
            A.wait(loaded, uh_free[s])
            hi = A.did(ac.activation(UH[s][:, 0], UR[:, r], ACT.Copy))
            E.wait(hi)
            lo = E.did(E.e.tensor_tensor(UH[s][:, 1], UR[:, r], UH[s][:, 0].bitcast(F32), ALU.subtract))
            ur_free[r] = (hi, lo)
            u_mark[i] = (hi, lo)

        def fetch_v(u):
            g, dh, i = u // 4, u % 4 // 2, u // 4 * GRP + u % 2 * 2
            S.wait(*vr_free[u % 2])
            src = a["v"][i:i + 2, :, dh * 512:dh * 512 + 512].rearrange("e p d -> p e d")
            vr_mark[u] = d_v[u % 2].did(sp.dma_start(VR[:, u % 2], src))

        def activate_by(i, steps):
            s, z = u_slot[i], n_ga[0] % 3
            ga_slot[i] = z
            n_ga[0] += 1
            b = bank()
            T.wait(*u_mark[i])
            n = 0
            for k in range(8):
                T.wait(*hs_mark[k])
                for w, h in PARTS:
                    ins = te.matmul(PS[b][:, :], UH[s][:, w, k, :], HS[:, h, k, :], start=n == 0, stop=n == 23)
                    n += 1
                if (k + 1) % (8 // steps) == 0 and k < 7:
                    yield
            m = T.did(ins)
            uh_free[s] = m
            A.wait(m, *ga_free[z])
            m = A.did(ac.activation(GA[:, z, :], PS[b][:, :], ACT.Gelu))
            bank_free[b] = [m]
            ga_mark[i] = m

        def activate(i):
            for _ in activate_by(i, 1):
                pass

        to_keep = []
        next_ahead = [0]

        def keep_one():
            i = to_keep.pop(0)
            z = ga_slot[i]
            A.wait(ga_mark[i])
            keep_mark[i] = d_keep[z].did(ac.dma_start(AD[ahead_at[i]], GA[:, z, :]))
            ga_free[z] = (keep_mark[i],)

        def ahead_by(steps):
            while next_ahead[0] < len(AHEAD):
                n = next_ahead[0]
                next_ahead[0] += 1
                part_u(order[n + 2], P)
                fetch_u(order[n + 3])
                yield from activate_by(AHEAD[n], steps)
                to_keep.append(AHEAD[n])
                if len(to_keep) > 1:
                    keep_one()
                yield

        def ahead(count):
            for _, _ in zip(range(count), ahead_by(1)):
                pass

        HKT = sb("HKT", [128, 3, 512], scope=pe_scope)
        with ExitStack() as sc:
            SC = sb("SC", [128, 4, 16, 128], scope=sc)
            with ExitStack() as qs:
                XN = sb("XN", [128, 4, 1024], scope=qs)
                KEYS = sb("KEYS", [128, 16, 128], scope=qs)
                got_keys = d_misc3.did(sp.dma_start(KEYS[:, :, :], a["keys"]))
                xn = norm_of_squares(XN, 4, A.last())
                leading.append(turn_by_k(XN, 4, G_FFN, xn))
                QT = sb("QT", [128, 2, 512], scope=qs)
                qt_free = [None, None]
                waiting = []

                def scores_of(hc, mark):
                    T.wait(mark, got_keys)
                    b = bank()
                    for tt in range(4):
                        ins = te.matmul(PS[b][:, tt * 128:tt * 128 + 128], QT[:, hc % 2, tt * 128:tt * 128 + 128],
                                        KEYS[:, hc, :], start=True, stop=True)
                    m = T.did(ins)
                    qt_free[hc % 2] = m
                    A.wait(m)
                    m = A.did(ac.activation(SC[:, :, hc, :], PS[b][:, :].rearrange("p (t n) -> p t n", t=4), ACT.Copy))
                    bank_free[b] = [m]

                def first_experts():
                    ur_free[:] = [raw_free[1]] * 2
                    uh_free[0:2] = [ws_free[1][0]] * 2
                    for n in range(2):
                        fetch_u(order[n])
                    for n in range(2):
                        part_u(order[n], P)
                    fetch_u(order[2])

                def query_block(n):
                    def f(s):
                        if n == 7:
                            first_experts()
                        for c, b, m in features_of(s):
                            hc = 2 * n + c
                            V.wait(m, qt_free[hc % 2])
                            m = V.did(ve.tensor_copy(QT[:, hc % 2, :], PS[b][:, :]))
                            bank_free[b] = [m]
                            if waiting:
                                scores_of(*waiting.pop())
                            waiting.append((hc, m))
                    return f

                stream([(a["w_query"][n], query_block(n)) for n in range(8)])
                scores_of(*waiting.pop())
                vr_free[:] = [raw_free[0]] * 2
                uh_free[2] = T.last()
                fence()
            CA = sb("CA", [128, 8, 256], scope=sc)
            S2 = CA[:, :, :].rearrange("p h (c n) -> p (h c) n", c=2)
            C2 = sb("C2", [128, 8, 256], scope=sc)
            EQ = sb("EQ", [128, 2, 128, 16], scope=sc)
            TV = sb("TV", [128, 16, 16], scope=sc)
            TI = sb("TI", [128, 16, 16], U32, scope=sc)
            TF = sb("TF", [128, 2, 16, 16], scope=sc)
            BV = sb("BV", [128, 8, 16], scope=sc)
            BI = sb("BI", [128, 8, 16], U32, scope=sc)
            BP = sb("BP", [128, 2, 8, 16], U32, scope=sc)
            BF = sb("BF", [128, 2, 2, 128], scope=sc)
            HK = sb("HK", [128, 2, 3, 128], scope=sc)
            SM = sb("SM", [128, 2, 8], scope=sc)
            hk_free, pick_mark, exp_mark = [None, None], {}, {}
            iota16 = IOTA[:, 0:16].unsqueeze(1).to_broadcast([128, 128, 16])

            def choose(tt):
                z = tt % 2
                V.own()
                for q in range(16):
                    V.did(ve.max(TV[:, q, 0:8], SC[:, tt, q, :]))
                V.own()
                for q in range(16):
                    V.did(ve.match_replace(S2[:, q, :], TV[:, q, 0:8], SC[:, tt, q, :], NEG))
                for q in range(16):
                    V.did(ve.max_index(TI[:, q, 0:8], TV[:, q, 0:8], SC[:, tt, q, :]))
                V.own()
                for q in range(16):
                    V.did(ve.max(TV[:, q, 8:16], S2[:, q, :]))
                V.own()
                for q in range(16):
                    V.did(ve.max_index(TI[:, q, 8:16], TV[:, q, 8:16], S2[:, q, :]))
                V.own()
                tv = TV[:, :, :].rearrange("p (h c) k -> p h c k", c=2)
                V.did(ve.tensor_tensor(CA[:, :, :].rearrange("p h (i j) -> p h i j", i=16),
                                       tv[:, :, 0, :].unsqueeze(3).to_broadcast([128, 8, 16, 16]),
                                       tv[:, :, 1, :].unsqueeze(2).to_broadcast([128, 8, 16, 16]), ALU.add))
                V.wait(pick_mark.get(tt - 2))
                V.did(ve.tensor_copy(TF[:, z], TI[:, :, :]))

            def choose_pairs(tt):
                z = tt % 2
                V.own()
                for h in range(8):
                    V.did(ve.max(BV[:, h, 0:8], CA[:, h, :]))
                V.own()
                for h in range(8):
                    V.did(ve.match_replace(C2[:, h, :], BV[:, h, 0:8], CA[:, h, :], NEG))
                for h in range(8):
                    V.did(ve.max_index(BI[:, h, 0:8], BV[:, h, 0:8], CA[:, h, :]))
                V.own()
                for h in range(8):
                    V.did(ve.max(BV[:, h, 8:16], C2[:, h, :]))
                V.own()
                for h in range(8):
                    V.did(ve.max_index(BI[:, h, 8:16], BV[:, h, 8:16], C2[:, h, :]))
                V.did(ve.tensor_copy(SM[:, 0, :], BV[:, :, 0]))
                V.own()
                V.did(ve.tensor_scalar(BP[:, 0], BI[:, :, :], 4, None, ALU.logical_shift_right))
                V.did(ve.tensor_scalar(BP[:, 1], BI[:, :, :], 15, None, ALU.bitwise_and))
                m = V.did(ve.tensor_tensor(BV[:, :, :], BV[:, :, :],
                                           SM[:, 0, :].unsqueeze(2).to_broadcast([128, 8, 16]), ALU.subtract))
                A.wait(m)
                exp_mark[tt] = A.did(ac.activation(BV[:, :, :], BV[:, :, :], ACT.Exp))
                V.wait(pick_mark.get(tt - 2))
                V.own()
                m = V.did(ve.tensor_copy(BF[:, z].rearrange("p c (h k) -> p c h k", h=8), BP[:, :, :, :]))
                tf = TF[:, z].rearrange("p (h c) k -> p h c k", c=2)
                V.own()
                for c in range(2):
                    o = V.did(ve.tensor_tensor(EQ[:, c], BF[:, z, c, :].unsqueeze(2).to_broadcast([128, 128, 16]),
                                               iota16, ALU.is_equal))
                    P.wait(o)
                    eq = EQ[:, c].rearrange("p (h k) e -> p h k e", h=8)
                    pick_mark[tt] = P.did(po.tensor_tensor(
                        eq, eq, tf[:, :, c, :].unsqueeze(2).to_broadcast([128, 8, 16, 16]), ALU.mult))

            def turn_chosen(tt):
                z = tt % 2
                V.wait(exp_mark[tt], hk_free[z])
                V.did(ve.tensor_reduce(SM[:, 1, :], BV[:, :, :], AX.X, ALU.add))
                V.own()
                V.did(ve.reciprocal(SM[:, 1, :], SM[:, 1, :]))
                V.own()
                V.did(ve.tensor_tensor(HK[:, z, 2, :].rearrange("p (h k) -> p h k", h=8), BV[:, :, :],
                                       SM[:, 1, :].unsqueeze(2).to_broadcast([128, 8, 16]), ALU.mult))
                V.wait(pick_mark[tt])
                for c in range(2):
                    m = V.did(ve.tensor_reduce(HK[:, z, c, :], EQ[:, c], AX.X, ALU.add))
                b = bank()
                T.wait(m)
                for c in range(3):
                    ins = te.transpose(PS[b][:, c * 128:c * 128 + 128], HK[:, z, c, :], IDENT)
                m = T.did(ins)
                hk_free[z] = m
                A.wait(m)
                m = A.did(ac.activation(HKT[:, :, tt * 128:tt * 128 + 128],
                                        PS[b][:, 0:384].rearrange("p (c t) -> p c t", c=3), ACT.Copy))
                bank_free[b] = [m]

            for tt in range(4):
                ahead(5)
                choose(tt)
                if tt:
                    turn_chosen(tt - 1)
                ahead(4)
                choose_pairs(tt)
            ahead(6)
            turn_chosen(3)
            fence()

        with ExitStack() as sc:
            STG = [sb(f"STG{n}", [128, 128, TBLK], scope=sc) for n in range(2)]
            OI = sb("OI", [128, 3, 8, 128], scope=sc)
            OJ = sb("OJ", [128, 3, 8, 128], scope=sc)
            OA = sb("OA", [128, 3, 8, 128], scope=sc)
            oi_free, oj_free, oa_free = [None] * 3, [None] * 3, [None] * 3
            stg_free = [None, None]
            d_g = [Arrival(nc, f"d_g{n}") for n in range(2)]
            iota8 = IOTA.unsqueeze(1).to_broadcast([128, 8, 128])
            PER = TBLK // 8
            one_mark, made = {}, []

            def one_hots(t8):
                z = t8 % 3
                cols = slice(t8 * 8, t8 * 8 + 8)

                def spread_out(c):
                    return HKT[:, c, cols].unsqueeze(2).to_broadcast([128, 8, 128])

                V.wait(oi_free[z])
                mi = V.did(ve.tensor_tensor(OI[:, z], iota8, spread_out(0), ALU.is_equal))
                V.wait(oj_free[z])
                mj = V.did(ve.tensor_tensor(OJ[:, z], iota8, spread_out(1), ALU.is_equal))
                if t8 % 2:
                    P.wait(mi, oa_free[z])
                    ma = P.did(po.tensor_tensor(OA[:, z], OI[:, z], spread_out(2), ALU.mult))
                else:
                    A.wait(mi, oa_free[z])
                    for t in range(8):
                        ma = A.did(ac.activation(OA[:, z, t, :], OI[:, z, t, :], ACT.Copy,
                                                 scale=HKT[:, 2, t8 * 8 + t:t8 * 8 + t + 1]))
                oi_free[z] = ma
                one_mark[t8] = (mj, ma)

            def gates(t8):
                z, tb = t8 % 3, t8 // PER
                T.wait(*one_mark[t8])
                for half in range(2):
                    b = bank()
                    for t in range(4):
                        ins = te.matmul(PS[b][:, t * 128:t * 128 + 128], OJ[:, z, half * 4 + t, :],
                                        OA[:, z, half * 4 + t, :], start=True, stop=True)
                    m = T.did(ins)
                    t0 = (t8 % PER) * 8 + half * 4
                    src = PS[b][:, :].rearrange("p (t i) -> p i t", t=4)
                    dst = STG[tb % 2][:, :, t0:t0 + 4]
                    if half > t8 % 2:
                        V.wait(m, stg_free[tb % 2])
                        e = V.did(ve.tensor_copy(dst, src))
                    else:
                        A.wait(m, stg_free[tb % 2])
                        e = A.did(ac.activation(dst, src, ACT.Copy))
                    bank_free[b] = [e]
                    made.append(e)
                oj_free[z] = m
                oa_free[z] = m
                if t8 % PER == PER - 1:
                    S.wait(*made[-2 * PER:])
                    stg_free[tb % 2] = d_g[tb % 2].did(sp.dma_start(GD[tb], STG[tb % 2][:, :, :]))

            one_hots(0)
            one_hots(1)
            pieces = ahead_by(4)
            for _ in range(8):
                next(pieces)
            for t8 in range(64):
                if t8 + 2 < 64:
                    one_hots(t8 + 2)
                gates(t8)
                next(pieces, None)
            fetch_v(0)
            fetch_v(1)
            marks = [x.last() for x in (V, A, T, P)]
            for _ in range(8):
                next(pieces)
            for x in (V, A, P, S):
                x.wait(*marks, *stg_free)

    with ExitStack() as sc:
        VH = sb("VH", [128, NV, 2, 2, 512], F32R, scope=sc)
        WH6 = sb("WH", [128, 6, 2, 512], F32R, scope=sc)
        WH2 = ws[:, 2048:4096].rearrange("p (s w t) -> p s w t", s=2, w=2)
        WH = [WH6[:, n] for n in range(6)] + [WH2[:, n] for n in range(2)]
        GB = sb("GB", [128, 2, TB, GRP, TBLK], scope=sc)

        def part_v(u):
            s, r = u % NV, u % 2
            A.wait(vr_mark[u], vh_free[s])
            hi = A.did(ac.activation(VH[:, s, 0], VR[:, r], ACT.Copy))
            P.wait(hi)
            lo = P.did(po.tensor_tensor(VH[:, s, 1], VR[:, r], VH[:, s, 0].bitcast(F32), ALU.subtract))
            vr_free[r] = (hi, lo)
            v_mark[u] = (hi, lo)

        def load_g(g):
            S.wait(gb_free[g % 2])
            src = GD[:, :, g * GRP:g * GRP + GRP, :].rearrange("b p i t -> p b (i t)")
            gb_mark[g] = d_gb[g % 2].did(sp.dma_start(GB[:, g % 2].rearrange("p b i t -> p b (i t)"), src))

        def bring(i):
            z = n_ga[0] % 3
            ga_slot[i] = z
            n_ga[0] += 1
            S.wait(*ga_free[z], keep_mark[i])
            ga_mark[i] = d_back[z].did(sp.dma_start(GA[:, z, :], AD[ahead_at[i]]))

        def gated(i):
            z, g = ga_slot[i], i // GRP
            V.wait(ga_mark[i], gb_mark[g])
            m = V.did(ve.tensor_tensor(GA[:, z, :].rearrange("p (b t) -> p b t", b=TB),
                                       GA[:, z, :].rearrange("p (b t) -> p b t", b=TB),
                                       GB[:, g % 2, :, i % GRP, :], ALU.mult))
            gb_free[g % 2] = m
            g_mark[i] = m

        def part(i):
            z = ga_slot[i]
            A.wait(g_mark[i], wh_free[i % NW])
            hi = A.did(ac.activation(WH[i % NW][:, 0, :], GA[:, z, :], ACT.Copy))
            V.wait(hi)
            lo = V.did(ve.tensor_tensor(WH[i % NW][:, 1, :], GA[:, z, :], WH[i % NW][:, 0, :].bitcast(F32),
                                        ALU.subtract))
            ga_free[z] = (hi, lo)
            w_mark[i] = (hi, lo)

        def combine(g, p):
            dh, tt = p // 4, p % 4
            b = bank()
            n = 0
            for ii in range(GRP):
                i, u = g * GRP + ii, g * 4 + 2 * dh + ii // 2
                T.wait(*w_mark[i], *v_mark[u])
                for w, v in PARTS:
                    ins = te.matmul(PS[b][:, :], WH[i % NW][:, w, tt * 128:tt * 128 + 128],
                                    VH[:, u % NV, v, ii % 2, :], start=n == 0, stop=n == 3 * GRP - 1)
                    n += 1
            m = T.did(ins)
            if tt == 3:
                vh_free[(g * 4 + 2 * dh) % NV] = m
                vh_free[(g * 4 + 2 * dh + 1) % NV] = m
            if p == 7:
                for i in range(g * GRP, g * GRP + GRP):
                    wh_free[i % NW] = m
            V.wait(m)
            V.own()
            dst = X[:, tt, dh * 512:dh * 512 + 512]
            bank_free[b] = [V.did(ve.tensor_tensor(dst, dst, PS[b][:, :], ALU.add))]
            if g == NG - 1:
                A.wait(V.last())
                square(tt, dh, 512)

        load_g(0)
        part_v(0)
        part_v(1)
        fetch_v(2)
        fetch_v(3)
        for _ in pieces:
            pass
        while to_keep:
            keep_one()
        bring(0)
        n_now = 0
        for g in range(NG + 1):
            if g + 1 < NG:
                load_g(g + 1)
            if g == NG:
                ready_root()
            for ii in range(GRP):
                i = g * GRP + ii
                if g < NG:
                    if i not in ahead_at:
                        activate(i)
                    if i + 1 in ahead_at:
                        bring(i + 1)
                    gated(i)
                    part(i)
                    if i not in ahead_at:
                        n_now += 1
                        if n_now + 1 < len(now):
                            part_u(now[n_now + 1])
                        if n_now + 2 < len(now):
                            fetch_u(now[n_now + 2])
                    if i > 1:
                        part_v(i)
                        if i < 126:
                            fetch_v(i + 2)
                if g >= 1:
                    combine(g - 1, 2 * ii)
                    combine(g - 1, 2 * ii + 1)
        raw_free[:] = [[m for f in (*ur_free, *vr_free) for m in f]] * 2
        ws_free[:] = [[T.last()]] * 2
        fetch(a["w_in2"][0])
        fetch(a["w_in2"][1])
        fence()

    expert_scope.close()

    with ExitStack() as sc:
        DT = sb("DT", [128, 3, 512], scope=sc)
        Y = sb("Y", [128, 4, 1024], scope=sc)
        QT2 = sb("QT2", [128, 6, 512], scope=sc)
        KT2 = sb("KT2", [128, 6, 512], scope=sc)
        V2 = sb("V2", [128, 4, 768], scope=sc)
        QM = sb("QM", [128, 2, 512], scope=sc)
        SP2 = sb("SP2", [128, 3, 1280], scope=sc)
        PT2 = sb("PT2", [128, 2, 1280], scope=sc)
        PM = sb("PM2", [128, 2, 2, 256], scope=sc)
        PT = sb("PTm", [128, 2, 512], scope=sc)
        TMP = sb("TMP", [128, 2, 64], scope=sc)
        nM = sb("nM2", [128, 32], scope=sc)
        SU = sb("SU2", [128, 32], scope=sc)
        d_d = Arrival(nc, "d_d")
        S.wait(V.last(), T.last())
        got_d = d_d.did(sp.dma_start(DT[:, :, :], a["dist"]))
        yn = norm_of_squares(Y, 2, A.last())
        part_next()
        leading.append(turn_by_k(Y, 4, G_N2, yn))
        y_free = [None]

        def features(dst, n, scale):
            def f(s):
                for c, b, m in features_of(s):
                    A.wait(m)
                    m = A.did(ac.activation(dst[:, 2 * n + c, :], PS[b][:, :], ACT.Copy, scale=scale))
                    bank_free[b] = [m]
                y_free[0] = y_free[0] or T.last()
            return f

        def pairs_of(evict):
            def f(s):
                for tts, src, b, m in tokens_of(s):
                    bank_free[b] = [evict(tts, src, m)]
            return f

        def v_into(col):
            def f(tts, src, m):
                V.wait(m)
                return V.did(ve.tensor_copy(V2[:, tts, col:col + 256], src))
            return f

        def gate_into(n):
            def f(tts, src, m):
                A.wait(m, y_free[0])
                return A.did(ac.activation(Y[:, tts, n * 256:n * 256 + 256], src, ACT.Silu))
            return f

        w2 = a["w_in2"]
        stream([(w2[n], features(QT2, n, 0.125)) for n in range(3)]
               + [(w2[3 + n], features(KT2, n, 1.0)) for n in range(3)]
               + [(w2[6 + n], pairs_of(v_into(256 * n))) for n in range(3)]
               + [(w2[9], features(QM, 0, 0.125))]
               + [(w2[10 + n], pairs_of(gate_into(n))) for n in range(4)],
               [a["w_out2"][0], a["w_out2"][1]])

        V.wait(got_d)
        T.wait(A.last(), V.last())
        V.wait(A.last())
        units = [(hh, qt) for hh in range(4) for qt in range(4)]
        sp_free, pt_free = [None] * 3, [None] * 2
        exp_mark, pt_mark = {}, {}

        def lay(qt):
            tiles, o = [], 0
            for g in range(3):
                c0 = max(0, qt - 1) if g == 0 else 0
                tiles.append((o, c0, qt + 1 - c0))
                o += (qt + 1 - c0) * 128
            return tiles, o

        def window_scores(u):
            hh, qt = units[u]
            z = u % 3
            tiles, total = lay(qt)
            for g, (o, c0, n) in enumerate(tiles):
                hd = g * 4 + hh
                c, p0 = hd // 2, 64 * (hd % 2)
                b = bank()
                m = T.did(te.matmul(PS[b][:, 0:n * 128], QT2[p0:p0 + 64, c, qt * 128:qt * 128 + 128],
                                    KT2[p0:p0 + 64, c, c0 * 128:(qt + 1) * 128], start=True, stop=True))
                V.wait(m, sp_free[z])
                m = V.did(ve.scalar_tensor_tensor(SP2[:, z, o:o + n * 128], DT[:, g, 512 - n * 128:512], SLOPES[hd],
                                                  PS[b][:, 0:n * 128], ALU.mult, ALU.add))
                bank_free[b] = [m]
            V.own()
            m = V.did(ve.tensor_reduce(nM[:, u:u + 1], SP2[:, z, 0:total], AX.X, ALU.max, negate=True))
            A.wait(m)
            m = A.did(ac.activation(SP2[:, z, 0:total], SP2[:, z, 0:total], ACT.Exp, bias=nM[:, u:u + 1],
                                    accum_out=SU[:, u:u + 1]))
            exp_mark[u] = m

        def window_turned(u):
            z, w2 = u % 3, u % 2
            tiles, total = lay(units[u][1])
            nblk = total // 128
            for lot in range(0, nblk, 4):
                k = min(4, nblk - lot)
                b = bank()
                T.wait(exp_mark[u])
                for w in range(k):
                    ins = te.transpose(PS[b][:, w * 128:w * 128 + 128],
                                       SP2[:, z, (lot + w) * 128:(lot + w) * 128 + 128], IDENT)
                m = T.did(ins)
                A.wait(m, pt_free[w2])
                e = A.did(ac.activation(PT2[:, w2, lot * 128:(lot + k) * 128], PS[b][:, 0:k * 128], ACT.Copy))
                bank_free[b] = [e]
            sp_free[z] = m
            pt_mark[u] = e

        def window_out(u):
            hh, qt = units[u]
            w2 = u % 2
            tiles, total = lay(qt)
            V.wait(exp_mark[u])
            V.did(ve.reciprocal(SU[:, u:u + 1], SU[:, u:u + 1]))
            b = bank()
            T.wait(pt_mark[u])
            for g, (o, c0, n) in enumerate(tiles):
                hd = g * 4 + hh
                for w in range(n):
                    ins = te.matmul(PS[b][:, g * 64:g * 64 + 64], PT2[:, w2, o + w * 128:o + w * 128 + 128],
                                    V2[:, c0 + w, hd * 64:hd * 64 + 64], start=w == 0, stop=w == n - 1)
            m = T.did(ins)
            pt_free[w2] = m
            V.wait(m)
            V.own()
            dst = Y[:, qt, 0:768].rearrange("p (g c) -> p g c", g=3)[:, :, hh * 64:hh * 64 + 64]
            m = V.did(ve.scalar_tensor_tensor(dst, PS[b][:, 0:192].rearrange("p (g d) -> p g d", g=3), SU[:, u:u + 1],
                                              dst, ALU.mult, ALU.mult))
            bank_free[b] = [m]

        mem_stages = memory_attention(QM, MKT[1], MV[1], 1.0, Y, 768, PM, PT, nM[:, 16:32], SU[:, 16:32],
                                      TMP[:, :, :])
        while fetched:
            part_next()
        every_other = [lambda v, f=f: f(v // 2) if v % 2 == 0 else None for f in mem_stages]
        skew((16, (window_scores, lambda u: None, window_turned, lambda u: None, window_out)),
             (16, (every_other[0], lambda v: None, every_other[1], lambda v: None, every_other[2])),
             oldest_first=True)

        leading.append(turn_by_k(Y, 4, None, [V.last()]))

        def add_out2(n):
            def f(tts, src, m):
                V.wait(m)
                V.own()
                dst = X[:, tts, n * 256:n * 256 + 256]
                m = V.did(ve.tensor_tensor(dst, dst, src, ALU.add))
                if n == 0 and tts.start == 0:
                    ready_root()
                    P.wait(got_f, T.last())
                P.wait(m)
                c = slice(n * 256, n * 256 + 256)
                P.did(po.tensor_tensor(Y[:, tts, c], dst, FG[:, c].unsqueeze(1).to_broadcast(
                    [128, tts.stop - tts.start, 256]), ALU.mult))
                A.wait(m)
                for tt in range(tts.start, tts.stop):
                    square(tt, n, 256)
                return m
            return f

        FG = QM[:, :, :].rearrange("p a b -> p (a b)")
        S.wait(T.last())
        got_f = d_misc3.did(sp.dma_start(FG, a["final"]))
        stream([(a["w_out2"][n], pairs_of(add_out2(n))) for n in range(4)])
        norm_of_squares(None, 4, A.last())
        V.wait(P.last())
        A.wait(P.last())
        d_o = [Arrival(nc, f"d_o{n}") for n in range(4)]
        for tt, m in enumerate(scaled(Y, Y, 4)):
            S.wait(m)
            d_o[tt].did(sp.dma_start(out[tt], Y[:, tt, :]))
        S.wait(*[d.last() for d in d_o])
        fence()
    ctx.__exit__(None, None, None)


def constants():
    p = np.arange(128)
    cst = np.zeros((128, 4, 128), np.float32)
    cst[:, 0] = np.eye(128)
    cst[:, 1] = p[:, None] >= p[None, :]
    cst[:, 2] = 1.0
    cst[:, 3] = p[None, :]
    mask = np.zeros((128, 8, 128), np.uint32)
    s, t = p[:, None], p[None, :]
    for n, h in enumerate(LEVELS):
        mask[:, n] = (s // (2 * h) == t // (2 * h)) & (s % (2 * h) < h) & (t % (2 * h) >= h)
    mask[:, 7] = s == t
    d = p[:, None] - np.arange(512)[None, :] + 384
    dist = np.zeros((128, 3, 512), np.float32)
    for g, (window, dil) in enumerate(((128, 1), (512, 4), (2048, 16))):
        dist[:, g] = np.where((d >= 0) & (d <= window) & (d % dil == 0), -d, -1e30)
    return cst, mask, dist


def kernel(**inputs):
    import concourse.bacc as _bacc
    from concourse import mybir as _mybir
    from concourse.bass_utils import run_bass_kernel_spmd as _run

    i = {k: np.asarray(v) for k, v in inputs.items()}

    def tiles(x):
        return np.ascontiguousarray(x.reshape(-1, 128, 1024).transpose(1, 0, 2))

    def weight(w):
        return np.ascontiguousarray(w.reshape(8, 128, -1, 256).transpose(2, 1, 0, 3))

    def column(g):
        return g.reshape(-1, 128).T

    cst, mask, dist = constants()
    small = np.concatenate(
        [column(i["norm_mix_gain"]), column(i["norm_ffn_gain"]), column(i["norm_g_2"]), column(i["mem_norm_gain"]),
         column(i["mem_norm_g_2"]), column(i["sb_out_gain"]), column(i["hg_out_gain"]), np.ones((128, 2), np.float32),
         column(i["gamma_lb"]), column(np.tile(i["mem_q_gain"][0], 2)), column(np.tile(i["mem_k_gain"][0], 2))], axis=1)
    arrays = {
        "x": tiles(i["x"][0]), "mem0": tiles(i["mem"][0]), "mem1": tiles(i["mem_2"][0]),
        "w_in": weight(i["w_in"][0]), "w_mem": weight(i["w_mem_kv"][0]), "w_out": weight(i["w_out"][0]),
        "w_query": weight(i["peer_w_query"][0]), "w_in2": weight(i["w_in_2"][0]),
        "w_mem2": weight(i["w_mem_kv_2"][0]), "w_out2": weight(i["w_out_2"][0]),
        "keys": np.ascontiguousarray(i["peer_sub_keys"][0].reshape(16, 128, 128).transpose(2, 0, 1)),
        "u": np.ascontiguousarray(i["peer_u"][0].reshape(128, 128, 8, 128).transpose(0, 3, 2, 1)),
        "v": np.ascontiguousarray(i["peer_v"][0].reshape(128, 128, 1024)),
        "small": np.ascontiguousarray(small), "final": np.tile(i["final_norm_g_2"][None, :], (128, 1)),
        "cst": cst, "mask": mask, "dist": dist,
    }
    nc = _bacc.Bacc("TRN2", target_bir_lowering=False, num_devices=1)
    named, sent = {}, {}
    for name, x in arrays.items():
        sent[f"in_{name}"] = x
        named[name] = nc.dram_tensor(f"in_{name}", x.shape, _mybir.dt.from_np(x.dtype), kind="ExternalInput").ap()
    out = nc.dram_tensor("out_0", (4, 128, 1024), _mybir.dt.float32, kind="ExternalOutput").ap()
    program(nc, named, out)
    r = _run(nc, [sent], core_ids=[0])
    return np.asarray(r.results[0]["out_0"]).reshape(1, 512, 1024)
```
